# Optimizing a Trainium2 kernel written in Bass

```python
import math
import jax, jax.numpy as jnp
from jax import lax
import numpy as np

D_MODEL = 1024
BATCH = 1
SEQ = 512
DEPTH = 1

HEAD_DIM = 64
NSA_HEADS = 8
NSA_KV_HEADS = 2
NSA_GROUP = NSA_HEADS // NSA_KV_HEADS
SB_HEADS = 8
CMP_BLOCK = 32
CMP_STRIDE = 16
CMP_HIDDEN = HEAD_DIM
SEL_BLOCK = 64
SEL_TOPK = 16
WINDOW = 512
NSA_QBLOCK = 64
SB_QBLOCK = 128
N_BUCKETS = 32
MAX_DISTANCE = 128
D_FF = 4 * D_MODEL
EPS = 1e-6
FORCED_BONUS = 1e4
NEG_BLOCK = -1e9
NEG_LOGIT = -1e30

Q_A_W = NSA_HEADS * HEAD_DIM
KV_A_W = NSA_KV_HEADS * HEAD_DIM
GATE_A_W = NSA_HEADS * 3
SB_W = SB_HEADS * HEAD_DIM
IN_SPLITS = (Q_A_W, KV_A_W, KV_A_W, KV_A_W, KV_A_W, KV_A_W, KV_A_W, GATE_A_W, SB_W, SB_W, SB_W, D_MODEL, D_MODEL)
IN_WIDTH = Q_A_W + 6 * KV_A_W + GATE_A_W + 3 * SB_W + 2 * D_MODEL


def rms_norm(x, g):
    x32 = x.astype(jnp.float32)
    y = x32 * lax.rsqrt(jnp.mean(x32 * x32, axis=-1, keepdims=True) + EPS)
    return (y * g.astype(jnp.float32)).astype(x.dtype)

def rel_bucket(dist):
    n = jnp.maximum(dist, 0)
    max_exact = N_BUCKETS // 2
    nf = jnp.maximum(n, 1).astype(jnp.float32)
    large = max_exact + (jnp.log(nf / max_exact) / math.log(MAX_DISTANCE / max_exact) * (N_BUCKETS - max_exact)).astype(jnp.int32)
    large = jnp.minimum(large, N_BUCKETS - 1)
    return jnp.where(n < max_exact, n, large)

def masked_softmax(logits, mask):
    masked = jnp.where(mask, logits, NEG_LOGIT)
    m = jnp.max(masked, axis=-1, keepdims=True)
    e = jnp.where(mask, jnp.exp(masked - m), 0.0)
    return e / jnp.maximum(jnp.sum(e, axis=-1, keepdims=True), 1e-30)

def compress_blocks(src, pos, w1, w2):
    B, S = src.shape[0], src.shape[1]
    nc = (S - CMP_BLOCK) // CMP_STRIDE + 1
    idx = jnp.arange(nc)[:, None] * CMP_STRIDE + jnp.arange(CMP_BLOCK)[None, :]
    blk = src[:, idx] + pos[None, None, :, None, :]
    blk = blk.transpose(0, 1, 3, 2, 4).reshape(B, nc, NSA_KV_HEADS, CMP_BLOCK * HEAD_DIM)
    return jax.nn.silu(blk @ w1) @ w2

def cmp_to_sel_overlap(nc, nsel):
    c_start = jnp.arange(nc) * CMP_STRIDE
    s_start = jnp.arange(nsel) * SEL_BLOCK
    ov = jnp.minimum(c_start[:, None] + CMP_BLOCK, s_start[None, :] + SEL_BLOCK) - jnp.maximum(c_start[:, None], s_start[None, :])
    return jnp.clip(ov, 0, CMP_BLOCK).astype(jnp.float32) / CMP_BLOCK

def nsa_attention(q, k_cmp, v_cmp, k_slc, v_slc, k_win, v_win, gates, rel_bias):
    B, S = q.shape[0], q.shape[1]
    nc = k_cmp.shape[1]
    nsel = S // SEL_BLOCK
    n_top = min(SEL_TOPK, nsel)
    scale = HEAD_DIM ** -0.5
    cmp_last = jnp.arange(nc) * CMP_STRIDE + CMP_BLOCK - 1
    overlap = cmp_to_sel_overlap(nc, nsel)
    tbl = rel_bias.astype(jnp.float32)
    tbl_g = tbl.reshape(N_BUCKETS, NSA_KV_HEADS, NSA_GROUP)
    ksel = k_slc.reshape(B, nsel, SEL_BLOCK, NSA_KV_HEADS, HEAD_DIM).transpose(0, 3, 1, 2, 4)
    vsel = v_slc.reshape(B, nsel, SEL_BLOCK, NSA_KV_HEADS, HEAD_DIM).transpose(0, 3, 1, 2, 4)
    kw_pad = jnp.pad(k_win, ((0, 0), (WINDOW, 0), (0, 0), (0, 0)))
    vw_pad = jnp.pad(v_win, ((0, 0), (WINDOW, 0), (0, 0), (0, 0)))
    bidx = jnp.arange(B)[:, None, None, None]
    hidx = jnp.arange(NSA_KV_HEADS)[None, :, None, None]
    blk = jnp.arange(nsel)
    tok_in_blk = jnp.arange(SEL_BLOCK)
    win_off = jnp.arange(WINDOW + NSA_QBLOCK)

    def head_bias(dist):
        b = tbl[rel_bucket(dist)]
        return jnp.moveaxis(b, -1, 0).reshape(NSA_KV_HEADS, NSA_GROUP, dist.shape[0], dist.shape[1])

    def block(i):
        start = i * NSA_QBLOCK
        t = start + jnp.arange(NSA_QBLOCK)
        qb = lax.dynamic_slice_in_dim(q, start, NSA_QBLOCK, axis=1)
        gb = lax.dynamic_slice_in_dim(gates, start, NSA_QBLOCK, axis=1)
        dist_c = t[:, None] - cmp_last[None, :]
        s_c = jnp.einsum('bqhgd,bchd->bhgqc', qb, k_cmp).astype(jnp.float32) * scale + head_bias(dist_c)
        p_c = masked_softmax(s_c, dist_c >= 0)
        o_c = jnp.einsum('bhgqc,bchd->bqhgd', p_c.astype(v_cmp.dtype), v_cmp)
        imp = jnp.einsum('bhgqc,cn->bhqn', p_c, overlap)
        cur = (t // SEL_BLOCK)[:, None]
        forced = (blk == 0) | (blk == cur) | (blk == cur - 1)
        imp = jnp.where(blk > cur, NEG_BLOCK, imp + jnp.where(forced, FORCED_BONUS, 0.0))
        _, top = lax.top_k(imp, n_top)
        kg = ksel[bidx, hidx, top]
        vg = vsel[bidx, hidx, top]
        tok = top[..., None] * SEL_BLOCK + tok_in_blk
        dist_s = t[:, None, None] - tok
        bias_s = jnp.moveaxis(tbl_g[rel_bucket(dist_s), hidx[..., None]], -1, 2)
        s_s = jnp.einsum('bqhgd,bhqnkd->bhgqnk', qb, kg).astype(jnp.float32) * scale + bias_s
        shp = s_s.shape
        m_s = (dist_s >= 0)[:, :, None].reshape(B, NSA_KV_HEADS, 1, NSA_QBLOCK, -1)
        p_s = masked_softmax(s_s.reshape(shp[0], shp[1], shp[2], shp[3], -1), m_s).reshape(shp)
        o_s = jnp.einsum('bhgqnk,bhqnkd->bqhgd', p_s.astype(vg.dtype), vg)
        kwb = lax.dynamic_slice_in_dim(kw_pad, start, WINDOW + NSA_QBLOCK, axis=1)
        vwb = lax.dynamic_slice_in_dim(vw_pad, start, WINDOW + NSA_QBLOCK, axis=1)
        s_pos = start - WINDOW + win_off
        dist_w = t[:, None] - s_pos[None, :]
        m_w = (dist_w >= 0) & (dist_w < WINDOW) & (s_pos >= 0)[None, :]
        s_w = jnp.einsum('bqhgd,bkhd->bhgqk', qb, kwb).astype(jnp.float32) * scale + head_bias(dist_w)
        p_w = masked_softmax(s_w, m_w)
        o_w = jnp.einsum('bhgqk,bkhd->bqhgd', p_w.astype(vwb.dtype), vwb)
        return gb[..., 0:1] * o_c + gb[..., 1:2] * o_s + gb[..., 2:3] * o_w

    out = lax.map(block, jnp.arange(S // NSA_QBLOCK))
    return jnp.swapaxes(out, 0, 1).reshape(B, S, NSA_HEADS * HEAD_DIM)

def stick_breaking_attention(q, k, v):
    B, S = q.shape[0], q.shape[1]
    scale = HEAD_DIM ** -0.5
    key_pos = jnp.arange(S)

    def block(i):
        start = i * SB_QBLOCK
        t = start + jnp.arange(SB_QBLOCK)
        qb = lax.dynamic_slice_in_dim(q, start, SB_QBLOCK, axis=1)
        z = jnp.einsum('bqhd,bshd->bhqs', qb, k).astype(jnp.float32) * scale
        mask = key_pos[None, :] < t[:, None]
        log_keep = jnp.where(mask, jax.nn.log_sigmoid(-z), 0.0)
        suffix = lax.cumsum(log_keep, axis=3, reverse=True) - log_keep
        a = jnp.where(mask, jnp.exp(jax.nn.log_sigmoid(z) + suffix), 0.0)
        return jnp.einsum('bhqs,bshd->bqhd', a.astype(v.dtype), v)

    out = lax.map(block, jnp.arange(S // SB_QBLOCK))
    return jnp.swapaxes(out, 0, 1).reshape(B, S, SB_HEADS * HEAD_DIM)

def first_inputs(seed: int = 0) -> dict:
    key = jax.random.key(seed)
    ks = jax.random.split(key, 20)
    f32 = jnp.float32
    nrm = lambda k, shape, s: jax.random.normal(k, shape, f32) * s
    gain = lambda k, shape: 1.0 + 0.02 * jax.random.normal(k, shape, f32)
    return {
        'x': nrm(ks[0], (BATCH, SEQ, D_MODEL), 1.0),
        'c': nrm(ks[1], (BATCH, D_MODEL), 1.0),
        'rel_bias': nrm(ks[2], (N_BUCKETS, NSA_HEADS), 0.5),
        'ada_w': nrm(ks[3], (DEPTH, D_MODEL, 6 * D_MODEL), 0.5 * D_MODEL ** -0.5),
        'ada_b': nrm(ks[4], (DEPTH, 6 * D_MODEL), 0.02),
        'norm1_g': gain(ks[5], (DEPTH, D_MODEL)),
        'norm2_g': gain(ks[6], (DEPTH, D_MODEL)),
        'w_in': nrm(ks[7], (DEPTH, D_MODEL, IN_WIDTH), D_MODEL ** -0.5),
        'cmp_pos': nrm(ks[8], (DEPTH, CMP_BLOCK, HEAD_DIM), 0.5),
        'cmp_k_w1': nrm(ks[9], (DEPTH, CMP_BLOCK * HEAD_DIM, CMP_HIDDEN), (CMP_BLOCK * HEAD_DIM) ** -0.5),
        'cmp_k_w2': nrm(ks[10], (DEPTH, CMP_HIDDEN, HEAD_DIM), CMP_HIDDEN ** -0.5),
        'cmp_v_w1': nrm(ks[11], (DEPTH, CMP_BLOCK * HEAD_DIM, CMP_HIDDEN), (CMP_BLOCK * HEAD_DIM) ** -0.5),
        'cmp_v_w2': nrm(ks[12], (DEPTH, CMP_HIDDEN, HEAD_DIM), CMP_HIDDEN ** -0.5),
        'q_norm_g': gain(ks[13], (DEPTH, HEAD_DIM)),
        'k_norm_g': gain(ks[14], (DEPTH, 3, HEAD_DIM)),
        'w_up_nsa': nrm(ks[15], (DEPTH, Q_A_W, D_MODEL), Q_A_W ** -0.5),
        'w_up_sb': nrm(ks[16], (DEPTH, SB_W, D_MODEL), SB_W ** -0.5),
        'w_out': nrm(ks[17], (DEPTH, D_MODEL, D_MODEL), D_MODEL ** -0.5),
        'mlp_w1': nrm(ks[18], (DEPTH, D_MODEL, D_FF), D_MODEL ** -0.5),
        'mlp_w2': nrm(ks[19], (DEPTH, D_FF, D_MODEL), D_FF ** -0.5),
    }

def first_block(x, c, rel_bias, ada_w, ada_b, norm1_g, norm2_g, w_in, cmp_pos, cmp_k_w1, cmp_k_w2, cmp_v_w1, cmp_v_w2, q_norm_g, k_norm_g, w_up_nsa, w_up_sb, w_out, mlp_w1, mlp_w2):
    B, S, _ = x.shape
    split_at = np.cumsum(IN_SPLITS)[:-1].tolist()
    kv_shape = (B, S, NSA_KV_HEADS, HEAD_DIM)
    sb_shape = (B, S, SB_HEADS, HEAD_DIM)
    h = x
    for layer in range(DEPTH):
        mod = jax.nn.silu(c) @ ada_w[layer] + ada_b[layer]
        shift1, scale1, gate1, shift2, scale2, gate2 = [m[:, None, :] for m in jnp.split(mod, 6, axis=-1)]
        u = rms_norm(h, norm1_g[layer]) * (1 + scale1) + shift1
        z = u @ w_in[layer]
        q_a, kc, vc, ksl, vsl, kwn, vwn, g_a, q_b, k_b, v_b, m_a, m_b = jnp.split(z, split_at, axis=-1)
        q_a = rms_norm(q_a.reshape(B, S, NSA_HEADS, HEAD_DIM), q_norm_g[layer]).reshape(B, S, NSA_KV_HEADS, NSA_GROUP, HEAD_DIM)
        k_cmp = rms_norm(compress_blocks(kc.reshape(kv_shape), cmp_pos[layer], cmp_k_w1[layer], cmp_k_w2[layer]), k_norm_g[layer, 0])
        v_cmp = compress_blocks(vc.reshape(kv_shape), cmp_pos[layer], cmp_v_w1[layer], cmp_v_w2[layer])
        k_slc = rms_norm(ksl.reshape(kv_shape), k_norm_g[layer, 1])
        k_win = rms_norm(kwn.reshape(kv_shape), k_norm_g[layer, 2])
        g_nsa = jax.nn.sigmoid(g_a).reshape(B, S, NSA_KV_HEADS, NSA_GROUP, 3)
        y_a = nsa_attention(q_a, k_cmp, v_cmp, k_slc, vsl.reshape(kv_shape), k_win, vwn.reshape(kv_shape), g_nsa, rel_bias) @ w_up_nsa[layer]
        y_b = stick_breaking_attention(q_b.reshape(sb_shape), k_b.reshape(sb_shape), v_b.reshape(sb_shape)) @ w_up_sb[layer]
        mixed = (jax.nn.sigmoid(m_a) * y_a + jax.nn.sigmoid(m_b) * y_b) @ w_out[layer]
        h = h + gate1 * mixed
        u2 = rms_norm(h, norm2_g[layer]) * (1 + scale2) + shift2
        ff = jnp.square(jax.nn.relu(u2 @ mlp_w1[layer])) @ mlp_w2[layer]
        h = h + gate2 * ff
    return h


D_MIX = D_MODEL
D_MLSTM = D_MIX // 2
D_MOBA = D_MIX - D_MLSTM
MLSTM_HEADS = 4
MLSTM_HEAD_DIM = D_MLSTM // MLSTM_HEADS
MLSTM_CHUNK = 64
CONV_WIDTH = 4
MOBA_HEADS = 8
MOBA_HEAD_DIM = D_MOBA // MOBA_HEADS
MOBA_BLOCK = 256
MOBA_TOPK = 3
MOBA_Q_CHUNK = 32
N_GROUPS = 4
EXPERTS_PER_GROUP = 8
N_EXPERTS = N_GROUPS * EXPERTS_PER_GROUP
EXPERT_TOPK = 2
D_EXPERT = 512
MOE_ROW_BLOCK = 256
IN_COLS = 4 * D_MLSTM + 2 * MLSTM_HEADS + 3 * D_MOBA


def rms_norm_2(x, g):
    xf = x.astype(jnp.float32)
    y = xf * lax.rsqrt(jnp.mean(xf * xf, axis=-1, keepdims=True) + EPS)
    return (y * g.astype(jnp.float32)).astype(x.dtype)

def split_heads(a, n_heads):
    b, s, _ = a.shape
    return a.reshape(b, s, n_heads, -1).transpose(0, 2, 1, 3)

def merge_heads(a):
    b, h, s, d = a.shape
    return a.transpose(0, 2, 1, 3).reshape(b, s, h * d)

def causal_depthwise_conv(x, w, b):
    s = x.shape[1]
    xp = jnp.pad(x, ((0, 0), (CONV_WIDTH - 1, 0), (0, 0)))
    y = b
    for j in range(CONV_WIDTH):
        y = y + w[j] * xp[:, j:j + s]
    return y

def mlstm_chunkwise(q, k, v, i_pre, f_pre):
    b, h, s, d = q.shape
    dv = v.shape[-1]
    nc = s // MLSTM_CHUNK
    out_dtype = v.dtype
    qf = q.astype(jnp.float32) * (d ** -0.5)
    kf = k.astype(jnp.float32)
    vf = v.astype(jnp.float32)
    log_i = i_pre.astype(jnp.float32)
    log_f = jax.nn.log_sigmoid(f_pre.astype(jnp.float32))

    def to_chunks(a):
        a = a.reshape(b, h, nc, MLSTM_CHUNK, *a.shape[3:])
        return jnp.moveaxis(a, 2, 0)

    causal = jnp.tril(jnp.ones((MLSTM_CHUNK, MLSTM_CHUNK), dtype=bool))

    def step(carry, inp):
        C, n, m = carry
        qt, kt, vt, it, ft = inp
        cum_f = jnp.cumsum(ft, axis=-1)
        cum_last = cum_f[..., -1]
        dmat = cum_f[..., :, None] - cum_f[..., None, :] + it[..., None, :]
        dmat = jnp.where(causal, dmat, -jnp.inf)
        inter = cum_f + m[..., None]
        m_t = jnp.maximum(inter, jnp.max(dmat, axis=-1))
        w_inter = jnp.exp(inter - m_t)
        sc = jnp.einsum('bhtd,bhsd->bhts', qt, kt) * jnp.exp(dmat - m_t[..., None])
        num = w_inter[..., None] * jnp.einsum('bhtd,bhde->bhte', qt, C) + jnp.einsum('bhts,bhse->bhte', sc, vt)
        den = w_inter * jnp.einsum('bhtd,bhd->bht', qt, n) + jnp.sum(sc, axis=-1)
        h_t = num / jnp.maximum(jnp.abs(den), jnp.exp(-m_t))[..., None]
        g_end = cum_last[..., None] - cum_f + it
        m_new = jnp.maximum(cum_last + m, jnp.max(g_end, axis=-1))
        w_old = jnp.exp(cum_last + m - m_new)
        w_new = jnp.exp(g_end - m_new[..., None])
        C_new = w_old[..., None, None] * C + jnp.einsum('bhs,bhsd,bhse->bhde', w_new, kt, vt)
        n_new = w_old[..., None] * n + jnp.einsum('bhs,bhsd->bhd', w_new, kt)
        return (C_new, n_new, m_new), h_t

    init = (jnp.zeros((b, h, d, dv), jnp.float32), jnp.zeros((b, h, d), jnp.float32),
            jnp.zeros((b, h), jnp.float32))
    _, hs = lax.scan(step, init, (to_chunks(qf), to_chunks(kf), to_chunks(vf),
                                  to_chunks(log_i), to_chunks(log_f)))
    return jnp.moveaxis(hs, 0, 2).reshape(b, h, s, dv).astype(out_dtype)

def moba_attention(q, k, v):
    b, h, s, d = q.shape
    nb = -(-s // MOBA_BLOCK)
    pad = nb * MOBA_BLOCK - s
    kp = jnp.pad(k.astype(jnp.float32), ((0, 0), (0, 0), (0, pad), (0, 0)))
    vp = jnp.pad(v.astype(jnp.float32), ((0, 0), (0, 0), (0, pad), (0, 0)))
    kb = kp.reshape(b, h, nb, MOBA_BLOCK, d)
    vb = vp.reshape(b, h, nb, MOBA_BLOCK, d)
    k_mean = jnp.mean(kb, axis=3)
    scale = d ** -0.5
    n_sel = min(MOBA_TOPK, nb - 1)
    bi = jnp.arange(b)[:, None, None, None]
    hi = jnp.arange(h)[None, :, None, None]
    blk_ids = jnp.arange(nb)

    def chunk(ci):
        t0 = ci * MOBA_Q_CHUNK
        qc = lax.dynamic_slice_in_dim(q, t0, MOBA_Q_CHUNK, axis=2).astype(jnp.float32)
        q_pos = t0 + jnp.arange(MOBA_Q_CHUNK)
        own = t0 // MOBA_BLOCK
        k_own = lax.dynamic_index_in_dim(kb, own, axis=2, keepdims=False)
        v_own = lax.dynamic_index_in_dim(vb, own, axis=2, keepdims=False)
        own_pos = own * MOBA_BLOCK + jnp.arange(MOBA_BLOCK)
        s_own = jnp.einsum('bhqd,bhkd->bhqk', qc, k_own) * scale
        s_own = jnp.where(own_pos[None, :] <= q_pos[:, None], s_own, -jnp.inf)
        if n_sel > 0:
            gate = jnp.einsum('bhqd,bhnd->bhqn', qc, k_mean)
            gate = jnp.where(blk_ids < own, gate, -jnp.inf)
            _, sel = lax.top_k(gate, n_sel)
            valid = sel < own
            k_sel = kb[bi, hi, sel]
            v_sel = vb[bi, hi, sel]
            s_sel = jnp.einsum('bhqd,bhqskd->bhqsk', qc, k_sel) * scale
            s_sel = jnp.where(valid[..., None], s_sel, -jnp.inf)
            p = jax.nn.softmax(jnp.concatenate(
                [s_sel.reshape(b, h, MOBA_Q_CHUNK, n_sel * MOBA_BLOCK), s_own], axis=-1), axis=-1)
            p_sel = p[..., :n_sel * MOBA_BLOCK].reshape(b, h, MOBA_Q_CHUNK, n_sel, MOBA_BLOCK)
            p_own = p[..., n_sel * MOBA_BLOCK:]
            return (jnp.einsum('bhqsk,bhqskd->bhqd', p_sel, v_sel)
                    + jnp.einsum('bhqk,bhkd->bhqd', p_own, v_own))
        p_own = jax.nn.softmax(s_own, axis=-1)
        return jnp.einsum('bhqk,bhkd->bhqd', p_own, v_own)

    outs = lax.map(chunk, jnp.arange(s // MOBA_Q_CHUNK))
    return jnp.moveaxis(outs, 0, 2).reshape(b, h, s, d).astype(q.dtype)

def hierarchical_moe(hx, w_rg, b_rg, w_re, b_re, w_gate, w_up, w_down):
    b, s, dm = hx.shape
    t = b * s
    xt = hx.reshape(t, dm)
    g_prob = jax.nn.softmax((xt @ w_rg).astype(jnp.float32) + b_rg, axis=-1)
    g_w, g_idx = lax.top_k(g_prob, 1)
    e_logits = ((xt @ w_re).astype(jnp.float32) + b_re).reshape(t, N_GROUPS, EXPERTS_PER_GROUP)
    e_logits = jnp.take_along_axis(e_logits, g_idx[:, :, None], axis=1)[:, 0]
    e_top, e_loc = lax.top_k(e_logits, EXPERT_TOPK)
    e_w = jax.nn.softmax(e_top, axis=-1) * g_w
    e_id = g_idx * EXPERTS_PER_GROUP + e_loc

    n_assign = t * EXPERT_TOPK
    flat_e = e_id.reshape(n_assign)
    flat_tok = jnp.repeat(jnp.arange(t), EXPERT_TOPK)
    flat_w = e_w.reshape(n_assign)
    order = jnp.argsort(flat_e)
    se, stok, sw = flat_e[order], flat_tok[order], flat_w[order]
    counts = jnp.zeros((N_EXPERTS,), jnp.int32).at[flat_e].add(1)
    starts = jnp.cumsum(counts) - counts
    padded = (counts + MOE_ROW_BLOCK - 1) // MOE_ROW_BLOCK * MOE_ROW_BLOCK
    pad_ends = jnp.cumsum(padded)
    pad_starts = pad_ends - padded
    dest = pad_starts[se] + (jnp.arange(n_assign) - starts[se])
    n_blocks = -(-n_assign // MOE_ROW_BLOCK) + N_EXPERTS
    rows = n_blocks * MOE_ROW_BLOCK
    x_pad = jnp.zeros((rows, dm), hx.dtype).at[dest].set(xt[stok])
    blk_expert = jnp.minimum(
        jnp.searchsorted(pad_ends, jnp.arange(n_blocks) * MOE_ROW_BLOCK, side='right'), N_EXPERTS - 1)

    def run_block(args):
        xb, e = args
        return (jax.nn.silu(xb @ w_gate[e]) * (xb @ w_up[e])) @ w_down[e]

    y_pad = lax.map(run_block, (x_pad.reshape(n_blocks, MOE_ROW_BLOCK, dm), blk_expert))
    y_sorted = y_pad.reshape(rows, dm)[dest].astype(jnp.float32)
    out = jnp.zeros((t, dm), jnp.float32).at[stok].add(y_sorted * sw[:, None])
    return out.reshape(b, s, dm).astype(hx.dtype)

def second_inputs(seed: int = 0) -> dict:
    key = jax.random.key(seed)
    ks = jax.random.split(key, 24)
    f32 = jnp.float32

    def nrm(k, shape, sc):
        return sc * jax.random.normal(k, shape, f32)

    L = DEPTH
    x = nrm(ks[0], (BATCH, SEQ, D_MODEL), 1.0)
    c = nrm(ks[1], (BATCH, D_MODEL), 1.0)
    w_ada = nrm(ks[2], (L, D_MODEL, 6 * D_MODEL), 0.5 * D_MODEL ** -0.5)
    b_ada = nrm(ks[3], (L, 6 * D_MODEL), 0.02)
    g_norm1 = 1.0 + nrm(ks[4], (L, D_MODEL), 0.02)
    w_in = nrm(ks[5], (L, D_MODEL, IN_COLS), D_MODEL ** -0.5)
    w_conv = nrm(ks[6], (L, CONV_WIDTH, 2 * D_MLSTM), CONV_WIDTH ** -0.5)
    b_conv = nrm(ks[7], (L, 2 * D_MLSTM), 0.02)
    b_i = nrm(ks[8], (L, MLSTM_HEADS), 0.1)
    b_f = jnp.linspace(3.0, 6.0, MLSTM_HEADS, dtype=f32) + nrm(ks[9], (L, MLSTM_HEADS), 0.1)
    b_gates = jnp.concatenate([b_i, b_f], axis=-1)
    g_mlstm_head = 1.0 + nrm(ks[10], (L, D_MLSTM), 0.02)
    w_out = nrm(ks[11], (L, D_MIX, D_MODEL), D_MIX ** -0.5)
    g_norm2 = 1.0 + nrm(ks[12], (L, D_MODEL), 0.02)
    w_router_group = nrm(ks[13], (L, D_MODEL, N_GROUPS), D_MODEL ** -0.5)
    b_router_group = nrm(ks[14], (L, N_GROUPS), 0.01)
    w_router_expert = nrm(ks[15], (L, D_MODEL, N_EXPERTS), D_MODEL ** -0.5)
    b_router_expert = nrm(ks[16], (L, N_EXPERTS), 0.01)
    w_expert_gate = nrm(ks[17], (L, N_EXPERTS, D_MODEL, D_EXPERT), D_MODEL ** -0.5)
    w_expert_up = nrm(ks[18], (L, N_EXPERTS, D_MODEL, D_EXPERT), D_MODEL ** -0.5)
    w_expert_down = nrm(ks[19], (L, N_EXPERTS, D_EXPERT, D_MODEL), D_EXPERT ** -0.5)
    g_final = 1.0 + nrm(ks[20], (D_MODEL,), 0.02)
    return {'x': x, 'c': c, 'w_ada': w_ada, 'b_ada': b_ada, 'g_norm1': g_norm1, 'w_in': w_in,
            'w_conv': w_conv, 'b_conv': b_conv, 'b_gates': b_gates, 'g_mlstm_head': g_mlstm_head,
            'w_out': w_out, 'g_norm2': g_norm2, 'w_router_group': w_router_group,
            'b_router_group': b_router_group, 'w_router_expert': w_router_expert,
            'b_router_expert': b_router_expert, 'w_expert_gate': w_expert_gate,
            'w_expert_up': w_expert_up, 'w_expert_down': w_expert_down, 'g_final': g_final}

def second_block(x, c, w_ada, b_ada, g_norm1, w_in, w_conv, b_conv, b_gates, g_mlstm_head,
              w_out, g_norm2, w_router_group, b_router_group, w_router_expert,
              b_router_expert, w_expert_gate, w_expert_up, w_expert_down, g_final):
    split_at = np.cumsum([D_MLSTM, D_MLSTM, D_MLSTM, D_MLSTM, 2 * MLSTM_HEADS, D_MOBA, D_MOBA]).tolist()
    for l in range(DEPTH):
        mod = jax.nn.silu(c) @ w_ada[l] + b_ada[l]
        shift1, scale1, gate1, shift2, scale2, gate2 = [m[:, None, :] for m in jnp.split(mod, 6, axis=-1)]

        hn = rms_norm_2(x, g_norm1[l]) * (1.0 + scale1) + shift1
        proj = hn @ w_in[l]
        q_m, k_m, v_m, o_m, gates, q_a, k_a, v_a = jnp.split(proj, split_at, axis=-1)

        qk = jax.nn.silu(causal_depthwise_conv(jnp.concatenate([q_m, k_m], axis=-1), w_conv[l], b_conv[l]))
        q_m, k_m = jnp.split(qk, 2, axis=-1)
        gates = gates + b_gates[l]
        i_pre = gates[..., :MLSTM_HEADS].transpose(0, 2, 1)
        f_pre = gates[..., MLSTM_HEADS:].transpose(0, 2, 1)
        h_m = mlstm_chunkwise(split_heads(q_m, MLSTM_HEADS), split_heads(k_m, MLSTM_HEADS),
                              split_heads(v_m, MLSTM_HEADS), i_pre, f_pre)
        h_m = rms_norm_2(h_m, g_mlstm_head[l].reshape(MLSTM_HEADS, 1, MLSTM_HEAD_DIM))
        h_m = merge_heads(h_m) * jax.nn.sigmoid(o_m)

        h_a = merge_heads(moba_attention(split_heads(q_a, MOBA_HEADS), split_heads(k_a, MOBA_HEADS),
                                         split_heads(v_a, MOBA_HEADS)))

        mix = jnp.concatenate([h_m, h_a], axis=-1) @ w_out[l]
        x = x + gate1 * mix

        hn2 = rms_norm_2(x, g_norm2[l]) * (1.0 + scale2) + shift2
        ffn = hierarchical_moe(hn2, w_router_group[l], b_router_group[l], w_router_expert[l],
                               b_router_expert[l], w_expert_gate[l], w_expert_up[l], w_expert_down[l])
        x = x + gate2 * ffn
    return rms_norm_2(x, g_final)


def setup_inputs(seed=0):
    out = dict(first_inputs(seed))
    for name, value in second_inputs(seed + 1).items():
        if name != "x":
            out[name + "_2"] = value
    return out


def reference(
    x, c, rel_bias, ada_w, ada_b, norm1_g, norm2_g, w_in, cmp_pos, cmp_k_w1, cmp_k_w2, cmp_v_w1,
    cmp_v_w2, q_norm_g, k_norm_g, w_up_nsa, w_up_sb, w_out, mlp_w1, mlp_w2, c_2, w_ada_2,
    b_ada_2, g_norm1_2, w_in_2, w_conv_2, b_conv_2, b_gates_2, g_mlstm_head_2, w_out_2,
    g_norm2_2, w_router_group_2, b_router_group_2, w_router_expert_2, b_router_expert_2,
    w_expert_gate_2, w_expert_up_2, w_expert_down_2, g_final_2,
):
    x = first_block(
        x, c, rel_bias, ada_w, ada_b, norm1_g, norm2_g, w_in, cmp_pos, cmp_k_w1, cmp_k_w2,
        cmp_v_w1, cmp_v_w2, q_norm_g, k_norm_g, w_up_nsa, w_up_sb, w_out, mlp_w1, mlp_w2,
    )
    return second_block(
        x, c_2, w_ada_2, b_ada_2, g_norm1_2, w_in_2, w_conv_2, b_conv_2, b_gates_2,
        g_mlstm_head_2, w_out_2, g_norm2_2, w_router_group_2, b_router_group_2,
        w_router_expert_2, b_router_expert_2, w_expert_gate_2, w_expert_up_2, w_expert_down_2,
        g_final_2,
    )


_drawn_inputs = setup_inputs


def setup_inputs(seed=0):
    import zlib

    import numpy as np

    out = dict(_drawn_inputs(seed))
    spreads = {}
    factors = {'rel_bias': 3.833,
     'norm1_g': 8.0,
     'norm2_g': 4.341,
     'cmp_k_w1': 3.564,
     'cmp_k_w2': 3.469,
     'q_norm_g': 8.0,
     'k_norm_g': 8.0,
     'b_ada_2': 3.022,
     'g_norm1_2': 8.0,
     'b_conv_2': 64.0,
     'g_mlstm_head_2': 30.457,
     'g_norm2_2': 5.202,
     'b_router_group_2': 32.209,
     'b_router_expert_2': 23.829,
     'g_final_2': 20.462}
    for name, (base, spread) in spreads.items():
        noise = np.random.default_rng([zlib.crc32(name.encode()), seed]).standard_normal(out[name].shape)
        drawn = base * np.exp(spread * noise) if base else spread * noise
        out[name] = __import__('jax').numpy.asarray(drawn.astype(out[name].dtype))
    for name, factor in factors.items():
        out[name] = (out[name] * factor).astype(out[name].dtype)
    return out
```

```python
from contextlib import ExitStack, nullcontext

import numpy as np

import concourse.bass as bass
from concourse import mybir

ALU = mybir.AluOpType
ACT = mybir.ActivationFunctionType
AX = mybir.AxisListType
F32 = mybir.dt.float32
U32 = mybir.dt.uint32
I32 = mybir.dt.int32

P = 128
TOK = 512
NT = TOK // P
D = 1024
KD = D // P
HD = 64
FF = 4096
BUCKETS = 32
CMP = 32
STRIDE = 16
NCMP = (TOK - CMP) // STRIDE + 1
EPS = 1e-6
BIG = 1e30
EXPERTS = 32
DE = 512
CAP = 64
PAIRS = EXPERTS // 2
LEVELS = TOK // CAP
OFF = [P * (j * (j + 1) // 2) for j in range(NT + 1)]
BIAS_X = 640
DIST0 = 528
FWD = 1024

_INS = [
    "x", "c", "rel_bias", "ada_w", "ada_b", "norm1_g", "norm2_g", "w_in", "cmp_pos", "cmp_k_w1",
    "cmp_k_w2", "cmp_v_w1", "cmp_v_w2", "q_norm_g", "k_norm_g", "w_up_nsa", "w_up_sb", "w_out",
    "mlp_w1", "mlp_w2", "c_2", "w_ada_2", "b_ada_2", "g_norm1_2", "w_in_2", "w_conv_2", "b_conv_2",
    "b_gates_2", "g_mlstm_head_2", "w_out_2", "g_norm2_2", "w_router_group_2",
    "b_router_group_2", "w_router_expert_2", "b_router_expert_2", "w_expert_gate_2",
    "w_expert_up_2", "w_expert_down_2", "g_final_2",
]


class Scope(ExitStack):

    used = []

    def __init__(self, nc):
        super().__init__()
        self.nc = nc

    @classmethod
    def clear(cls, nc):
        nc.clear_and_free_semaphores(cls.used)
        nc.all_engine_barrier()
        cls.used.clear()

    def sb(self, name, shape, dt=F32):
        return self.enter_context(self.nc.sbuf_tensor(name, shape, dt))

    def bank(self, name):
        return self.enter_context(self.nc.psum_tensor(name, [P, 512], F32))

    def sem(self, name):
        sem = self.nc.alloc_semaphore(name=name)
        self.used.append(sem)
        return sem

    def sems(self, name, n):
        return [self.sem(f"{name}{i}") for i in range(n)]


class Chain:

    def __init__(self, eng, sem, base=0):
        self.eng, self.sem, self.base, self.n = eng, sem, base, 0

    def link(self, ins):
        self.n += 1
        ins.then_inc(self.sem, 1)
        self.eng.wait_ge(self.sem, self.base + self.n)


def bcast(ap, n):
    return bass.AP(tensor=ap.tensor, offset=ap.offset, ap=[*ap.ap, [0, n]])


def rows_to_all(ap, n):
    return bass.AP(tensor=ap.tensor, offset=ap.offset, ap=[[0, P], [1, n]])


def chunk(w, col, n):
    return w[:, col:col + n].rearrange("(k p) n -> p k n", p=P)


def constants(nc, C, A):
    with Scope(nc) as s:
        rows1 = s.sb("rows1", [P, P])
        rows2 = s.sb("rows2", [P, P])
        turned = s.bank("turned_ps")
        rows_in = s.sem("rows_in")
        made = s.sem("made")
        zeroed = s.sem("zeroed")
        cols_ready = s.sem("cols_ready")
        x_in = s.sem("x_in")
        with nc.Block() as block:
            @block.sync
            def _(sp):
                sp.dma_start(C.h[:, :, :], A["x"][0].rearrange("(t p) d -> p t d", p=P)).then_inc(x_in, 16)
                sp.wait_ge(zeroed, 2)
                r = lambda ap: ap.rearrange("(r n) -> r n", n=P)
                rows = lambda dst, src: sp.dma_start(dst, src).then_inc(rows_in, 16)
                rows(rows1[0:48, :], r(A["ada_b"][0]))
                rows(rows1[48:56, :], r(A["c"][0]))
                rows(rows1[56:64, :], r(A["norm1_g"][0]))
                rows(rows1[64:72, :], r(A["norm2_g"][0]))
                g64 = [A["q_norm_g"][0]] + [A["k_norm_g"][0, i] for i in range(3)]
                for i, g in enumerate(g64):
                    for half in range(2):
                        rows(rows1[72 + i:73 + i, 64 * half:64 * half + 64], g.rearrange("(a n) -> a n", a=1))
                rows(rows2[0:48, :], r(A["b_ada_2"][0]))
                rows(rows2[48:56, :], r(A["c_2"][0]))
                rows(rows2[56:64, :], r(A["g_norm1_2"][0]))
                rows(rows2[64:72, :], r(A["g_norm2_2"][0]))
                rows(rows2[72:104, :], A["w_conv_2"][0].rearrange("w (r n) -> (w r) n", n=P))
                rows(rows2[104:112, :], r(A["b_conv_2"][0]))
                rows(rows2[112:116, :], r(A["g_mlstm_head_2"][0]))
                sp.wait_ge(x_in, 16)

            @block.gpsimd
            def _(pool):
                ch = Chain(pool, made)
                ch.link(pool.memset(rows1[:, :], 0.0))
                ch.link(pool.memset(rows2[:, :], 0.0))
                pool.sem_inc(zeroed, 2)
                for m, v in ((C.neghalf, -0.5), (C.ident, 0.0), (C.ones, 1.0), (C.later, 0.0), (C.ban, 0.0),
                             (C.ban_self, 0.0), (C.allow, 0.0)):
                    ch.link(pool.memset(m[:, :], v))
                ch.link(pool.affine_select(out=C.ident[:, :], in_=C.ident[:, :], compare_op=ALU.not_equal,
                                           fill=1.0, base=0, pattern=[[-1, P]], channel_multiplier=1))
                ch.link(pool.affine_select(out=C.later[:, :], in_=C.later[:, :], compare_op=ALU.is_ge,
                                           fill=1.0, base=0, pattern=[[-1, P]], channel_multiplier=1))
                for m, op, fill in ((C.ban, ALU.is_ge, BIG), (C.ban_self, ALU.is_gt, -BIG), (C.allow, ALU.is_ge, -BIG)):
                    ch.link(pool.affine_select(out=m[:, :], in_=m[:, :], compare_op=op, fill=fill,
                                               base=384, pattern=[[-1, 512]], channel_multiplier=1))

            @block.vector
            def _(dve):
                dve.wait_ge(cols_ready, 2)
                nc.vector.tensor_copy(C.cols1[:, :], turned[:, 0:P])
                nc.vector.tensor_copy(C.cols2[:, :], turned[:, P:2 * P])

            @block.tensor
            def _(pe):
                pe.wait_ge(rows_in, 16 * 19)
                pe.wait_ge(made, 10)
                nc.tensor.transpose(turned[:, 0:P], rows1[:, :], C.ident[:, :]).then_inc(cols_ready, 1)
                nc.tensor.transpose(turned[:, P:2 * P], rows2[:, :], C.ident[:, :]).then_inc(cols_ready, 1)


def bias_tables(nc, C, A):
    with Scope(nc) as s:
        tbl = s.sb("tbl", [BUCKETS + 1, 8])
        onehot = s.sb("onehot", [BUCKETS + 1, BIAS_X + FWD])
        vrow = s.sb("vrow", [8, BIAS_X])
        vdram = nc.dram_tensor("bias_by_distance", [8, BIAS_X], F32).ap()
        upside = s.sb("upside", [P, 8, 512])
        flip = s.sb("flip", [P, P])
        fps = [s.bank("flip_ps0"), s.bank("flip_ps1")]
        zeroed = s.sem("flip_made")
        flipped = s.sem("flipped")
        b_copied = s.sem("b_copied")
        vps = [s.bank("v_ps0"), s.bank("v_ps1")]
        cps = [s.bank(f"c_ps{j}") for j in range(NT)]
        tbl_in = s.sem("tbl_in")
        negated = s.sem("negated")
        v_ready = s.sem("v_ready")
        c_ready = s.sem("c_ready")
        v_copied = s.sem("v_copied")
        v_out = s.sem("v_out")
        bias_in = s.sem("bias_in")
        with nc.Block() as block:
            @block.sync
            def _(sp):
                sp.dma_start(onehot[:, :], A["onehot"]).then_inc(tbl_in, 16)
                sp.dma_start(tbl[0:BUCKETS, :], A["rel_bias"]).then_inc(tbl_in, 16)
                sp.wait_ge(v_copied, 2)
                sp.dma_start(vdram, vrow[:, :]).then_inc(v_out, 16)
                sp.wait_ge(v_out, 16)
                src = bass.AP(tensor=vdram.tensor, offset=0, ap=[[1, P], [BIAS_X, 8], [1, 512]])
                sp.dma_start(upside[:, :, :], src).then_inc(bias_in, 16)

            @block.gpsimd
            def _(pool):
                pool.memset(tbl[BUCKETS:BUCKETS + 1, :], -BIG).then_inc(negated, 1)
                pool.wait_ge(negated, 1)
                pool.memset(flip[:, :], 0.0).then_inc(zeroed, 1)
                pool.wait_ge(zeroed, 1)
                pool.affine_select(out=flip[:, :], in_=flip[:, :], compare_op=ALU.not_equal, fill=1.0,
                                   base=-(P - 1), pattern=[[1, P]], channel_multiplier=1).then_inc(zeroed, 1)

            @block.vector
            def _(dve):
                dve.wait_ge(tbl_in, 32)
                dve.wait_ge(negated, 1)
                nc.vector.tensor_scalar(tbl[:, :], tbl[:, :], -1.0, None, ALU.mult).then_inc(negated, 1)
                dve.wait_ge(v_ready, 2)
                nc.vector.tensor_copy(vrow[:, 0:512], vps[0][0:8, :]).then_inc(v_copied, 1)
                nc.vector.tensor_copy(vrow[:, 512:BIAS_X], vps[1][0:8, 0:BIAS_X - 512]).then_inc(v_copied, 1)
                for j in range(NT):
                    dve.wait_ge(c_ready, j + 1)
                    src = cps[j][:, 0:256].rearrange("p (c f i) -> p i f c", f=2, i=4)
                    dst = C.cbias[:, j, :].rearrange("p (i f c) -> p i f c", i=4, f=2)
                    for i in range(4):
                        nc.vector.tensor_copy(dst[:, i], src[:, i]).then_inc(v_copied, 1)
                dve.wait_ge(v_copied, 2 + 4 * NT)
                nc.vector.tensor_scalar(C.cmask[:, :, :], C.cbias[:, :, 0:CMP], 1e29, None, ALU.is_lt)

            @block.scalar
            def _(act):
                for h in range(8):
                    act.wait_ge(flipped, h + 1)
                    nc.scalar.activation(C.bias[:, h, :], fps[h % 2][:, :], ACT.Copy).then_inc(b_copied, 1)

            @block.tensor
            def _(pe):
                pe.wait_ge(negated, 2)
                nc.tensor.matmul(vps[0][0:8, :], tbl[:, :], onehot[:, 0:512], start=True, stop=True).then_inc(v_ready, 1)
                nc.tensor.matmul(vps[1][0:8, 0:BIAS_X - 512], tbl[:, :], onehot[:, 512:BIAS_X],
                                 start=True, stop=True).then_inc(v_ready, 1)
                for j in range(NT):
                    for k in range(CMP):
                        y = BIAS_X + P * j - STRIDE * k - (CMP - 1) + DIST0
                        mm = nc.tensor.matmul(cps[j][:, 8 * k:8 * k + 8], onehot[:, y:y + P], tbl[:, :],
                                              start=True, stop=True)
                    mm.then_inc(c_ready, 1)
                pe.wait_ge(zeroed, 2)
                pe.wait_ge(bias_in, 16)
                for h in range(8):
                    if h >= 2:
                        pe.wait_ge(b_copied, h - 1)
                    nc.tensor.matmul(fps[h % 2][:, :], flip[:, :], upside[:, h, :], start=True, stop=True).then_inc(flipped, 1)


class Modulation:

    def __init__(self, s, nc, C, M, cols, w, bias, parts, tag):
        self.nc, self.C, self.M, self.cols, self.w, self.bias, self.parts = nc, C, M, cols, w, bias, parts
        self.units = [(m, n) for m in parts for n in range(2)]
        self.wbuf = [s.sb(f"adaw{i}{tag}", [P, KD, 512]) for i in range(2)]
        self.acc = [s.sb(f"acc{i}{tag}", [P, 512]) for i in range(2)]
        self.gbias = {m: s.sb(f"gbias{m}{tag}", [P, D]) for m in parts if m in (2, 5)}
        self.t = s.sb(f"t{tag}", [P, 4])
        self.ps = [s.bank(f"mod_ps{i}{tag}") for i in range(2)]
        self.landed = s.sems(f"ada_landed{tag}", 2)
        self.gb_in = s.sem(f"gb_in{tag}")
        self.summed = s.sem(f"ada_summed{tag}")
        self.spread_out = s.sem(f"ada_spread{tag}")
        self.finished = s.sem(f"ada_finished{tag}")
        self.own = s.sem(f"ada_own{tag}")
        self.chain = None

    def load(self, eng):
        for m, dst in self.gbias.items():
            eng.dma_start(dst[:, :], rows_to_all(self.bias[m * D:(m + 1) * D], D)).then_inc(self.gb_in, 16)
        for u, (m, n) in enumerate(self.units):
            if u >= 2:
                eng.wait_ge(self.summed, u - 1)
            eng.dma_start(self.wbuf[u % 2][:, :, :], chunk(self.w, m * D + 512 * n, 512)).then_inc(self.landed[u % 2], 16)

    def sum(self, dve, u):
        v, a, w, sc = self.nc.vector, self.acc[u % 2], self.wbuf[u % 2], self.M.sc
        self.chain = self.chain or Chain(dve, self.own)
        dve.wait_ge(self.landed[u % 2], 16 * (u // 2 + 1))
        if u >= 2:
            dve.wait_ge(self.spread_out, u - 1)
        self.chain.link(v.tensor_scalar(a[:, :], w[:, 0, :], sc[:, 0:1], None, ALU.mult))
        for k in range(1, KD):
            ins = v.scalar_tensor_tensor(out=a[:, :], in0=w[:, k, :], scalar=sc[:, k:k + 1], in1=a[:, :],
                                         op0=ALU.mult, op1=ALU.add)
            if k < KD - 1:
                self.chain.link(ins)
        ins.then_inc(self.summed, 1)

    def spread(self, pe, u):
        m, a, ps, ones = self.units[u][0], self.acc[u % 2], self.ps[u % 2], self.C.ones
        pe.wait_ge(self.summed, u + 1)
        if u >= 2:
            pe.wait_ge(self.finished, u - 1)
        if m in (2, 5):
            mm = self.nc.tensor.matmul(ps[:, :], ones[:, :], a[:, :], start=True, stop=True)
        else:
            for k in range(4):
                mm = self.nc.tensor.matmul(ps[:, k:k + 1], a[:, P * k:P * k + P], ones[:, 0:1], start=True, stop=True)
        mm.then_inc(self.spread_out, 1)

    def finish(self, dve, u):
        v, M, ps, (m, n) = self.nc.vector, self.M, self.ps[u % 2], self.units[u]
        c = slice(4 * n, 4 * n + 4)
        dve.wait_ge(self.spread_out, u + 1)
        if m in (2, 5):
            dve.wait_ge(self.gb_in, 16 * len(self.gbias))
            cols = slice(512 * n, 512 * n + 512)
            self.chain.link(v.tensor_tensor(M.gate[m // 3][:, cols], ps[:, :], self.gbias[m][:, cols], ALU.add))
        elif m in (0, 3):
            self.chain.link(v.tensor_tensor(M.shift[m // 3][:, c], ps[:, 0:4], self.cols[:, 8 * m + 4 * n:8 * m + 4 * n + 4],
                                            ALU.add))
        else:
            g = 56 + 8 * (m // 3) + 4 * n
            self.chain.link(v.tensor_tensor(self.t[:, :], ps[:, 0:4], self.cols[:, 8 * m + 4 * n:8 * m + 4 * n + 4], ALU.add))
            self.chain.link(v.scalar_tensor_tensor(out=M.scale[m // 3][:, c], in0=self.t[:, :], scalar=1.0,
                                                   in1=self.cols[:, g:g + 4], op0=ALU.add, op1=ALU.mult))
        dve.sem_inc(self.finished, 1)


def first_modulation(nc, C, M, A):
    with Scope(nc) as s:
        mod = Modulation(s, nc, C, M[0], C.cols1, A["ada_w"][0], A["ada_b"][0], [1, 0], "m1")
        sig_ready = s.sem("sc_sig")
        own = s.sem("sc_own")
        with nc.Block() as block:
            @block.sync
            def _(sp):
                mod.load(sp)

            @block.scalar
            def _(act):
                for b, cols in enumerate((C.cols1, C.cols2)):
                    nc.scalar.activation(M[b].sc[:, :], cols[:, 48:56], ACT.Sigmoid).then_inc(sig_ready, 1)

            @block.vector
            def _(dve):
                ch = Chain(dve, own)
                dve.wait_ge(sig_ready, 2)
                for b, cols in enumerate((C.cols1, C.cols2)):
                    ch.link(nc.vector.tensor_tensor(M[b].sc[:, :], M[b].sc[:, :], cols[:, 48:56], ALU.mult))
                for u in range(5):
                    if u < 4:
                        mod.sum(dve, u)
                    if u >= 1:
                        mod.finish(dve, u - 1)

            @block.tensor
            def _(pe):
                for u in range(4):
                    mod.spread(pe, u)


def norm_turn(nc, C, scale, shift, uT, tag, xn_dram=None):
    with Scope(nc) as s:
        xn = s.sb(f"xn{tag}", [P, NT, D])
        ssq = s.sb(f"ssq{tag}", [P, NT])
        var = s.sb(f"var{tag}", [P, NT])
        rstd = s.sb(f"rstd{tag}", [P, NT])
        ps = [s.bank(f"nt_ps{i}{tag}") for i in range(4)]
        squares = s.sem(f"squares{tag}")
        var_ready = s.sem(f"var_ready{tag}")
        rstd_ready = s.sem(f"rstd_ready{tag}")
        xn_ready = s.sem(f"xn_ready{tag}")
        turned = s.sem(f"turned{tag}")
        out_done = s.sems(f"out_done{tag}", 2)
        stored = s.sem(f"stored{tag}")
        with nc.Block() as block:
            @block.scalar
            def _(act):
                for t in range(NT):
                    nc.scalar.activation(xn[:, t, :], C.h[:, t, :], ACT.Square,
                                         accum_out=ssq[:, t:t + 1]).then_inc(squares, 1)
                for k in range(1, KD, 2):
                    act.wait_ge(turned, k + 1)
                    nc.scalar.activation(uT[:, k, :], ps[k % 4][:, :], ACT.Identity, scale=scale[:, k:k + 1],
                                         bias=shift[:, k:k + 1]).then_inc(out_done[1], 1)

            @block.gpsimd
            def _(pool):
                pool.wait_ge(var_ready, 1)
                pool.tensor_tensor(rstd[:, :], var[:, :], C.neghalf[:, 0:NT], ALU.pow).then_inc(rstd_ready, 1)

            @block.vector
            def _(dve):
                dve.wait_ge(squares, NT)
                nc.vector.tensor_scalar(var[:, :], ssq[:, :], 1.0 / D, EPS, ALU.mult, ALU.add).then_inc(var_ready, 1)
                dve.wait_ge(rstd_ready, 1)
                for t in range(NT):
                    nc.vector.tensor_scalar(xn[:, t, :], C.h[:, t, :], rstd[:, t:t + 1], None,
                                            ALU.mult).then_inc(xn_ready, 1)
                for k in range(0, KD, 2):
                    dve.wait_ge(turned, k + 1)
                    nc.vector.tensor_scalar(uT[:, k, :], ps[k % 4][:, :], scale[:, k:k + 1], shift[:, k:k + 1],
                                            ALU.mult, ALU.add).then_inc(out_done[0], 1)

            @block.tensor
            def _(pe):
                pe.wait_ge(xn_ready, NT)
                for k in range(KD):
                    if k >= 4:
                        pe.wait_ge(out_done[k % 2], k // 2 - 1)
                    for t in range(NT):
                        mm = nc.tensor.transpose(ps[k % 4][:, P * t:P * t + P], xn[:, t, P * k:P * k + P], C.ident[:, :])
                    mm.then_inc(turned, 1)

            if xn_dram is not None:
                @block.sync
                def _(sp):
                    sp.wait_ge(xn_ready, NT)
                    sp.dma_start(xn_dram.rearrange("(t p) d -> p t d", p=P), xn[:, :, :]).then_inc(stored, 16)
                    sp.wait_ge(stored, 16)


def project(nc, C, uT, w, steps, tag):
    with Scope(nc) as s:
        wbuf = [s.sb(f"pw{i}{tag}", [P, KD, 512]) for i in range(2)]
        ps = [[s.bank(f"pp{i}{b}{tag}") for b in range(4)] for i in range(2)]
        landed = s.sems(f"p_landed{tag}", 2)
        bank_ready = s.sem(f"bank_ready{tag}")
        bank_out = s.sem(f"bank_out{tag}")
        banks = [(n // P if turned else NT) for _, n, turned, _ in steps]
        upto = [sum(banks[:i]) for i in range(len(steps) + 1)]
        with nc.Block() as block:
            @block.sync
            def _(sp):
                for i, (col, n, _, _) in enumerate(steps):
                    if i >= 2:
                        sp.wait_ge(bank_ready, upto[i - 1])
                    sp.dma_start(wbuf[i % 2][:, :, 0:n], chunk(w, col, n)).then_inc(landed[i % 2], 16)

            @block.tensor
            def _(pe):
                for i, (_, n, turned, _) in enumerate(steps):
                    wt = wbuf[i % 2]
                    pe.wait_ge(landed[i % 2], 16 * (i // 2 + 1))
                    if i >= 2:
                        pe.wait_ge(bank_out, upto[i - 1])
                    for b in range(banks[i]):
                        for k in range(KD):
                            if turned:
                                mm = nc.tensor.matmul(ps[i % 2][b][:, :], wt[:, k, P * b:P * b + P], uT[:, k, :],
                                                      start=(k == 0), stop=(k == KD - 1))
                            else:
                                mm = nc.tensor.matmul(ps[i % 2][b][:, 0:n], uT[:, k, P * b:P * b + P], wt[:, k, 0:n],
                                                      start=(k == 0), stop=(k == KD - 1))
                        mm.then_inc(bank_ready, 1)

            @block.scalar
            def _(act):
                for i, (_, _, _, out) in enumerate(steps):
                    for b in range(banks[i]):
                        act.wait_ge(bank_ready, upto[i] + b + 1)
                        for dst, src, func, scale in out(b, ps[i % 2][b]):
                            ins = nc.scalar.activation(dst, src, func, scale=scale)
                        ins.then_inc(bank_out, 1)



def head_norms(nc, C, B):
    with Scope(nc) as s:
        sq = s.sb("sq", [P, NT * 512])
        kn = s.sb("kn", [P, NT, 2, P])
        ss = s.sb("ss", [P, 48])
        rs = s.sb("rs", [P, 48])
        qn = s.sb("qn", [P, NT, 4, 2, HD])
        ps = [s.bank(f"hn_ps{i}") for i in range(6)]
        own = s.sem("hn_own")
        var_ready = s.sem("hn_var")
        rs_ready = s.sem("hn_rs")
        qn_ready = s.sem("qn_ready")
        turned = s.sem("hn_turned")
        zeroed = s.sem("hn_zeroed")
        with nc.Block() as block:
            @block.vector
            def _(dve):
                ch = Chain(dve, own)
                q = B.qa[:, :, :].rearrange("p t n -> p (t n)")
                ch.link(nc.vector.tensor_tensor(sq[:, :], q, q, ALU.mult))
                ch.link(nc.vector.tensor_reduce(ss[:, 0:32], sq[:, :].rearrange("p (h d) -> p h d", d=HD), AX.X, ALU.add))
                for w in range(2):
                    k = B.kv[:, :, 256 * w:256 * w + P]
                    o = sq[:, 0:NT * P].rearrange("p (t n) -> p t n", t=NT)
                    ch.link(nc.vector.tensor_tensor(o, k, k, ALU.mult))
                    ch.link(nc.vector.tensor_reduce(ss[:, 32 + 8 * w:40 + 8 * w],
                                                    sq[:, 0:NT * P].rearrange("p (h d) -> p h d", d=HD), AX.X, ALU.add))
                nc.vector.tensor_scalar(ss[:, :], ss[:, :], 1.0 / HD, EPS, ALU.mult, ALU.add).then_inc(var_ready, 1)
                dve.wait_ge(rs_ready, 1)
                for t in range(NT):
                    src = B.qa[:, t, :].rearrange("p (f i d) -> p i f d", f=2, i=4)
                    r = rs[:, 8 * t:8 * t + 8].rearrange("p (f i) -> p f i", f=2)
                    for f in range(2):
                        nc.vector.tensor_tensor(qn[:, t, :, f, :], src[:, :, f, :], bcast(r[:, f, :], HD), ALU.mult)
                    for w in range(2):
                        ins = nc.vector.tensor_tensor(
                            kn[:, t, w, :].rearrange("p (f d) -> p f d", f=2),
                            B.kv[:, t, 256 * w:256 * w + P].rearrange("p (f d) -> p f d", f=2),
                            bcast(rs[:, 32 + 8 * w + 2 * t:34 + 8 * w + 2 * t], HD), ALU.mult)
                    ins.then_inc(qn_ready, 1)
                for i in range(4):
                    dve.wait_ge(turned, i + 1)
                    nc.vector.tensor_scalar(B.qT[:, i, :], ps[i][:, :], C.cols1[:, 72:73], -HD ** -0.5, ALU.mult, ALU.mult)

            @block.gpsimd
            def _(pool):
                pool.memset(B.ksz[:, :, :], 0.0).then_inc(zeroed, 1)
                pool.memset(B.kwz[:, :, :], 0.0).then_inc(zeroed, 1)
                pool.wait_ge(var_ready, 1)
                pool.tensor_tensor(rs[:, :], ss[:, :], C.neghalf[:, 0:48], ALU.pow).then_inc(rs_ready, 1)

            @block.scalar
            def _(act):
                act.wait_ge(zeroed, 2)
                for w, kz in enumerate((B.ksz, B.kwz)):
                    act.wait_ge(turned, 5 + w)
                    for f in range(2):
                        r = slice(64 * f, 64 * f + 64)
                        nc.scalar.activation(kz[r, f, :], ps[4 + w][r, :], ACT.Identity, bias=0.0,
                                             scale=C.cols1[r, 74 + w:75 + w])

            @block.tensor
            def _(pe):
                pe.wait_ge(qn_ready, NT)
                for i in range(4):
                    for t in range(NT):
                        mm = nc.tensor.transpose(ps[i][:, P * t:P * t + P],
                                                 qn[:, t, i, :, :].rearrange("p f d -> p (f d)"), C.ident[:, :])
                    mm.then_inc(turned, 1)
                for w in range(2):
                    for t in range(NT):
                        mm = nc.tensor.transpose(ps[4 + w][:, P * t:P * t + P], kn[:, t, w, :], C.ident[:, :])
                    mm.then_inc(turned, 1)


def compress(nc, C, A, B):
    with Scope(nc) as s:
        w1 = [s.sb(f"cw1{i}", [P, CMP, P]) for i in range(2)]
        w2 = [s.sb(f"cw2{i}", [P, P]) for i in range(2)]
        post = s.sb("post", [P, CMP])
        posr = s.sb("posr", [CMP, P])
        win = [s.sb(f"win{i}", [P, CMP, CMP]) for i in range(2)]
        e = [s.sb(f"ce{i}", [P, CMP]) for i in range(2)]
        pre = [s.sb(f"cpre{i}", [P, CMP]) for i in range(2)]
        pc = [s.sb(f"cpc{i}", [P, 2]) for i in range(2)]
        hid = [s.sb(f"hid{i}", [P, 4, CMP]) for i in range(2)]
        kc = s.sb("kc", [64, P])
        ksq = s.sb("ksq", [64, P])
        ss = s.sb("css", [64, 1])
        rs = s.sb("crs", [64, 1])
        hps = [s.bank(f"hps{i}") for i in range(2)]
        ops = [s.bank(f"cops{i}") for i in range(2)]
        tps = s.bank("ctps")
        pps = s.bank("cpps")
        zeroed = s.sem("c_zeroed")
        w_in = s.sem("cw_in")
        pos_in = s.sem("pos_in")
        pos_ready = s.sem("pos_ready")
        pos_copied = s.sem("pos_copied")
        win_ready = s.sem("win_ready")
        hid_ps = s.sem("hid_ps")
        pre_ready = s.sem("pre_ready")
        exp_done = s.sem("c_exp")
        hid_ready = s.sem("hid_ready")
        out_ready = s.sem("c_out_ready")
        own = s.sem("c_own")
        var_ready = s.sem("c_var")
        rs_ready = s.sem("c_rs")
        kc_ready = s.sem("kc_ready")
        kc_turned = s.sem("kc_turned")
        with nc.Block() as block:
            @block.gpsimd
            def _(pool):
                ch = Chain(pool, zeroed)
                for i in range(2):
                    ch.link(pool.memset(w1[i][:, :, :], 0.0))
                    ch.link(pool.memset(w2[i][:, :], 0.0))
                    ch.link(pool.memset(hid[i][:, :, :], 0.0))
                ch.link(pool.memset(B.vcd[:, :], 0.0))
                pool.wait_ge(var_ready, 1)
                pool.tensor_tensor(rs[:, :], ss[:, :], C.neghalf[0:64, 0:1], ALU.pow).then_inc(rs_ready, 1)

            @block.sync
            def _(sp):
                for f in range(2):
                    sp.dma_start(posr[:, 64 * f:64 * f + 64], A["cmp_pos"][0]).then_inc(pos_in, 16)
                sp.wait_ge(zeroed, 7)
                for i, n in enumerate("kv"):
                    for f in range(2):
                        r = slice(64 * f, 64 * f + 64)
                        sp.dma_start(w1[i][r, :, r], A[f"cmp_{n}_w1"][0].rearrange("(j d) h -> d j h", d=HD)).then_inc(w_in, 16)
                        sp.dma_start(w2[i][r, r], A[f"cmp_{n}_w2"][0]).then_inc(w_in, 16)

            @block.vector
            def _(dve):
                ch = Chain(dve, own)
                dve.wait_ge(pos_ready, 1)
                nc.vector.tensor_copy(post[:, :], pps[:, 0:CMP]).then_inc(pos_copied, 1)
                dve.wait_ge(pos_copied, 1)
                for i, src in enumerate((B.kcT, B.vcT)):
                    base = src[:, :]
                    view = bass.AP(tensor=base.tensor, offset=base.offset, ap=[base.ap[0], [1, CMP], [STRIDE, NCMP]])
                    nc.vector.tensor_copy(win[i][:, :, 0:NCMP], view)
                    nc.vector.tensor_copy(win[i][:, :, NCMP:CMP], post[:, :].rearrange("p (j a) -> p j a", a=1)).then_inc(win_ready, 1)
                for i in range(2):
                    dve.wait_ge(hid_ps, i + 1)
                    ch.link(nc.vector.tensor_copy(pc[i][:, 0:1], hps[i][:, NCMP:CMP]))
                    ch.link(nc.vector.tensor_scalar(pre[i][:, :], hps[i][:, 0:CMP], pc[i][:, 0:1], None, ALU.add))
                    dve.sem_inc(pre_ready, 1)
                for i in range(2):
                    dve.wait_ge(exp_done, i + 1)
                    dve.wait_ge(zeroed, 7)
                    for g in range(4):
                        r = slice(64 * (g % 2), 64 * (g % 2) + 64)
                        if i == 0 and g >= 2:
                            continue
                        ins = nc.vector.tensor_tensor(hid[i][r, g, 0:NCMP], e[i][r, 0:NCMP], pre[i][r, 0:NCMP], ALU.mult)
                    ins.then_inc(hid_ready, 1)
                dve.wait_ge(out_ready, 1)
                ch.link(nc.vector.tensor_copy(kc[:, :], ops[0][0:64, 0:P]))
                ch.link(nc.vector.tensor_tensor(ksq[:, :], kc[:, :], kc[:, :], ALU.mult))
                ch.link(nc.vector.tensor_reduce(ss[:, :], ksq[:, :], AX.X, ALU.add))
                nc.vector.tensor_scalar(ss[:, :], ss[:, :], 1.0 / HD, EPS, ALU.mult, ALU.add).then_inc(var_ready, 1)
                dve.wait_ge(rs_ready, 1)
                nc.vector.tensor_scalar(kc[:, :], kc[:, :], rs[:, 0:1], None, ALU.mult).then_inc(kc_ready, 1)
                dve.wait_ge(out_ready, 2)
                for a in range(2):
                    r = slice(64 * a, 64 * a + 64)
                    nc.vector.tensor_copy(B.vcd[r, P * a:P * a + P], ops[1][r, 0:P])
                dve.wait_ge(kc_turned, 1)
                nc.vector.tensor_scalar(B.kcd[:, :], tps[:, 0:64], C.cols1[:, 73:74], None, ALU.mult)

            @block.scalar
            def _(act):
                for i in range(2):
                    act.wait_ge(pre_ready, i + 1)
                    nc.scalar.activation(e[i][:, :], pre[i][:, :], ACT.Sigmoid).then_inc(exp_done, 1)

            @block.tensor
            def _(pe):
                pe.wait_ge(pos_in, 32)
                nc.tensor.transpose(pps[:, 0:CMP], posr[:, :], C.ident[0:CMP, 0:CMP]).then_inc(pos_ready, 1)
                pe.wait_ge(w_in, 128)
                for i in range(2):
                    pe.wait_ge(win_ready, i + 1)
                    for j in range(CMP):
                        mm = nc.tensor.matmul(hps[i][:, 0:CMP], w1[i][:, j, :], win[i][:, j, :],
                                              start=(j == 0), stop=(j == CMP - 1))
                    mm.then_inc(hid_ps, 1)
                pe.wait_ge(hid_ready, 1)
                nc.tensor.matmul(ops[0][0:64, 0:P], hid[0][:, 0:2, :].rearrange("p g c -> p (g c)"), w2[0][:, :],
                                 start=True, stop=True).then_inc(out_ready, 1)
                pe.wait_ge(hid_ready, 2)
                nc.tensor.matmul(ops[1][:, 0:P], hid[1][:, :, :].rearrange("p g c -> p (g c)"), w2[1][:, :],
                                 start=True, stop=True).then_inc(out_ready, 1)
                pe.wait_ge(kc_ready, 1)
                nc.tensor.transpose(tps[:, 0:64], kc[:, :], C.ident[0:64, 0:64]).then_inc(kc_turned, 1)


def compressed_attention(nc, C, B):
    with Scope(nc) as s:
        L = [s.sb(f"cl{i}", [P, 8, CMP]) for i in range(2)]
        mn = s.sb("cmn", [P, 8])
        sm = s.sb("csm", [P, 8])
        pT = [s.sb(f"cpt{i}", [P, 2, P]) for i in range(2)]
        sps = [s.bank(f"csps{i}") for i in range(2)]
        tps = [s.bank(f"ctp{i}") for i in range(2)]
        ops = [s.bank(f"cop{i}") for i in range(2)]
        scores = s.sem("ca_scores")
        ready = s.sem("ca_ready")
        exps = s.sem("ca_exps")
        probs = s.sem("ca_probs")
        turned = s.sem("ca_turned")
        copied = s.sem("ca_copied")
        summed = s.sem("ca_summed")
        outs = s.sem("ca_outs")
        own = s.sem("ca_own")
        with nc.Block() as block:
            @block.tensor
            def _(pe):
                def score(j):
                    if j >= 2:
                        pe.wait_ge(ready, j - 1)
                    for i in range(4):
                        mm = nc.tensor.matmul(sps[j % 2][:, 64 * i:64 * i + 64], B.qT[:, i, P * j:P * j + P], B.kcd[:, :],
                                              start=True, stop=True)
                    mm.then_inc(scores, 1)

                score(0)
                for j in range(NT):
                    if j + 1 < NT:
                        score(j + 1)
                    pe.wait_ge(probs, j + 1)
                    if j >= 2:
                        pe.wait_ge(copied, j - 1)
                    for g in range(2):
                        mm = nc.tensor.transpose(tps[j % 2][:, P * g:P * g + P],
                                                 L[j % 2][:, 4 * g:4 * g + 4, :].rearrange("p h c -> p (h c)"), C.ident[:, :])
                    mm.then_inc(turned, 1)
                    pe.wait_ge(copied, j + 1)
                    if j >= 2:
                        pe.wait_ge(outs, j - 1)
                    for g in range(2):
                        mm = nc.tensor.matmul(ops[j % 2][:, 256 * g:256 * g + 256], pT[j % 2][:, g, :], B.vcd[:, :],
                                              start=True, stop=True)
                    mm.then_inc(summed, 1)

            @block.scalar
            def _(act):
                for j in range(NT):
                    act.wait_ge(ready, j + 1)
                    nc.scalar.activation(L[j % 2][:, :, :], L[j % 2][:, :, :], ACT.Exp, scale=-1.0).then_inc(exps, 1)
                    act.wait_ge(turned, j + 1)
                    if j >= 2:
                        act.wait_ge(summed, j - 1)
                    nc.scalar.activation(pT[j % 2][:, :, :].rearrange("p g c -> p (g c)"), tps[j % 2][:, 0:256],
                                         ACT.Copy).then_inc(copied, 1)

            @block.vector
            def _(dve):
                ch = Chain(dve, own)
                for j in range(NT):
                    l = L[j % 2]
                    if j >= 2:
                        dve.wait_ge(turned, j - 1)
                    dve.wait_ge(scores, j + 1)
                    ch.link(nc.vector.tensor_tensor(l[:, :, :].rearrange("p h c -> p (h c)"), sps[j % 2][:, 0:256],
                                                    C.cbias[:, j, :], ALU.add))
                    ch.link(nc.vector.tensor_reduce(mn[:, :], l[:, :, :], AX.X, ALU.min))
                    nc.vector.tensor_tensor(l[:, :, :], l[:, :, :], bcast(mn[:, :], CMP), ALU.subtract).then_inc(ready, 1)
                    dve.wait_ge(exps, j + 1)
                    base = C.cmask[:, j, :]
                    mask = bass.AP(tensor=base.tensor, offset=base.offset, ap=[base.ap[0], [0, 8], [1, CMP]])
                    ch.link(nc.vector.tensor_tensor(l[:, :, :], l[:, :, :], mask, ALU.mult))
                    dve.sem_inc(probs, 1)
                    ch.link(nc.vector.tensor_reduce(sm[:, :], l[:, :, :], AX.X, ALU.add))
                    ch.link(nc.vector.tensor_scalar(sm[:, :], sm[:, :], 1e-30, None, ALU.max))
                    ch.link(nc.vector.reciprocal(sm[:, :], sm[:, :]))
                    g0 = B.ga[:, j, 0:24:3].rearrange("p (f i) -> p i f", f=2)
                    ch.link(nc.vector.tensor_tensor(sm[:, :].rearrange("p (i f) -> p i f", f=2),
                                                    sm[:, :].rearrange("p (i f) -> p i f", f=2), g0, ALU.mult))
                    dve.wait_ge(summed, j + 1)
                    for f in range(2):
                        src = ops[j % 2][:, :].rearrange("p (i f d) -> p i f d", f=2, d=HD)[:, :, f, :]
                        r = sm[:, f:8:2]
                        ins = nc.vector.tensor_tensor(
                            B.oa[:, j, 256 * f:256 * f + 256].rearrange("p (i d) -> p i d", d=HD), src, bcast(r, HD), ALU.mult)
                    ins.then_inc(outs, 1)


def repeat(eng, start, end):
    return nullcontext(start) if end == start + 1 else eng.Fori(start, end)


class Heads:

    def __init__(self, s, nc, tag, qst, dv=HD):
        self.nc, self.dv = nc, dv
        self.qst = qst
        self.probs = [s.sb(f"probs{i}{tag}", [P, OFF[NT]]) for i in range(2)]
        self.pT = [s.sb(f"pT{i}{tag}", [P, 512]) for i in range(2)]
        self.sps = [s.bank(f"sps{j}{tag}") for j in range(NT)]
        self.tps = [s.bank(f"tps{j}{tag}") for j in range(2)]
        self.ops = [s.bank(f"ops{j}{tag}") for j in range(2)]
        self.probs_begin = 0
        self.q_staged = s.sem(f"q_staged{tag}")
        self.scores_ready = s.sem(f"scores_ready{tag}")
        self.scores_read = s.sem(f"scores_read{tag}")
        self.probs_ready = s.sem(f"probs_ready{tag}")
        self.turned = s.sem(f"turned{tag}")
        self.copied = s.sems(f"copied{tag}", 2)
        self.weighed = s.sem(f"weighed{tag}")
        self.head_out = s.sem(f"head_out{tag}")

    def pe(self, pe, C, units, keys, values):
        nc = self.nc

        def scores(n, half, i):
            pe.wait_ge(self.q_staged, i + 1)
            for j in range(NT):
                w = P * (j + 1)
                pe.wait_ge(self.scores_read, 4 * n + j + 1)
                nc.tensor.matmul(self.sps[j][:, 0:w], self.qst[half][:, P * j:P * j + P], keys(half, i, w),
                                 start=True, stop=True).then_inc(self.scores_ready, 1)

        def turn(n, half, j):
            pe.wait_ge(self.probs_ready, 4 * n + j + 1 + self.probs_begin)
            pe.wait_ge(self.copied[j % 2], 2 * n + j // 2 + 1)
            for b in range(j + 1):
                mm = nc.tensor.transpose(self.tps[j % 2][:, P * b:P * b + P],
                                         self.probs[half][:, OFF[j] + P * b:OFF[j] + P * b + P], C.ident[:, :])
            mm.then_inc(self.turned, 1)

        def weigh(n, half, i, j):
            if j == 0:
                pe.wait_ge(self.head_out, n + 1)
            pe.wait_ge(self.copied[j % 2], 2 * n + j // 2 + 2)
            for b in range(j + 1):
                mm = nc.tensor.matmul(self.ops[half][:, self.dv * j:self.dv * (j + 1)], self.pT[j % 2][:, P * b:P * b + P],
                                      values(b, half, i), start=(b == 0), stop=(b == j))
            mm.then_inc(self.weighed, 1)

        def head(n, half, i):
            turn(n, half, 0)
            turn(n, half, 1)
            weigh(n, half, i, 0)
            turn(n, half, 2)
            weigh(n, half, i, 1)
            turn(n, half, 3)
            weigh(n, half, i, 2)
            weigh(n, half, i, 3)

        pe.sem_inc(self.turned, 8)
        pe.sem_inc(self.weighed, 2)
        scores(0, 0, 0)
        with repeat(pe, 0, units - 1) as i:
            scores(2 * i + 1, 1, i)
            head(2 * i, 0, i)
            scores(2 * i + 2, 0, i + 1)
            head(2 * i + 1, 1, i)
        i = units - 1
        scores(2 * i + 1, 1, i)
        head(2 * i, 0, i)
        head(2 * i + 1, 1, i)

    def copy_turned(self, eng, n, j):
        w = P * (j + 1)
        eng.wait_ge(self.turned, 4 * n + j + 9)
        eng.wait_ge(self.weighed, 4 * n + j + 1)
        if j % 2:
            self.nc.scalar.activation(self.pT[1][:, 0:w], self.tps[1][:, 0:w], ACT.Copy).then_inc(self.copied[1], 1)
        else:
            self.nc.vector.tensor_copy(self.pT[0][:, 0:w], self.tps[0][:, 0:w]).then_inc(self.copied[0], 1)

    def run(self, eng, units, rounds):
        rounds(None, (0, 0, 0))
        with repeat(eng, 0, units - 1) as i:
            rounds((2 * i, 0, i), (2 * i + 1, 1, i))
            rounds((2 * i + 1, 1, i), (2 * i + 2, 0, i + 1))
        i = units - 1
        rounds((2 * i, 0, i), (2 * i + 1, 1, i))
        rounds((2 * i + 1, 1, i), None)


def softmax_attention(nc, C, tag, qT, keys, values, out, units=4, bias=None, gate=None, add=False):
    with Scope(nc) as s:
        qst = s.sb(f"qst{tag}", [P, 512])
        H = Heads(s, nc, tag, [qst, qst])
        bst = [s.sb(f"bst{i}{tag}", [P, 512]) for i in range(2)] if bias else [C.ban, C.ban]
        low = [s.sb(f"low{i}{tag}", [P, NT]) for i in range(2)]
        sums = [s.sb(f"sums{i}{tag}", [P, NT]) for i in range(2)]
        coef = [s.sb(f"coef{i}{tag}", [P, NT]) for i in range(2)]
        tmp = s.sb(f"tmp{tag}", [P, NT, HD])
        bias_staged = s.sem(f"bias_staged{tag}")
        begun = s.sem(f"begun{tag}")
        own = s.sem(f"own{tag}")
        links = 1 + bool(gate) + bool(add) + 1
        with nc.Block() as block:
            @block.tensor
            def _(pe):
                H.pe(pe, C, units, keys, values)

            @block.gpsimd
            def _(pool):
                def stage(i, first):
                    if not first:
                        pool.wait_ge(H.scores_ready, 8 * i)
                    pool.tensor_copy(qst[:, :], qT(i)).then_inc(H.q_staged, 1)
                    if bias:
                        for half in range(2):
                            if not first:
                                pool.wait_ge(H.scores_read, 8 * i + 4 * half)
                            pool.tensor_copy(bst[half][:, :], bias(half, i)).then_inc(bias_staged, 1)
                stage(0, True)
                with pool.Fori(1, units) as i:
                    stage(i, False)

            @block.vector
            def _(dve):
                def logits(n, half, j):
                    w = P * (j + 1)
                    if j == 0:
                        dve.wait_ge(H.turned, 4 * n + 4)
                        if bias:
                            dve.wait_ge(bias_staged, n + 1)
                    dve.wait_ge(H.scores_ready, 4 * n + j + 1)
                    dve.sem_inc(begun, 1)
                    nc.vector.tensor_tensor_reduce(H.probs[half][:, OFF[j]:OFF[j + 1]], H.sps[j][:, 0:w],
                                                   bst[half][:, P * (NT - 1 - j):512], 1.0, 3e38, ALU.add, ALU.min,
                                                   low[half][:, j:j + 1]).then_inc(H.scores_read, 1)

                def finish(n, half, i):
                    ch = Chain(dve, own, n * links)
                    dve.wait_ge(H.weighed, 4 * n + 6)
                    ch.link(nc.vector.reciprocal(coef[half][:, :], sums[half][:, :]))
                    if gate:
                        ch.link(nc.vector.tensor_tensor(coef[half][:, :], coef[half][:, :], gate(half, i), ALU.mult))
                    o = H.ops[half][:, 0:NT * HD].rearrange("p (t d) -> p t d", d=HD)
                    if add:
                        ch.link(nc.vector.tensor_tensor(tmp[:, :, :], o, bcast(coef[half][:, :], HD), ALU.mult))
                        ch.link(nc.vector.tensor_tensor(out(half, i), out(half, i), tmp[:, :, :], ALU.add))
                    else:
                        ch.link(nc.vector.tensor_tensor(out(half, i), o, bcast(coef[half][:, :], HD), ALU.mult))
                    dve.sem_inc(H.head_out, 1)
                    assert ch.n == links

                def rounds(now, nxt):
                    for j in range(NT):
                        if nxt:
                            logits(nxt[0], nxt[1], j)
                        if now and j % 2 == 0:
                            H.copy_turned(dve, now[0], j)
                    if now:
                        finish(*now)
                dve.sem_inc(H.scores_read, 4)
                dve.sem_inc(H.copied[0], 1)
                dve.sem_inc(H.head_out, 2)
                H.run(dve, units, rounds)

            @block.scalar
            def _(act):
                def rounds(now, nxt):
                    for j in range(NT):
                        if now and j % 2:
                            H.copy_turned(act, now[0], j)
                        if nxt:
                            n, half, _ = nxt
                            if j == 0:
                                act.wait_ge(H.head_out, n + 1)
                            act.wait_ge(H.scores_read, 4 * n + j + 5)
                            p = H.probs[half][:, OFF[j]:OFF[j + 1]]
                            nc.scalar.activation(p, p, ACT.Exp, scale=-1.0, bias=low[half][:, j:j + 1],
                                                 accum_out=sums[half][:, j:j + 1]).then_inc(H.probs_ready, 1)
                act.sem_inc(H.copied[1], 1)
                H.run(act, units, rounds)


def stick_breaking(nc, C, B):
    with Scope(nc) as s:
        qst = s.sb("sb_qst", [P, 512])
        H = Heads(s, nc, "sb", [qst, qst])
        soft = [s.sb(f"soft{i}", [P, OFF[NT]]) for i in range(2)]
        pos = [s.sb(f"pos{i}", [P, OFF[NT]]) for i in range(2)]
        abs_ready = s.sem("sb_abs")
        soft_ready = s.sem("sb_soft")
        exponent_ready = s.sem("sb_exponent")
        own = s.sem("sb_own")
        act_own = s.sem("sb_act_own")
        with nc.Block() as block:
            @block.tensor
            def _(pe):
                H.pe(pe, C, 4, lambda half, i, w: B.sbk[:, bass.ds(i, 1), half, 0:w].rearrange("p a n -> p (a n)"),
                     lambda b, half, i: B.sbv[:, b, bass.ds(i * 128 + 64 * half, 64)])

            @block.gpsimd
            def _(pool):
                src = lambda i: B.sbq[:, bass.ds(i, 1), :].rearrange("p a n -> p (a n)")
                pool.tensor_copy(qst[:, :], src(0)).then_inc(H.q_staged, 1)
                with pool.Fori(1, 4) as i:
                    pool.wait_ge(H.scores_ready, 8 * i)
                    pool.tensor_copy(qst[:, :], src(i)).then_inc(H.q_staged, 1)

            @block.vector
            def _(dve):
                links = 3 * NT

                def logits(ch, n, half, j):
                    z, w = H.probs[half][:, OFF[j]:OFF[j + 1]], P * (j + 1)
                    if j == 0:
                        dve.wait_ge(H.turned, 4 * n + 4)
                    dve.wait_ge(H.scores_ready, 4 * n + j + 1)
                    nc.vector.tensor_tensor(z, H.sps[j][:, 0:w], C.ban_self[:, P * (NT - 1 - j):512],
                                            ALU.add).then_inc(H.scores_read, 1)
                    dve.wait_ge(H.scores_read, 4 * n + j + 5)
                    nc.vector.scalar_tensor_tensor(out=soft[half][:, OFF[j]:OFF[j + 1]], in0=z, scalar=-1.0, in1=z,
                                                   op0=ALU.mult, op1=ALU.min).then_inc(abs_ready, 1)
                    ch.link(nc.vector.tensor_scalar(pos[half][:, OFF[j]:OFF[j + 1]], z, 0.0, None, ALU.max))

                def suffix(ch, n, half, j):
                    z = H.probs[half][:, OFF[j]:OFF[j + 1]]
                    p = pos[half][:, OFF[j]:OFF[j + 1]]
                    dve.wait_ge(soft_ready, 4 * n + j + 1)
                    ch.link(nc.vector.tensor_tensor_scan(p[:, ::-1], p[:, ::-1], soft[half][:, OFF[j]:OFF[j + 1]][:, ::-1],
                                                         0.0, ALU.add, ALU.add))
                    nc.vector.tensor_tensor(z, z, p, ALU.subtract).then_inc(exponent_ready, 1)
                    ch.link(dve.nop())

                def rounds(now, nxt):
                    if nxt:
                        ch = Chain(dve, own, nxt[0] * links)
                    for j in range(NT):
                        if nxt:
                            logits(ch, nxt[0], nxt[1], j)
                        if now and j % 2 == 0:
                            H.copy_turned(dve, now[0], j)
                        if nxt and j:
                            suffix(ch, nxt[0], nxt[1], j - 1)
                    if nxt:
                        suffix(ch, nxt[0], nxt[1], NT - 1)
                        assert ch.n == links
                    if now:
                        n, half, i = now
                        dve.wait_ge(H.weighed, 4 * n + 6)
                        nc.vector.tensor_copy(B.ob[:, :, bass.ds(i * 128 + 64 * half, 64)],
                                              H.ops[half][:, 0:NT * HD].rearrange("p (t d) -> p t d", d=HD)).then_inc(H.head_out, 1)
                dve.sem_inc(H.scores_read, 4)
                dve.sem_inc(H.copied[0], 1)
                dve.sem_inc(H.head_out, 2)
                H.run(dve, 4, rounds)

            @block.scalar
            def _(act):
                def softplus(n, half, j):
                    x = soft[half][:, OFF[j]:OFF[j + 1]]
                    act.wait_ge(abs_ready, 4 * n + j + 1)
                    ch = Chain(act, act_own, 4 * n + j)
                    ch.link(nc.scalar.activation(x, x, ACT.Exp))
                    nc.scalar.activation(x, x, ACT.Ln, bias=1.0).then_inc(soft_ready, 1)

                def weights(n, half, j):
                    x = H.probs[half][:, OFF[j]:OFF[j + 1]]
                    act.wait_ge(exponent_ready, 4 * n + j + 1)
                    nc.scalar.activation(x, x, ACT.Exp).then_inc(H.probs_ready, 1)

                def rounds(now, nxt):
                    for j in range(NT):
                        if nxt:
                            softplus(nxt[0], nxt[1], j)
                        if now and j % 2:
                            H.copy_turned(act, now[0], j)
                        if nxt and j:
                            weights(nxt[0], nxt[1], j - 1)
                    if nxt:
                        weights(nxt[0], nxt[1], NT - 1)
                act.sem_inc(H.copied[1], 1)
                H.run(act, 4, rounds)


def turn_tokens(nc, C, jobs, tag):
    with Scope(nc) as s:
        ps = [s.bank(f"tt_ps{i}{tag}") for i in range(4)]
        turned = s.sem(f"tt_turned{tag}")
        out = s.sems(f"tt_out{tag}", 2)
        with nc.Block() as block:
            @block.tensor
            def _(pe):
                for k, (src, _, _) in enumerate(jobs):
                    if k >= 4:
                        pe.wait_ge(out[k % 2], k // 2 - 1)
                    for t in range(NT):
                        mm = nc.tensor.transpose(ps[k % 4][:, P * t:P * t + P], src(t), C.ident[:, :])
                    mm.then_inc(turned, 1)

            @block.vector
            def _(dve):
                for k in range(0, len(jobs), 2):
                    dve.wait_ge(turned, k + 1)
                    _, dst, scale = jobs[k]
                    if scale is None:
                        ins = nc.vector.tensor_copy(dst, ps[k % 4][:, :])
                    else:
                        ins = nc.vector.tensor_scalar(dst, ps[k % 4][:, :], scale, None, ALU.mult)
                    ins.then_inc(out[0], 1)

            @block.scalar
            def _(act):
                for k in range(1, len(jobs), 2):
                    act.wait_ge(turned, k + 1)
                    _, dst, scale = jobs[k]
                    nc.scalar.activation(dst, ps[k % 4][:, :], ACT.Copy,
                                         scale=1.0 if scale is None else scale).then_inc(out[1], 1)


def mix_branches(nc, C, A, B, mixed):
    with Scope(nc) as s:
        wu = [s.sb(f"wu{i}", [P, 4, D]) for i in range(2)]
        tmp = [s.sb(f"mixt{i}", [P, 512]) for i in range(2)]
        ps = [[s.bank(f"mx{i}{b}") for b in range(2)] for i in range(2)]
        w_in = s.sems("up_in", 2)
        ready = s.sem("mx_ready")
        own = s.sem("mx_own")
        read = s.sem("mx_read")
        summed = s.sem("mx_sum")
        parts = [(t, n) for n in range(2) for t in range(NT)]
        with nc.Block() as block:
            @block.sync
            def _(sp):
                for b, n in enumerate(("w_up_nsa", "w_up_sb")):
                    sp.dma_start(wu[b][:, :, :], A[n][0].rearrange("(k p) n -> p k n", p=P)).then_inc(w_in[b], 16)

            @block.tensor
            def _(pe):
                for i, (t, n) in enumerate(parts):
                    if i >= 2:
                        pe.wait_ge(read, i - 1)
                    for b in range(2):
                        if i == 0:
                            pe.wait_ge(w_in[b], 16)
                        for k in range(4):
                            mm = nc.tensor.matmul(ps[i % 2][b][:, :], B.oT[b][:, k, P * t:P * t + P],
                                                  wu[b][:, k, 512 * n:512 * n + 512], start=(k == 0), stop=(k == 3))
                    mm.then_inc(ready, 1)

            @block.vector
            def _(dve):
                ch = Chain(dve, own)
                for i, (t, n) in enumerate(parts):
                    dve.wait_ge(ready, i + 1)
                    dst = mixed[:, t, 512 * n:512 * n + 512]
                    if i >= 2:
                        dve.wait_ge(summed, i - 1)
                    ch.link(nc.vector.tensor_tensor(dst, ps[i % 2][0][:, :], B.sig[:, t, 512 * n:512 * n + 512], ALU.mult))
                    ch.link(nc.vector.tensor_tensor(tmp[i % 2][:, :], ps[i % 2][1][:, :],
                                                    B.sig[:, t, D + 512 * n:D + 512 * n + 512], ALU.mult))
                    dve.sem_inc(read, 1)

            @block.gpsimd
            def _(pool):
                for i, (t, n) in enumerate(parts):
                    pool.wait_ge(read, i + 1)
                    dst = mixed[:, t, 512 * n:512 * n + 512]
                    pool.tensor_tensor(dst, dst, tmp[i % 2][:, :], ALU.add).then_inc(summed, 1)


def project_residual(nc, C, aT, w, gate, tag, beside=None):
    kc = w.shape[0] // P
    slots = kc // KD
    with Scope(nc) as s:
        wbuf = [s.sb(f"rw{i}{tag}", [P, KD, 512]) for i in range(2)]
        tmp = [s.sb(f"rt{i}{tag}", [P, 512]) for i in range(2)]
        banks = [s.bank(f"rp{b}{tag}") for b in range(6)]
        mod, after, early = (beside[0](s), beside[1], beside[2]) if beside else (None, None, 0)
        units = len(mod.units) if mod else 0
        landed = s.sems(f"r_landed{tag}", 2)
        used = s.sem(f"r_used{tag}")
        ready = s.sem(f"r_ready{tag}")
        scaled = s.sem(f"r_scaled{tag}")
        added = s.sem(f"r_added{tag}")
        with nc.Block() as block:
            @block.sync
            def _(sp):
                for i in range(2 * slots):
                    if i >= 2:
                        sp.wait_ge(used, i - 1)
                    n, q = i // slots, i % slots
                    sp.dma_start(wbuf[i % 2][:, :, :], chunk(w[q * D:(q + 1) * D, :], 512 * n, 512)).then_inc(landed[i % 2], 16)

            @block.scalar
            def _(act):
                if mod:
                    mod.load(act)

            @block.tensor
            def _(pe):
                unit = 0
                for i in range(2 * slots):
                    n, q = i // slots, i % slots
                    pe.wait_ge(landed[i % 2], 16 * (i // 2 + 1))
                    for t in range(NT):
                        b = NT * n + t
                        if b >= 6 and q == 0:
                            pe.wait_ge(scaled, b - 5)
                        for k in range(KD):
                            first, last = (q == 0 and k == 0), (q == slots - 1 and k == KD - 1)
                            mm = nc.tensor.matmul(banks[b % 6][:, :], aT[:, KD * q + k, P * t:P * t + P], wbuf[i % 2][:, k, :],
                                                  start=first, stop=last)
                        if q == slots - 1 and t < NT - 1:
                            mm.then_inc(ready, 1)
                        if t == NT - 1:
                            mm.then_inc(used, 1)
                        while unit < units and after(unit) == NT * i + t:
                            mod.spread(pe, unit)
                            unit += 1
                for u in range(unit, units):
                    mod.spread(pe, u)

            @block.vector
            def _(dve):
                def take(n):
                    for t in range(NT):
                        i = NT * n + t
                        if t < NT - 1:
                            dve.wait_ge(ready, (NT - 1) * n + t + 1)
                        else:
                            dve.wait_ge(used, slots * (n + 1))
                        if i >= 2:
                            dve.wait_ge(added, i - 1)
                        nc.vector.tensor_tensor(tmp[i % 2][:, :], banks[i % 6][:, :], gate[:, 512 * n:512 * n + 512],
                                                ALU.mult).then_inc(scaled, 1)
                if mod:
                    mod.sum(dve, 0)
                for u in range(units):
                    if u == early:
                        take(0)
                    if u + 1 < units:
                        mod.sum(dve, u + 1)
                    mod.finish(dve, u)
                if not mod:
                    take(0)
                take(1)

            @block.gpsimd
            def _(pool):
                for i in range(2 * NT):
                    n, t = i // NT, i % NT
                    pool.wait_ge(scaled, i + 1)
                    dst = C.h[:, t, 512 * n:512 * n + 512]
                    pool.tensor_tensor(dst, dst, tmp[i % 2][:, :], ALU.add).then_inc(added, 1)


def gate_rows(nc, C, A, G):
    with Scope(nc) as s:
        rows = {n: s.sb(f"gr_{n}", [4, TOK]) for n in ("i", "f", "low", "soft", "F", "a", "top", "m")}
        bias = s.sb("gbias_if", [4, 2])
        zero = s.sb("gr_zero", [4, TOK])
        rps = [s.bank(f"gr_ps{i}") for i in range(2)]
        tps = [s.bank(f"gr_t{i}") for i in range(2)]
        aps = [s.bank(f"gr_a{i}") for i in range(4)]
        bias_in = s.sem("gr_bias_in")
        zeroed = s.sem("gr_zeroed")
        rows_ready = s.sem("gr_rows")
        abs_ready = s.sem("gr_abs")
        act_own = s.sem("gr_act_own")
        soft_ready = s.sem("gr_soft")
        own = s.sem("gr_own")
        scanned = s.sem("gr_scanned")
        cols_ready = s.sem("gr_cols")
        spread = s.sem("gr_spread")
        m_ready = s.sem("gr_m")
        with nc.Block() as block:
            @block.sync
            def _(sp):
                b = A["b_gates_2"][0]
                sp.dma_start(bias[:, 0:1], b[0:4].rearrange("(n a) -> n a", a=1)).then_inc(bias_in, 16)
                sp.dma_start(bias[:, 1:2], b[4:8].rearrange("(n a) -> n a", a=1)).then_inc(bias_in, 16)

            @block.gpsimd
            def _(pool):
                pool.memset(zero[:, :], 0.0).then_inc(zeroed, 1)

            @block.tensor
            def _(pe):
                for g in range(2):
                    for t in range(NT):
                        mm = nc.tensor.transpose(rps[g][0:4, P * t:P * t + P], G.gt[:, t, 4 * g:4 * g + 4], C.ident[:, :])
                    mm.then_inc(rows_ready, 1)
                pe.wait_ge(scanned, 2)
                for g, n in enumerate(("top", "m")):
                    for t in range(NT):
                        mm = nc.tensor.transpose(tps[g][:, 4 * t:4 * t + 4], rows[n][:, P * t:P * t + P], C.ident[0:4, 0:4])
                    mm.then_inc(cols_ready, 1)
                for h in range(4):
                    one = C.ident[0:4, h:h + 1]
                    pick = bass.AP(tensor=one.tensor, offset=one.offset, ap=[one.ap[0], [0, P]])
                    nc.tensor.matmul(aps[h][:, :], pick, rows["a"][:, :], start=True, stop=True).then_inc(spread, 1)

            @block.scalar
            def _(act):
                act.wait_ge(abs_ready, 1)
                ch = Chain(act, act_own)
                ch.link(nc.scalar.activation(rows["soft"][:, :], rows["soft"][:, :], ACT.Exp))
                nc.scalar.activation(rows["soft"][:, :], rows["soft"][:, :], ACT.Ln, bias=1.0).then_inc(soft_ready, 1)
                act.wait_ge(m_ready, 1)
                nc.scalar.activation(G.em[:, :], G.em[:, :], ACT.Exp, scale=-1.0)
                for h in range(4):
                    act.wait_ge(spread, h + 1)
                    nc.scalar.activation(G.a[h][:, :], aps[h][:, :], ACT.Copy)

            @block.vector
            def _(dve):
                ch = Chain(dve, own)
                dve.wait_ge(bias_in, 32)
                dve.wait_ge(rows_ready, 2)
                ch.link(nc.vector.tensor_scalar(rows["i"][:, :], rps[0][0:4, :], bias[:, 0:1], None, ALU.add))
                ch.link(nc.vector.tensor_scalar(rows["f"][:, :], rps[1][0:4, :], bias[:, 1:2], None, ALU.add))
                nc.vector.scalar_tensor_tensor(out=rows["soft"][:, :], in0=rows["f"][:, :], scalar=-1.0, in1=rows["f"][:, :],
                                               op0=ALU.mult, op1=ALU.min).then_inc(abs_ready, 1)
                ch.link(nc.vector.tensor_scalar(rows["low"][:, :], rows["f"][:, :], 0.0, None, ALU.min))
                dve.wait_ge(soft_ready, 1)
                ch.link(nc.vector.tensor_tensor_scan(rows["F"][:, :], rows["low"][:, :], rows["soft"][:, :], 0.0,
                                                     ALU.add, ALU.subtract))
                ch.link(nc.vector.tensor_tensor(rows["a"][:, :], rows["i"][:, :], rows["F"][:, :], ALU.subtract))
                dve.wait_ge(zeroed, 1)
                nc.vector.tensor_tensor_scan(rows["top"][:, :], rows["a"][:, :], zero[:, :], 0.0,
                                             ALU.max, ALU.max).then_inc(scanned, 1)
                dve.wait_ge(scanned, 1)
                nc.vector.tensor_tensor(rows["m"][:, :], rows["F"][:, :], rows["top"][:, :], ALU.add).then_inc(scanned, 1)
                dve.wait_ge(cols_ready, 2)
                nc.vector.tensor_scalar(G.negtop[:, :], tps[0][:, 0:16], -1.0, None, ALU.mult)
                nc.vector.tensor_copy(G.em[:, :], tps[1][:, 0:16]).then_inc(m_ready, 1)


def convolve(nc, C, G):
    with Scope(nc) as s:
        sg = [s.sb(f"cv_s{i}", [P, TOK]) for i in range(2)]
        own = s.sem("cv_own")
        summed = s.sem("cv_sum")
        sig_ready = s.sem("cv_sig")
        out = s.sem("cv_out")
        with nc.Block() as block:
            @block.vector
            def _(dve):
                ch = Chain(dve, own)

                def taps(g):
                    dst = G.qk[:, g, :]
                    ch.link(nc.vector.tensor_scalar(dst, G.raw[:, g, 0:TOK], C.cols2[:, 72 + g:73 + g],
                                                    C.cols2[:, 104 + g:105 + g], ALU.mult, ALU.add))
                    for j in range(1, 4):
                        w = C.cols2[:, 72 + 8 * j + g:73 + 8 * j + g]
                        ch.link(nc.vector.scalar_tensor_tensor(out=dst, in0=G.raw[:, g, j:j + TOK], scalar=w, in1=dst,
                                                               op0=ALU.mult, op1=ALU.add))
                    dve.sem_inc(summed, 1)
                taps(0)
                for g in range(KD):
                    if g + 1 < KD:
                        taps(g + 1)
                    dve.wait_ge(sig_ready, g + 1)
                    nc.vector.scalar_tensor_tensor(out=G.qk[:, g, :], in0=G.qk[:, g, :], scalar=(P ** -0.5 if g < 4 else 1.0),
                                                   in1=sg[g % 2][:, :], op0=ALU.mult, op1=ALU.mult).then_inc(out, 1)

            @block.scalar
            def _(act):
                for g in range(KD):
                    act.wait_ge(summed, g + 1)
                    if g >= 2:
                        act.wait_ge(out, g - 1)
                    nc.scalar.activation(sg[g % 2][:, :], G.qk[:, g, :], ACT.Sigmoid).then_inc(sig_ready, 1)


def mlstm(nc, C, G, hm):
    with Scope(nc) as s:
        qst = [s.sb(f"ml_q{i}", [P, 512]) for i in range(2)]
        H = Heads(s, nc, "ml", qst, dv=P)
        decay = [s.sb(f"decay{i}", [P, OFF[NT]]) for i in range(2)]
        den = [s.sb(f"den{i}", [P, NT]) for i in range(2)]
        exponent_ready = s.sem("ml_exponent")
        decay_ready = s.sem("ml_decay")
        own = s.sem("ml_own")
        H.probs_ready, H.probs_begin = H.scores_read, 4
        links = 4
        with nc.Block() as block:
            @block.tensor
            def _(pe):
                H.pe(pe, C, 2, lambda half, i, w: G.qk[:, 4 + 2 * i + half, 0:w],
                     lambda b, half, i: G.vm[:, b, P * (2 * i + half):P * (2 * i + half) + P])

            @block.gpsimd
            def _(pool):
                for i in range(2):
                    if i:
                        pool.wait_ge(H.scores_ready, 8 * i)
                    pool.tensor_copy(qst[0][:, :], G.qk[:, 2 * i, :])
                    pool.tensor_copy(qst[1][:, :], G.qk[:, 2 * i + 1, :]).then_inc(H.q_staged, 1)

            @block.vector
            def _(dve):
                def exponents(n, half, j):
                    w = P * (j + 1)
                    if n >= 2:
                        dve.wait_ge(H.scores_read, 4 * (n - 2) + j + 5)
                    nc.vector.scalar_tensor_tensor(out=decay[half][:, OFF[j]:OFF[j + 1]], in0=G.a[n][:, 0:w],
                                                   scalar=G.negtop[:, 4 * j + n:4 * j + n + 1],
                                                   in1=C.allow[:, P * (NT - 1 - j):512],
                                                   op0=ALU.add, op1=ALU.min).then_inc(exponent_ready, 1)

                def logits(n, half, j):
                    if j == 0:
                        dve.wait_ge(H.turned, 4 * n + 4)
                    dve.wait_ge(H.scores_ready, 4 * n + j + 1)
                    dve.wait_ge(decay_ready, 4 * n + j + 1)
                    nc.vector.tensor_tensor_reduce(H.probs[half][:, OFF[j]:OFF[j + 1]], H.sps[j][:, 0:P * (j + 1)],
                                                   decay[half][:, OFF[j]:OFF[j + 1]], 1.0, 0.0, ALU.mult, ALU.add,
                                                   den[half][:, j:j + 1]).then_inc(H.scores_read, 1)

                def rounds(now, nxt):
                    if nxt:
                        for j in range(NT):
                            exponents(nxt[0], nxt[1], j)
                    for j in range(NT):
                        if now and j % 2 == 0:
                            H.copy_turned(dve, now[0], j)
                        if nxt:
                            logits(nxt[0], nxt[1], j)
                    if now:
                        n, half, i = now
                        d = den[half][:, :]
                        ch = Chain(dve, own, n * links)
                        dve.wait_ge(H.weighed, 4 * n + 6)
                        ch.link(nc.vector.scalar_tensor_tensor(out=d, in0=d, scalar=-1.0, in1=d, op0=ALU.mult, op1=ALU.max))
                        ch.link(nc.vector.tensor_tensor(d, d, G.em[:, n:16:4], ALU.max))
                        ch.link(nc.vector.reciprocal(d, d))
                        ch.link(nc.vector.tensor_tensor(hm[:, :, P * n:P * n + P],
                                                        H.ops[half][:, :].rearrange("p (t d) -> p t d", d=P), bcast(d, P), ALU.mult))
                        dve.sem_inc(H.head_out, 1)
                dve.sem_inc(H.scores_read, 4)
                dve.sem_inc(H.copied[0], 1)
                dve.sem_inc(H.head_out, 2)
                H.run(dve, 2, rounds)

            @block.scalar
            def _(act):
                def rounds(now, nxt):
                    for j in range(NT):
                        if nxt:
                            n, half, _ = nxt
                            x = decay[half][:, OFF[j]:OFF[j + 1]]
                            act.wait_ge(exponent_ready, 4 * n + j + 1)
                            nc.scalar.activation(x, x, ACT.Exp).then_inc(decay_ready, 1)
                        if now and j % 2:
                            H.copy_turned(act, now[0], j)
                act.sem_inc(H.copied[1], 1)
                H.run(act, 2, rounds)


def norm_heads_gate(nc, C, hm, so):
    with Scope(nc) as s:
        sq = s.sb("nh_sq", [P, NT * 512])
        ss = s.sb("nh_ss", [P, 16])
        rs = s.sb("nh_rs", [P, 16])
        own = s.sem("nh_own")
        var_ready = s.sem("nh_var")
        rs_ready = s.sem("nh_rs")
        with nc.Block() as block:
            @block.vector
            def _(dve):
                ch = Chain(dve, own)
                x = hm[:, :, :].rearrange("p t n -> p (t n)")
                x3 = x.rearrange("p (h d) -> p h d", d=P)
                ch.link(nc.vector.tensor_tensor(sq[:, :], x, x, ALU.mult))
                ch.link(nc.vector.tensor_reduce(ss[:, :], sq[:, :].rearrange("p (h d) -> p h d", d=P), AX.X, ALU.add))
                nc.vector.tensor_scalar(ss[:, :], ss[:, :], 1.0 / P, EPS, ALU.mult, ALU.add).then_inc(var_ready, 1)
                ch.link(nc.vector.tensor_tensor(x, x, so[:, :, :].rearrange("p t n -> p (t n)"), ALU.mult))
                dve.wait_ge(rs_ready, 1)
                ch.link(nc.vector.tensor_tensor(x3, x3, bcast(rs[:, :], P), ALU.mult))

            @block.gpsimd
            def _(pool):
                pool.wait_ge(var_ready, 1)
                pool.tensor_tensor(rs[:, :], ss[:, :], C.neghalf[:, 0:16], ALU.pow).then_inc(rs_ready, 1)


def route(nc, C, A, uT, R):
    with Scope(nc) as s:
        wr = s.sb("wr", [P, KD, 36])
        rb = s.sb("rb", [P, 36])
        L = s.sb("rl", [P, NT, 40])
        top = s.sb("rtop", [P, NT, 8])
        idx = s.sb("ridx", [P, NT, 8], U32)
        gi = s.sb("rgi", [P, NT])
        ex = s.sb("rex", [P, NT, 4])
        gsum = s.sb("rgsum", [P, NT])
        ngm = s.sb("rngm", [P, NT])
        gid = s.sb("gid", [P, EXPERTS])
        pen = s.sb("pen", [P, NT, EXPERTS])
        top2 = s.sb("rtop2", [P, NT, 8])
        idx2 = s.sb("ridx2", [P, NT, 8], U32)
        e = s.sb("re", [P, NT, 2])
        d = s.sb("rd", [P, NT, 1])
        oh = [s.sb(f"roh{i}", [P, NT, EXPERTS]) for i in range(2)]
        both = s.sb("rboth", [P, NT, EXPERTS])
        junk = s.sb("rjunk", [P, 2 * NT, EXPERTS])
        cnt = s.sb("rcnt", [P, EXPERTS])
        pmax = s.sb("rpmax", [1, LEVELS, PAIRS])
        ohs = s.sb("rohs", [P, 2, 8, P])
        row = s.sb("rrow", [P, NT, 2])
        kk = s.sb("rkk", [P, NT, 2])
        tf = s.sb("rtf", [P, PAIRS])
        te = s.sb("rte", [P, PAIRS])
        lps = [s.bank(f"r_l{t}") for t in range(NT)]
        kps = s.bank("r_rank")
        cps = s.bank("r_cnt")
        xps = s.bank("r_idx")
        w_in = s.sem("r_w_in")
        fill = s.sem("r_fill")
        logits = s.sem("r_logits")
        own = s.sem("r_own")
        ng_ready = s.sem("r_ng")
        exps = s.sem("r_exps")
        dd_ready = s.sem("r_dd")
        exp2 = s.sem("r_exp2")
        oh_ready = s.sem("r_oh")
        ranks = s.sem("r_ranks")
        slots_ready = s.sem("r_slots")
        table = s.sem("r_table")
        with nc.Block() as block:
            @block.sync
            def _(sp):
                sp.dma_start(wr[:, :, 0:4], A["w_router_group_2"][0].rearrange("(k p) n -> p k n", p=P)).then_inc(w_in, 16)
                sp.dma_start(wr[:, :, 4:36], A["w_router_expert_2"][0].rearrange("(k p) n -> p k n", p=P)).then_inc(w_in, 16)
                sp.dma_start(rb[:, 0:4], rows_to_all(A["b_router_group_2"][0], 4)).then_inc(w_in, 16)
                sp.dma_start(rb[:, 4:36], rows_to_all(A["b_router_expert_2"][0], EXPERTS)).then_inc(w_in, 16)

            @block.gpsimd
            def _(pool):
                ch = Chain(pool, fill)
                ok = dict(allow_small_or_imprecise_dtypes=True)
                ch.link(pool.memset(L[:, :, :], -3e38))
                ch.link(pool.iota(gid[:, :], pattern=[[1, 4], [0, 8]], base=0, channel_multiplier=0, **ok))
                ch.link(pool.iota(R.eid[:, :], pattern=[[1, P]], base=0, channel_multiplier=0, **ok))
                ch.link(pool.iota(R.aid[:, :, :], pattern=[[TOK, 2], [P, NT]], base=1, channel_multiplier=1, **ok))
                ch.link(pool.iota(R.spare[:, :], pattern=[[1, 1]], base=2 * TOK, channel_multiplier=1, **ok))

            @block.tensor
            def _(pe):
                pe.wait_ge(w_in, 64)
                for t in range(NT):
                    for k in range(KD):
                        mm = nc.tensor.matmul(lps[t][:, 0:36], uT[:, k, P * t:P * t + P], wr[:, k, :],
                                              start=(k == 0), stop=(k == KD - 1))
                    mm.then_inc(logits, 1)
                pe.wait_ge(oh_ready, 1)
                for t in range(NT):
                    for u in range(t + 1):
                        nc.tensor.matmul(kps[:, EXPERTS * t:EXPERTS * (t + 1)], C.ones[:, :] if u < t else C.later[:, :],
                                         both[:, u, :], start=(u == 0), stop=(u == t))
                for u in range(NT):
                    mm = nc.tensor.matmul(cps[:, 0:EXPERTS], C.ones[:, :], both[:, u, :], start=(u == 0), stop=(u == NT - 1))
                mm.then_inc(ranks, 1)
                for m in range(2):
                    pe.wait_ge(slots_ready, m + 1)
                    for q in range(8):
                        mm = nc.tensor.matmul(xps[:, PAIRS * m:PAIRS * (m + 1)], ohs[:, m, q, :], R.ptok[:, q, :],
                                              start=(q == 0), stop=(q == 7))
                    mm.then_inc(table, 1)

            @block.scalar
            def _(act):
                act.wait_ge(ng_ready, 1)
                for t in range(NT):
                    ins = nc.scalar.activation(ex[:, t, :], L[:, t, 0:4], ACT.Exp, bias=ngm[:, t:t + 1],
                                               accum_out=gsum[:, t:t + 1])
                ins.then_inc(exps, 1)
                act.wait_ge(dd_ready, 1)
                nc.scalar.activation(R.w[:, :, 1:2], d[:, :, :], ACT.Exp).then_inc(exp2, 1)

            @block.vector
            def _(dve):
                ch = Chain(dve, own)
                v = nc.vector
                dve.wait_ge(fill, 5)
                for t in range(NT):
                    dve.wait_ge(logits, t + 1)
                    v.tensor_tensor(L[:, t, 0:4], lps[t][:, 0:4], rb[:, 0:4], ALU.add)
                    ch.link(v.tensor_tensor(L[:, t, 8:40], lps[t][:, 4:36], rb[:, 4:36], ALU.add))
                    ch.link(v.max(top[:, t, :], L[:, t, 0:8]))
                    ch.link(v.max_index(idx[:, t, :], top[:, t, :], L[:, t, 0:8]))
                v.tensor_scalar(ngm[:, :], top[:, :, 0], -1.0, None, ALU.mult).then_inc(ng_ready, 1)
                ch.link(v.tensor_copy(gi[:, :], idx[:, :, 0]))
                for t in range(NT):
                    ch.link(v.tensor_scalar(pen[:, t, :], gid[:, :], gi[:, t:t + 1], 1.0, ALU.is_equal, ALU.subtract))
                    ch.link(v.scalar_tensor_tensor(out=pen[:, t, :], in0=pen[:, t, :], scalar=3e38, in1=L[:, t, 8:40],
                                                   op0=ALU.mult, op1=ALU.add))
                    ch.link(v.max(top2[:, t, :], pen[:, t, :]))
                    ch.link(v.max_index(idx2[:, t, :], top2[:, t, :], pen[:, t, :]))
                v.tensor_tensor(d[:, :, :], top2[:, :, 1:2], top2[:, :, 0:1], ALU.subtract).then_inc(dd_ready, 1)
                ch.link(v.tensor_copy(e[:, :, :], idx2[:, :, 0:2]))
                for t in range(NT):
                    for j in range(2):
                        ch.link(v.tensor_scalar(oh[j][:, t, :], R.eid[:, 0:EXPERTS], e[:, t, j:j + 1], None, ALU.is_equal))
                v.tensor_tensor(both[:, :, :], oh[0][:, :, :], oh[1][:, :, :], ALU.add).then_inc(oh_ready, 1)
                dve.wait_ge(exps, 1)
                dve.wait_ge(exp2, 1)
                ch.link(v.reciprocal(gsum[:, :], gsum[:, :]))
                w0, w1 = R.w[:, :, 0], R.w[:, :, 1]
                ch.link(v.tensor_scalar(w0, w1, 1.0, None, ALU.add))
                ch.link(v.reciprocal(w0, w0))
                ch.link(v.tensor_tensor(w0, w0, gsum[:, :], ALU.mult))
                ch.link(v.tensor_tensor(w1, w1, w0, ALU.mult))
                dve.wait_ge(ranks, 1)
                for t in range(NT):
                    for j in range(2):
                        ch.link(v.tensor_tensor_reduce(junk[:, 2 * t + j, :], oh[j][:, t, :], kps[:, EXPERTS * t:EXPERTS * (t + 1)],
                                                       1.0, 0.0, ALU.mult, ALU.add, R.rank[:, t, j:j + 1]))
                ch.link(v.tensor_scalar(R.level[:, :, :], R.rank[:, :, :], float(CAP), None, ALU.is_ge))
                for m in range(2, LEVELS):
                    ch.link(v.scalar_tensor_tensor(out=R.level[:, :, :], in0=R.rank[:, :, :], scalar=float(CAP * m),
                                                   in1=R.level[:, :, :], op0=ALU.is_ge, op1=ALU.add))
                ch.link(v.scalar_tensor_tensor(out=row[:, :, :], in0=e[:, :, :], scalar=float(CAP), in1=R.rank[:, :, :],
                                               op0=ALU.mult, op1=ALU.add))
                ch.link(v.tensor_scalar(R.pair[:, :, :], e[:, :, :], 2.0, None, ALU.is_ge))
                for m in range(2, PAIRS):
                    ch.link(v.scalar_tensor_tensor(out=R.pair[:, :, :], in0=e[:, :, :], scalar=2.0 * m,
                                                   in1=R.pair[:, :, :], op0=ALU.is_ge, op1=ALU.add))
                ch.link(v.scalar_tensor_tensor(out=kk[:, :, :], in0=R.level[:, :, :], scalar=-float(CAP),
                                               in1=row[:, :, :], op0=ALU.mult, op1=ALU.add))
                ch.link(v.scalar_tensor_tensor(out=R.place[:, :, :], in0=R.pair[:, :, :], scalar=-2.0 * CAP,
                                               in1=kk[:, :, :], op0=ALU.mult, op1=ALU.add))
                for q in range(8):
                    t, j = q // 2, q % 2
                    ch.link(v.tensor_scalar(R.ptok[:, q, :], R.eid[:, 0:PAIRS], R.pair[:, t, j:j + 1], R.aid[:, j, t:t + 1],
                                            ALU.is_equal, ALU.mult))
                for m in range(2):
                    place_onehots(v, ch, R, kk[:, :, :], ohs[:, m, :, :], float(m))
                    dve.sem_inc(slots_ready, 1)
                for m in range(2):
                    dve.wait_ge(table, 2)
                    fill_table(v, ch, R, xps[:, PAIRS * m:PAIRS * (m + 1)], m, tf[:, :], te[:, :])
                ch.link(v.tensor_copy(cnt[:, :], cps[:, 0:EXPERTS]))
                for m in range(LEVELS):
                    ch.link(v.tensor_reduce(pmax[:, m, :], cnt[0:1, :].rearrange("p (q f) -> p q f", f=2), AX.X, ALU.max))
                    ch.link(v.tensor_scalar(pmax[:, m, :], pmax[:, m, :], float(-CAP * m), None, ALU.add))
                v.tensor_copy(R.over[:, 0:LEVELS * PAIRS], pmax[:, :, :].rearrange("p m q -> p (m q)"))
                ch.link(v.tensor_reduce(R.most[:, :], pmax[:, :, :], AX.X, ALU.max))


class Experts:

    def __init__(self, s, nc, C, A, M, R, xn, y, tag):
        self.nc, self.C, self.A, self.M, self.R, self.xn, self.y = nc, C, A, M, R, xn, y
        sb, sem = (lambda n, sh, dt=F32: s.sb(f"{n}{tag}", sh, dt)), (lambda n: s.sem(f"{n}{tag}"))
        self.ids = sb("x_ids", [P, 1], U32)
        self.to = sb("x_to", [P, 1], U32)
        self.xg = sb("x_g", [P, D])
        self.xT = sb("x_T", [P, KD, P])
        self.act = sb("x_act", [P, DE])
        self.sig = sb("x_sig", [P, DE])
        self.aT = sb("x_aT", [P, 4, P])
        self.out = sb("x_out", [P, D])
        self.w = [sb(f"x_w{i}", [P, KD, DE]) for i in range(6)]
        self.tps = [s.bank(f"x_t{i}{tag}") for i in range(2)]
        self.gps = s.bank(f"x_gp{tag}")
        self.ups = s.bank(f"x_up{tag}")
        self.aps = s.bank(f"x_ap{tag}")
        self.yps = [s.bank(f"x_y{i}{tag}") for i in range(2)]
        self.landed = [sem(f"x_landed{i}") for i in range(6)]
        self.ids_ready = sem("x_ids_ready")
        self.to_ready = sem("x_to_ready")
        self.out_free = sem("x_out_free")
        self.asked = sem("x_asked")
        self.gathered = sem("x_gathered")
        self.turned = sem("x_turned")
        self.modulated = [sem("x_mod_dve"), sem("x_mod_act")]
        self.gate_ready = sem("x_gate")
        self.up_ready = sem("x_up_s")
        self.sig_ready = sem("x_sig_s")
        self.act_ready = sem("x_act_s")
        self.act_turned = sem("x_act_turned")
        self.act_copied = sem("x_act_copied")
        self.down_ready = sem("x_down")
        self.out_ready = [sem("x_out_dve"), sem("x_out_act")]
        self.stored = sem("x_stored")
        self.own = sem("x_own")

    def begin(self, pool):
        for sem, n in ([(x, 16) for x in self.landed] + [(self.turned, 2), (self.own, 2)]
                       + [(x, 4) for x in self.modulated]
                       + [(x, 1) for x in (self.ids_ready, self.to_ready, self.gate_ready, self.up_ready, self.sig_ready,
                                           self.act_ready, self.act_turned, self.out_free, self.act_copied, self.down_ready,
                                           *self.out_ready)]):
            pool.sem_inc(sem, n)

    def load(self, sp, done, q):
        free = (self.gate_ready, self.up_ready, self.down_ready)
        names = ("w_expert_gate_2", "w_expert_up_2", "w_expert_down_2")
        for m in range(6):
            sp.wait_ge(free[m // 2], done)
            w = self.A[names[m // 2]][0][bass.ds(q * 2 + m % 2, 1)]
            if m < 4:
                dst, src = self.w[m][:, :, :], w.rearrange("a (k p) n -> p (a k) n", p=P)
            else:
                dst = self.w[m][:, :, :].rearrange("p (k f) n -> p k (f n)", k=4)
                src = w.rearrange("a (k p) n -> p (a k) n", p=P)
            sp.dma_start(dst, src).then_inc(self.landed[m], 16)

    def gather(self, pool, i, col):
        pool.wait_ge(self.turned, 2 * i)
        pool.sem_inc(self.asked, 1)
        pool.tensor_copy(self.ids[:, :], self.R.tokens[:, bass.ds(col, 1)]).then_inc(self.ids_ready, 1)
        pool.wait_ge(self.ids_ready, i + 1)
        pool.sem_inc(self.asked, 1)
        pool.indirect_dma_start(out=self.xg[:, :], out_offset=None, in_=self.xn,
                                in_offset=bass.IndirectOffsetOnAxis(ap=self.ids[:, 0:1], axis=0)).then_inc(self.gathered, 16)

    def aim(self, pool, col):
        pool.tensor_copy(self.to[:, :], self.R.rows[:, bass.ds(col, 1)]).then_inc(self.to_ready, 1)

    def scatter(self, pool, i):
        pool.wait_ge(self.to_ready, i + 1)
        for f in range(2):
            pool.wait_ge(self.out_ready[f], i + 1)
        pool.sem_inc(self.asked, 1)
        pool.indirect_dma_start(out=self.y, out_offset=bass.IndirectOffsetOnAxis(ap=self.to[:, 0:1], axis=0),
                                in_=self.out[:, :], in_offset=None).then_inc(self.stored, 16)
        pool.wait_ge(self.stored, 16 * i)
        pool.sem_inc(self.out_free, 1)

    def pe(self, pe, i, pair):
        nc, C = self.nc, self.C
        pe.wait_ge(self.gathered, 16 * i)
        for b in range(2):
            for k in range(4):
                mm = nc.tensor.transpose(self.tps[b][:, P * k:P * k + P], self.xg[:, P * (4 * b + k):P * (4 * b + k) + P],
                                         C.ident[:, :])
            mm.then_inc(self.turned, 1)
        for m, ps, ready in ((0, self.gps, self.gate_ready), (2, self.ups, self.up_ready)):
            if m == 0:
                for b in range(2):
                    pe.wait_ge(self.modulated[b], 4 * i + 4)
            pe.wait_ge(self.act_ready, i)
            for f in range(2):
                pe.wait_ge(self.landed[m + f], 16 * pair + 16)
            for k in range(KD):
                for f in range(2):
                    mm = nc.tensor.matmul(ps[CAP * f:CAP * f + CAP, :], self.xT[:, k, CAP * f:CAP * f + CAP], self.w[m + f][:, k, :],
                                          start=(k == 0), stop=(k == KD - 1))
            mm.then_inc(ready, 1)
        pe.wait_ge(self.act_ready, i + 1)
        for k in range(4):
            mm = nc.tensor.transpose(self.aps[:, P * k:P * k + P], self.act[:, P * k:P * k + P], C.ident[:, :])
        mm.then_inc(self.act_turned, 1)
        pe.wait_ge(self.act_copied, i + 1)
        for f in range(2):
            pe.wait_ge(self.landed[4 + f], 16 * pair + 16)
            pe.wait_ge(self.out_ready[f], i)
        for n in range(2):
            for k in range(4):
                for f in range(2):
                    w = self.w[4 + f][:, 2 * k + n, :]
                    mm = nc.tensor.matmul(self.yps[n][CAP * f:CAP * f + CAP, :], self.aT[:, k, CAP * f:CAP * f + CAP], w,
                                          start=(k == 0), stop=(k == 3))
        mm.then_inc(self.down_ready, 1)

    def dve(self, dve, i):
        nc, M = self.nc, self.M
        ch = Chain(dve, self.own, i * 2)
        dve.wait_ge(self.turned, 2 * i + 1)
        dve.wait_ge(self.up_ready, i)
        for k in range(4):
            nc.vector.tensor_scalar(self.xT[:, k, :], self.tps[0][:, P * k:P * k + P], M.scale[1][:, k:k + 1],
                                    M.shift[1][:, k:k + 1], ALU.mult, ALU.add).then_inc(self.modulated[0], 1)
        dve.wait_ge(self.sig_ready, i + 1)
        ch.link(nc.vector.tensor_tensor(self.sig[:, :], self.sig[:, :], self.gps[:, :], ALU.mult))
        dve.wait_ge(self.act_turned, i)
        dve.wait_ge(self.up_ready, i + 1)
        ch.link(nc.vector.tensor_tensor(self.act[:, :], self.sig[:, :], self.ups[:, :], ALU.mult))
        dve.sem_inc(self.act_ready, 1)
        dve.wait_ge(self.down_ready, i + 1)
        dve.wait_ge(self.out_free, i)
        nc.vector.tensor_copy(self.out[:, 0:512], self.yps[0][:, :]).then_inc(self.out_ready[0], 1)

    def scalar(self, act, i):
        nc, M = self.nc, self.M
        act.wait_ge(self.turned, 2 * i + 2)
        act.wait_ge(self.up_ready, i)
        for k in range(4, 8):
            nc.scalar.activation(self.xT[:, k, :], self.tps[1][:, P * (k - 4):P * (k - 4) + P], ACT.Identity,
                                 scale=M.scale[1][:, k:k + 1], bias=M.shift[1][:, k:k + 1]).then_inc(self.modulated[1], 1)
        act.wait_ge(self.gate_ready, i + 1)
        act.wait_ge(self.act_ready, i)
        nc.scalar.activation(self.sig[:, :], self.gps[:, :], ACT.Sigmoid).then_inc(self.sig_ready, 1)
        act.wait_ge(self.act_turned, i + 1)
        nc.scalar.activation(self.aT[:, :, :].rearrange("p k n -> p (k n)"), self.aps[:, :], ACT.Copy).then_inc(self.act_copied, 1)
        act.wait_ge(self.down_ready, i + 1)
        act.wait_ge(self.out_free, i)
        nc.scalar.activation(self.out[:, 512:D], self.yps[1][:, :], ACT.Copy).then_inc(self.out_ready[1], 1)


def first_places(nc, C, A, M, R, xn, y):
    with Scope(nc) as s:
        X = Experts(s, nc, C, A, M, R, xn, y, "a")

        def count(eng, tag):
            ran = eng.alloc_register(f"ran_{tag}")
            eng.reg_mov(ran, 1)
            return ran

        def on_both(eng, ran, q, round_):
            round_(eng.snap(ran), q)
            eng.reg_add(ran, ran, 1)
            on_next(eng, ran, q, round_)

        def on_next(eng, ran, q, round_):
            over = eng.value_load(R.over[0:1, bass.ds(q + PAIRS, 1)])
            with eng.If(over > 0):
                round_(eng.snap(ran), q + PAIRS)
                eng.reg_add(ran, ran, 1)

        with nc.Block() as block:
            @block.sync
            def _(sp):
                ran = count(sp, "load")
                with sp.Fori(0, PAIRS) as q:
                    X.load(sp, sp.snap(ran), q)
                    on_both(sp, ran, q, lambda i, col: None)

            @block.gpsimd
            def _(pool):
                def move(i, col):
                    X.gather(pool, i, col)
                    X.scatter(pool, i - 1)
                    X.aim(pool, col)
                X.begin(pool)
                ran = count(pool, "move")
                X.gather(pool, 1, 0)
                X.aim(pool, 0)
                pool.reg_add(ran, ran, 1)
                on_next(pool, ran, 0, move)
                with pool.Fori(1, PAIRS) as q:
                    on_both(pool, ran, q, move)
                X.scatter(pool, pool.snap(ran) - 1)

            @block.tensor
            def _(pe):
                ran = count(pe, "multiply")
                with pe.Fori(0, PAIRS) as q:
                    on_both(pe, ran, q, lambda i, col: X.pe(pe, i, q + 1))

            @block.vector
            def _(dve):
                ran = count(dve, "vector")
                with dve.Fori(0, PAIRS) as q:
                    on_both(dve, ran, q, lambda i, col: X.dve(dve, i))

            @block.scalar
            def _(act):
                ran = count(act, "scalar")
                with act.Fori(0, PAIRS) as q:
                    on_both(act, ran, q, lambda i, col: X.scalar(act, i))


def fill_table(v, ch, R, ps, level, f, e):
    cols = slice(level * PAIRS, (level + 1) * PAIRS)
    ch.link(v.tensor_scalar(f, ps, -1.0, 0.0, ALU.add, ALU.max))
    ch.link(v.tensor_scalar(e, f, float(TOK), -float(TOK), ALU.is_ge, ALU.mult))
    ch.link(v.tensor_tensor(R.tokens[:, cols], f, e, ALU.add))
    ch.link(v.tensor_scalar(e, ps, 0.0, R.spare[:, 0:1], ALU.is_equal, ALU.mult))
    ch.link(v.tensor_tensor(R.rows[:, cols], f, e, ALU.add))


FILL_LINKS = 5


def place_onehots(v, ch, R, kk, ohs, level):
    ch.link(v.tensor_scalar(kk, R.level[:, :, :], level, None, ALU.is_equal))
    ch.link(v.scalar_tensor_tensor(out=kk, in0=R.place[:, :, :], scalar=1.0, in1=kk, op0=ALU.add, op1=ALU.mult))
    ch.link(v.tensor_scalar(kk, kk, -1.0, None, ALU.add))
    for q in range(8):
        t, j = q // 2, q % 2
        ch.link(v.tensor_scalar(ohs[:, q, :], R.eid[:, :], kk[:, t, j:j + 1], None, ALU.is_equal))


ONEHOT_LINKS = 11


def later_places(nc, C, A, M, R, xn, y):
    links = ONEHOT_LINKS + FILL_LINKS
    with Scope(nc) as s:
        X = Experts(s, nc, C, A, M, R, xn, y, "b")
        kk = s.sb("lp_kk", [P, NT, 2])
        ohs = s.sb("lp_ohs", [P, 8, P])
        f = s.sb("lp_f", [P, PAIRS])
        e = s.sb("lp_e", [P, PAIRS])
        xps = s.bank("lp_ps")
        own = s.sem("lp_own")
        ohs_ready = s.sem("lp_ohs_ready")
        summed = s.sem("lp_summed")
        tables = s.sem("lp_tables")

        def levels(eng, start, round_):
            ran = eng.alloc_register(f"ran_{start.__name__}")
            eng.reg_mov(ran, 1)
            with eng.Fori(2, LEVELS) as m:
                most = eng.value_load(R.most[0:1, bass.ds(m, 1)])
                with eng.If(most > 0):
                    start(eng, m, ran)
                    with eng.Fori(0, PAIRS) as q:
                        over = eng.value_load(R.over[0:1, bass.ds(m * PAIRS + q, 1)])
                        with eng.If(over > 0):
                            round_(eng, eng.snap(ran), q)
                            eng.reg_add(ran, ran, 1)

        with nc.Block() as block:
            @block.sync
            def _(sp):
                def load_start(sp, m, ran):
                    pass
                levels(sp, load_start, X.load)

            @block.gpsimd
            def _(pool):
                def move_start(pool, m, ran):
                    pool.wait_ge(tables, m - 1)
                    pool.sem_inc(X.asked, 1)

                def move(pool, i, q):
                    X.gather(pool, i, q)
                    X.aim(pool, q)
                    X.scatter(pool, i)
                X.begin(pool)
                levels(pool, move_start, move)

            @block.tensor
            def _(pe):
                def table_sums(pe, m, ran):
                    pe.wait_ge(ohs_ready, m - 1)
                    for q in range(8):
                        mm = nc.tensor.matmul(xps[:, 0:PAIRS], ohs[:, q, :], R.ptok[:, q, :], start=(q == 0), stop=(q == 7))
                    mm.then_inc(summed, 1)
                levels(pe, table_sums, lambda pe, i, q: X.pe(pe, i, i))

            @block.vector
            def _(dve):
                def table_fill(dve, m, ran):
                    ch = Chain(dve, own, (m - 2) * links)
                    before = dve.snap(ran)
                    place_onehots(nc.vector, ch, R, kk[:, :, :], ohs[:, :, :], R.eid[:, bass.ds(m, 1)])
                    dve.sem_inc(ohs_ready, 1)
                    dve.wait_ge(summed, m - 1)
                    dve.wait_ge(X.out_free, before)
                    fill_table(nc.vector, ch, R, xps[:, 0:PAIRS], 0, f[:, :], e[:, :])
                    dve.sem_inc(tables, 1)
                levels(dve, table_fill, lambda dve, i, q: X.dve(dve, i))

            @block.scalar
            def _(act):
                def scalar_start(act, m, ran):
                    pass
                levels(act, scalar_start, lambda act, i, q: X.scalar(act, i))


def combine(nc, C, A, M, R, y, out):
    with Scope(nc) as s:
        yg = [[s.sb(f"yg{t}{j}", [P, D]) for j in range(2)] for t in range(NT)]
        tmp = s.sb("cb_tmp", [P, NT, D])
        gain = s.sb("gain", [P, D])
        ssq = s.sb("cb_ssq", [P, NT])
        rs = s.sb("cb_rs", [P, NT])
        got = [s.sems(f"cb_got{j}", NT) for j in range(2)]
        gain_in = s.sem("cb_gain")
        own = s.sem("cb_own")
        summed = s.sem("cb_summed")
        squares = s.sem("cb_squares")
        var_ready = s.sem("cb_var")
        rs_ready = s.sem("cb_rs_s")
        res = s.sem("cb_res")
        stored = s.sem("cb_stored")
        with nc.Block() as block:
            @block.gpsimd
            def _(pool):
                for t in range(NT):
                    pool.wait_ge(var_ready, t + 1)
                    pool.tensor_tensor(rs[:, t:t + 1], ssq[:, t:t + 1], C.neghalf[:, 0:1], ALU.pow).then_inc(rs_ready, 1)

            @block.sync
            def _(sp):
                for t in range(NT):
                    for j in range(2):
                        src = y[j * TOK + P * t:j * TOK + P * t + P, :]
                        sp.dma_start(yg[t][j][:, :], src).then_inc(got[j][t], 16)
                sp.dma_start(gain[:, :], rows_to_all(A["g_final_2"], D)).then_inc(gain_in, 16)
                for t in range(NT):
                    sp.wait_ge(res, t + 1)
                    sp.dma_start(out[0, P * t:P * t + P, :], tmp[:, t, :]).then_inc(stored, 16)
                sp.wait_ge(stored, 16 * NT)

            @block.scalar
            def _(act):
                for t in range(NT):
                    act.wait_ge(summed, t + 1)
                    nc.scalar.activation(tmp[:, t, :], C.h[:, t, :], ACT.Square, accum_out=ssq[:, t:t + 1]).then_inc(squares, 1)

            @block.vector
            def _(dve):
                ch = Chain(dve, own)
                v = nc.vector

                def scaled(t):
                    dve.wait_ge(rs_ready, t + 1)
                    v.scalar_tensor_tensor(out=tmp[:, t, :], in0=C.h[:, t, :], scalar=rs[:, t:t + 1], in1=gain[:, :],
                                           op0=ALU.mult, op1=ALU.mult).then_inc(res, 1)
                for t in range(NT):
                    dve.wait_ge(got[0][t], 16)
                    ch.link(v.tensor_scalar(yg[t][0][:, :], yg[t][0][:, :], R.w[:, t, 0:1], None, ALU.mult))
                    dve.wait_ge(got[1][t], 16)
                    ch.link(v.scalar_tensor_tensor(out=yg[t][0][:, :], in0=yg[t][1][:, :], scalar=R.w[:, t, 1:2],
                                                   in1=yg[t][0][:, :], op0=ALU.mult, op1=ALU.add))
                    ch.link(v.tensor_tensor(yg[t][0][:, :], yg[t][0][:, :], M.gate[1][:, :], ALU.mult))
                    ch.link(v.tensor_tensor(C.h[:, t, :], C.h[:, t, :], yg[t][0][:, :], ALU.add))
                    dve.sem_inc(summed, 1)
                    dve.wait_ge(squares, t + 1)
                    v.tensor_scalar(ssq[:, t:t + 1], ssq[:, t:t + 1], 1.0 / D, EPS, ALU.mult, ALU.add).then_inc(var_ready, 1)
                dve.wait_ge(gain_in, 16)
                for t in range(NT):
                    scaled(t)


def project_second(nc, C, A, G, uT):
    with Scope(nc) as s:
        zeroed = s.sem("kaz_zeroed")
        with nc.Block() as block:
            @block.gpsimd
            def _(pool):
                ch = Chain(pool, zeroed)
                ch.link(pool.memset(G.kaz[:, :, :, :], 0.0))
                ch.link(pool.memset(G.raw[:, :, 0:3], 0.0))

    def halves(b, ps):
        return [(G.kaz[64 * f:64 * f + 64, b, f, :], ps[64 * f:64 * f + 64, :], ACT.Copy, 1.0) for f in range(2)]

    w = P * NT
    steps = [
        (0, 512, True, lambda b, ps: [(G.raw[:, b, 3:3 + TOK], ps[:, :], ACT.Copy, 1.0)]),
        (512, 512, True, lambda b, ps: [(G.raw[:, 4 + b, 3:3 + TOK], ps[:, :], ACT.Copy, 1.0)]),
        (1024, 512, False, lambda b, ps: [(G.vm[:, b, :], ps[:, :], ACT.Copy, 1.0)]),
        (1536, 512, False, lambda b, ps: [(G.so[:, b, :], ps[:, :], ACT.Sigmoid, 1.0)]),
        (2048, 8, False, lambda b, ps: [(G.gt[:, b, :], ps[:, 0:8], ACT.Copy, 1.0)]),
        (2056, 512, True, lambda b, ps: [(G.qa[:, b, :], ps[:, :], ACT.Copy, -HD ** -0.5)]),
        (2568, 512, True, halves),
        (3080, 512, False, lambda b, ps: [(G.va[:, b, :], ps[:, :], ACT.Copy, 1.0)]),
    ]
    project(nc, C, uT, A["w_in_2"][0], steps, "p2")


def mlp_up(nc, C, uT, w, hT):
    rounds = FF // 1024
    with Scope(nc) as s:
        wbuf = [s.sb(f"mw{i}", [P, KD, 512]) for i in range(2)]
        rt = [s.sb(f"mr{i}", [P, 512]) for i in range(4)]
        ps = [s.bank(f"mp{i}") for i in range(8)]
        landed = s.sems("m_landed", 2)
        ready = s.sem("m_ready")
        relued = s.sem("m_relued")
        out = s.sem("m_out")
        with nc.Block() as block:
            @block.sync
            def _(sp):
                def load(i, c):
                    src = w[:, bass.ds(i * 1024 + c * 512, 512)].rearrange("(k p) n -> p k n", p=P)
                    sp.dma_start(wbuf[c][:, :, :], src).then_inc(landed[c], 16)
                load(0, 0)
                load(0, 1)
                with sp.Fori(1, rounds) as i:
                    for c in range(2):
                        sp.wait_ge(ready, 8 * i + 4 * c - 4)
                        load(i, c)

            @block.tensor
            def _(pe):
                with pe.Fori(0, rounds) as i:
                    for c in range(2):
                        pe.wait_ge(landed[c], 16 * i + 16)
                        for g in range(4):
                            pe.wait_ge(out, 8 * i + 4 * c + g + 1)
                            for k in range(KD):
                                mm = nc.tensor.matmul(ps[4 * c + g][:, :], wbuf[c][:, k, P * g:P * g + P], uT[:, k, :],
                                                      start=(k == 0), stop=(k == KD - 1))
                            mm.then_inc(ready, 1)

            @block.scalar
            def _(act):
                with act.Fori(0, rounds) as i:
                    for b in range(8):
                        act.wait_ge(ready, 8 * i + b + 1)
                        act.wait_ge(out, 8 * i + b + 5)
                        nc.scalar.activation(rt[b % 4][:, :], ps[b][:, :], ACT.Relu).then_inc(relued, 1)

            @block.vector
            def _(dve):
                dve.sem_inc(out, 8)
                with dve.Fori(0, rounds) as i:
                    for b in range(8):
                        dve.wait_ge(relued, 8 * i + b + 1)
                        nc.vector.tensor_tensor(hT[:, bass.ds(i * 8 + b, 1), :].rearrange("p a n -> p (a n)"),
                                                rt[b % 4][:, :], ps[b][:, :], ALU.mult).then_inc(out, 1)


class Bag:
    pass


def first_attention(nc, C, M, A):
    pass


def program(nc, A, out, dump=None):
    Scope.used.clear()
    with Scope(nc) as s:
        C = Bag()
        C.h = s.sb("h", [P, NT, D])
        C.ident = s.sb("ident", [P, P])
        C.ones = s.sb("ones", [P, P])
        C.later = s.sb("later", [P, P])
        C.ban = s.sb("ban", [P, 512])
        C.ban_self = s.sb("ban_self", [P, 512])
        C.allow = s.sb("allow", [P, 512])
        C.neghalf = s.sb("neghalf", [P, 48])
        C.cols1 = s.sb("cols1", [P, P])
        C.cols2 = s.sb("cols2", [P, P])
        M = [Bag(), Bag()]
        for b in range(2):
            M[b].sc = s.sb(f"silu_c{b}", [P, KD])
            M[b].scale = [s.sb(f"scale{b}{i}", [P, KD]) for i in range(2)]
            M[b].shift = [s.sb(f"shift{b}{i}", [P, KD]) for i in range(2)]
            M[b].gate = [s.sb(f"gate{b}{i}", [P, D]) for i in range(2)]
        constants(nc, C, A)
        first_modulation(nc, C, M, A)
        B = Bag()
        with Scope(nc) as s0:
            mT = s0.sb("mT", [P, KD, TOK])
            with Scope(nc) as s1:
                B.sig = s1.sb("sig", [P, NT, 2 * D])
                B.oa, B.ob = mT[:, 0:NT, :], mT[:, NT:2 * NT, :]
                with Scope(nc) as s1b:
                    B.sbq = s1b.sb("sbq", [P, 4, TOK])
                    B.sbk = s1b.sb("sbk", [P, 4, 2, TOK])
                    B.sbv = s1b.sb("sbv", [P, NT, 512])
                    with Scope(nc) as s2:
                        B.kv = s2.sb("kv", [P, NT, 512])
                        B.ga = s2.sb("ga", [P, NT, 24])
                        B.qT = s2.sb("qT", [P, 4, TOK])
                        B.ksz = s2.sb("ksz", [P, 2, TOK])
                        B.kwz = s2.sb("kwz", [P, 2, TOK])
                        B.kcd = s2.sb("kcd", [P, 64])
                        B.vcd = s2.sb("vcd", [P, 256])
                        with Scope(nc) as s3:
                            B.qa = s3.sb("qa", [P, NT, 512])
                            B.kcT = s3.sb("kcT", [P, TOK])
                            B.vcT = s3.sb("vcT", [P, TOK])
                            with Scope(nc) as s4:
                                uT = s4.sb("uT", [P, KD, TOK])
                                norm_turn(nc, C, M[0].scale[0], M[0].shift[0], uT, "n1")
                                project_first(nc, C, A, B, uT)
                            head_norms(nc, C, B)
                            compress(nc, C, A, B)
                        if dump: dump("prep", B.qT[:, 1, :], B.kcd[:, :], B.vcd[:, :], B.ksz[:, 1, :])
                        C.bias = s2.sb("bias", [P, 8, 512])
                        C.cbias = s2.sb("cbias", [P, NT, 256])
                        C.cmask = s2.sb("cmask", [P, NT, CMP])
                        bias_tables(nc, C, A)
                        compressed_attention(nc, C, B)
                        for tag, kz, branch in (("sl", B.ksz, 1), ("wn", B.kwz, 2)):
                            softmax_attention(
                                nc, C, tag, lambda i: B.qT[:, bass.ds(i, 1), :].rearrange("p a n -> p (a n)"),
                                lambda half, i, w: kz[:, half, 0:w],
                                lambda b, half, i: B.kv[:, b, 256 * branch - 128 + 64 * half:256 * branch - 64 + 64 * half],
                                lambda half, i: B.oa[:, :, bass.ds(i * 64 + 256 * half, 64)],
                                bias=lambda half, i: C.bias[:, bass.ds(i + 4 * half, 1), :].rearrange("p a n -> p (a n)"),
                                gate=lambda half, i: B.ga[:, :, bass.ds(i * 3 + 12 * half + branch, 1)].rearrange("p t a -> p (t a)"),
                                add=True)
                        if dump: dump("nsa", B.oa[:, 0, :],  B.oa[:, 3, :])
                    stick_breaking(nc, C, B)
                    if dump: dump("sb", B.ob[:, :, :])
                    B.oT = [s1b.sb(f"oT{i}", [P, 4, TOK]) for i in range(2)]
                    turn_tokens(nc, C, [(lambda t, o=o, k=k: o[:, t, P * k:P * k + P], B.oT[i][:, k, :], None)
                                        for i, o in enumerate((B.oa, B.ob)) for k in range(4)], "oT")
                    mixed = s1b.sb("mixed", [P, NT, D])
                    mix_branches(nc, C, A, B, mixed)
                    turn_tokens(nc, C, [(lambda t, k=k: mixed[:, t, P * k:P * k + P], mT[:, k, :], None)
                                        for k in range(KD)], "mT")
            rest = lambda sc: Modulation(sc, nc, C, M[0], C.cols1, A["ada_w"][0], A["ada_b"][0], [2, 4, 3, 5], "m2")
            project_residual(nc, C, mT, A["w_out"][0], M[0].gate[0], "o1", (rest, lambda u: u + 1, 3))
        if dump: dump("res1", C.h[:, :, :])
        with Scope(nc) as s1:
            hT = s1.sb("hT", [P, FF // P, TOK])
            with Scope(nc) as s2:
                uT = s2.sb("uT2", [P, KD, TOK])
                norm_turn(nc, C, M[0].scale[1], M[0].shift[1], uT, "n2")
                mlp_up(nc, C, uT, A["mlp_w1"][0], hT)
            second = lambda sc: Modulation(sc, nc, C, M[1], C.cols2, A["w_ada_2"][0], A["b_ada_2"][0],
                                           [1, 0, 2, 4, 3, 5], "m3")
            project_residual(nc, C, hT, A["mlp_w2"][0], M[0].gate[1], "o2",
                             (second, lambda u: 2 * u + (3 if u < 7 else 5), 7))
        if dump: dump("h1", C.h[:, :, :])
        Scope.clear(nc)
        R = Bag()
        R.w = s.sb("rw", [P, NT, 2])
        R.rank = s.sb("rrank", [P, NT, 2])
        R.level = s.sb("rlevel", [P, NT, 2])
        R.pair = s.sb("rpair", [P, NT, 2])
        R.place = s.sb("rplace", [P, NT, 2])
        R.eid = s.sb("eid", [P, P])
        R.aid = s.sb("aid", [P, 2, NT])
        R.spare = s.sb("spare", [P, 1])
        R.ptok = s.sb("ptok", [P, 8, PAIRS])
        R.tokens = s.sb("slot_tokens", [P, 2 * PAIRS], U32)
        R.rows = s.sb("slot_rows", [P, 2 * PAIRS], U32)
        R.over = s.sb("over", [1, LEVELS * PAIRS], I32)
        R.most = s.sb("most", [1, LEVELS], I32)
        xn = nc.dram_tensor("normed_rows", [TOK, D], F32).ap()
        y = nc.dram_tensor("expert_rows", [2 * TOK + P, D], F32).ap()
        with Scope(nc) as s1:
            cat = [s1.sb("hm", [P, NT, 512]), s1.sb("ha", [P, NT, 512])]
            with Scope(nc) as s2:
                G = Bag()
                G.vm = s2.sb("vm", [P, NT, 512])
                G.so = s2.sb("so", [P, NT, 512])
                G.gt = s2.sb("gt", [P, NT, 8])
                G.qa = s2.sb("qa2", [P, 4, TOK])
                G.kaz = s2.sb("kaz", [P, 4, 2, TOK])
                G.va = s2.sb("va", [P, NT, 512])
                G.qk = s2.sb("qk", [P, KD, TOK])
                G.a = [s2.sb(f"ga{h}", [P, TOK]) for h in range(4)]
                G.negtop = s2.sb("negtop", [P, 16])
                G.em = s2.sb("em", [P, 16])
                with Scope(nc) as s3:
                    G.raw = s3.sb("raw", [P, KD, TOK + 3])
                    with Scope(nc) as s4:
                        uT = s4.sb("uT3", [P, KD, TOK])
                        norm_turn(nc, C, M[1].scale[0], M[1].shift[0], uT, "n3")
                        project_second(nc, C, A, G, uT)
                    gate_rows(nc, C, A, G)
                    convolve(nc, C, G)
                mlstm(nc, C, G, cat[0])
                norm_heads_gate(nc, C, cat[0], G.so)
                softmax_attention(
                    nc, C, "ma", lambda i: G.qa[:, bass.ds(i, 1), :].rearrange("p a n -> p (a n)"),
                    lambda half, i, w: G.kaz[:, bass.ds(i, 1), half, 0:w].rearrange("p a n -> p (a n)"),
                    lambda b, half, i: G.va[:, b, bass.ds(i * 128 + 64 * half, 64)],
                    lambda half, i: cat[1][:, :, bass.ds(i * 128 + 64 * half, 64)])
                if dump: dump("cat", cat[0][:, :, :], cat[1][:, :, :])
            cT = s1.sb("cT", [P, KD, TOK])
            turn_tokens(nc, C, [(lambda t, k=k: cat[k // 4][:, t, P * (k % 4):P * (k % 4) + P], cT[:, k, :],
                                 C.cols2[:, 112 + k:113 + k] if k < 4 else None) for k in range(KD)], "cT")
            project_residual(nc, C, cT, A["w_out_2"][0], M[1].gate[0], "o3")
        with Scope(nc) as s1:
            uT = s1.sb("uT4", [P, KD, TOK])
            norm_turn(nc, C, M[1].scale[1], M[1].shift[1], uT, "n4", xn_dram=xn)
            route(nc, C, A, uT, R)
        first_places(nc, C, A, M[1], R, xn, y)
        later_places(nc, C, A, M[1], R, xn, y)
        combine(nc, C, A, M[1], R, y, out)


def project_first(nc, C, A, B, uT):
    copy = lambda dst: (lambda b, ps: [(dst(b), ps, ACT.Copy, 1.0)])
    with Scope(nc) as s:
        zeroed = s.sem("sbk_zeroed")
        with nc.Block() as block:
            @block.gpsimd
            def _(pool):
                pool.memset(B.sbk[:, :, :, :], 0.0).then_inc(zeroed, 1)
                pool.wait_ge(zeroed, 1)

    def halves(b, ps):
        return [(B.sbk[64 * f:64 * f + 64, b, f, :], ps[64 * f:64 * f + 64, :], ACT.Copy, 1.0) for f in range(2)]

    steps = [
        (0, 512, False, lambda b, ps: [(B.qa[:, b, :], ps[:, :], ACT.Copy, 1.0)]),
        (512, 256, True, lambda b, ps: [((B.kcT, B.vcT)[b][:, :], ps[:, :], ACT.Copy, 1.0)]),
        (768, 512, False, lambda b, ps: [(B.kv[:, b, :], ps[:, :], ACT.Copy, 1.0)]),
        (1280, 24, False, lambda b, ps: [(B.ga[:, b, :], ps[:, 0:24], ACT.Sigmoid, 1.0)]),
        (1304, 512, True, lambda b, ps: [(B.sbq[:, b, :], ps[:, :], ACT.Copy, HD ** -0.5)]),
        (1816, 512, True, halves),
        (2328, 512, False, lambda b, ps: [(B.sbv[:, b, :], ps[:, :], ACT.Copy, 1.0)]),
    ] + [
        (2840 + 512 * m, 512, False,
         lambda b, ps, m=m: [(B.sig[:, b, 512 * m:512 * m + 512], ps[:, :], ACT.Sigmoid, 1.0)]) for m in range(4)
    ]
    project(nc, C, uT, A["w_in"][0], steps, "p1")


def distance_onehots():
    dist = np.concatenate([511 - np.arange(BIAS_X), np.arange(FWD) - DIST0])
    n = np.maximum(dist, 0)
    exact = BUCKETS // 2
    nf = np.maximum(n, 1).astype(np.float32)
    large = exact + (np.log(nf / np.float32(exact)) / np.float32(np.log(128 / exact)) * (BUCKETS - exact)).astype(np.int32)
    bucket = np.where(n < exact, n, np.minimum(large, BUCKETS - 1))
    bucket = np.where(dist < 0, BUCKETS, bucket)
    return (bucket[None, :] == np.arange(BUCKETS + 1)[:, None]).astype(np.float32)


def kernel(**inputs):
    import concourse.bacc as bacc
    from concourse.bass_utils import run_bass_kernel_spmd

    nc = bacc.Bacc("TRN2", target_bir_lowering=False, num_devices=1)
    arrays, A = {}, {}
    for name in [*_INS, "onehot"]:
        a = distance_onehots() if name == "onehot" else np.ascontiguousarray(inputs[name])
        arrays[f"in_{name}_dram"] = a
        A[name] = nc.dram_tensor(f"in_{name}_dram", a.shape, mybir.dt.from_np(a.dtype), kind="ExternalInput").ap()
    out = nc.dram_tensor("out_0_dram", (1, TOK, D), F32, kind="ExternalOutput").ap()
    program(nc, A, out)
    r = run_bass_kernel_spmd(nc, [arrays], core_ids=[0])
    return r.results[0]["out_0_dram"]
```

```python
from contextlib import ExitStack, nullcontext

import numpy as np

import concourse.bass as bass
from concourse import mybir

ALU = mybir.AluOpType
ACT = mybir.ActivationFunctionType
AX = mybir.AxisListType
F32 = mybir.dt.float32
F32R = mybir.dt.float32r
U32 = mybir.dt.uint32
I32 = mybir.dt.int32

P = 128
TOK = 512
NT = TOK // P
D = 1024
KD = D // P
HD = 64
FF = 4096
BUCKETS = 32
CMP = 32
STRIDE = 16
NCMP = (TOK - CMP) // STRIDE + 1
EPS = 1e-6
BIG = 1e30
EXPERTS = 32
DE = 512
CAP = 64
PAIRS = EXPERTS // 2
LEVELS = TOK // CAP
OFF = [P * (j * (j + 1) // 2) for j in range(NT + 1)]
BIAS_C = TOK - P + CMP + STRIDE * (CMP - 1)
BIAS_X = 1056

_INS = [
    "x", "c", "rel_bias", "ada_w", "ada_b", "norm1_g", "norm2_g", "w_in", "cmp_pos", "cmp_k_w1",
    "cmp_k_w2", "cmp_v_w1", "cmp_v_w2", "q_norm_g", "k_norm_g", "w_up_nsa", "w_up_sb", "w_out",
    "mlp_w1", "mlp_w2", "c_2", "w_ada_2", "b_ada_2", "g_norm1_2", "w_in_2", "w_conv_2", "b_conv_2",
    "b_gates_2", "g_mlstm_head_2", "w_out_2", "g_norm2_2", "w_router_group_2",
    "b_router_group_2", "w_router_expert_2", "b_router_expert_2", "w_expert_gate_2",
    "w_expert_up_2", "w_expert_down_2", "g_final_2",
]


class Scope(ExitStack):

    used = []
    at = {}

    def __init__(self, nc):
        super().__init__()
        self.nc = nc

    @classmethod
    def clear(cls, nc):
        nc.clear_and_free_semaphores(cls.used)
        nc.all_engine_barrier()
        cls.used.clear()

    def sb(self, name, shape, dt=F32):
        t = self.enter_context(self.nc.sbuf_tensor(name, shape, dt))
        self.at[name] = self.nc.sbuf_base - int(np.prod(shape[1:])) * 4
        return t

    def twin(self, name, of, shape):
        return self.nc.alloc_sbuf_tensor_at(name, shape, F32R, offset=self.at[of])

    def bank(self, name):
        return self.enter_context(self.nc.psum_tensor(name, [P, 512], F32))

    def sem(self, name):
        sem = self.nc.alloc_semaphore(name=name)
        self.used.append(sem)
        return sem

    def sems(self, name, n):
        return [self.sem(f"{name}{i}") for i in range(n)]


class Chain:

    def __init__(self, eng, sem, base=0):
        self.eng, self.sem, self.base, self.n = eng, sem, base, 0

    def link(self, ins):
        self.n += 1
        ins.then_inc(self.sem, 1)
        self.eng.wait_ge(self.sem, self.base + self.n)


def bcast(ap, n):
    return bass.AP(tensor=ap.tensor, offset=ap.offset, ap=[*ap.ap, [0, n]])


def rows_to_all(ap, n):
    return bass.AP(tensor=ap.tensor, offset=ap.offset, ap=[[0, P], [1, n]])


def chunk(w, col, n):
    return w[:, col:col + n].rearrange("(k p) n -> p k n", p=P)


def constants(nc, C, A, ahead):
    with Scope(nc) as s:
        rows1 = s.sb("rows1", [P, P])
        rows2 = s.sb("rows2", [P, P])
        turned = s.bank("turned_ps")
        rows_in = s.sem("rows_in")
        made = s.sem("made")
        zeroed = s.sem("zeroed")
        cols_ready = s.sem("cols_ready")
        x_in = s.sem("x_in")
        with nc.Block() as block:
            @block.sync
            def _(sp):
                sp.wait_ge(zeroed, 2)
                r = lambda ap: ap.rearrange("(r n) -> r n", n=P)
                rows = lambda dst, src: sp.dma_start(dst, src).then_inc(rows_in, 16)
                rows(rows1[0:48, :], r(A["ada_b"][0]))
                rows(rows1[48:56, :], r(A["c"][0]))
                rows(rows1[56:64, :], r(A["norm1_g"][0]))
                rows(rows1[64:72, :], r(A["norm2_g"][0]))
                g64 = [A["q_norm_g"][0]] + [A["k_norm_g"][0, i] for i in range(3)]
                for i, g in enumerate(g64):
                    for half in range(2):
                        rows(rows1[72 + i:73 + i, 64 * half:64 * half + 64], g.rearrange("(a n) -> a n", a=1))
                rows(rows2[0:48, :], r(A["b_ada_2"][0]))
                rows(rows2[48:56, :], r(A["c_2"][0]))
                rows(rows2[56:64, :], r(A["g_norm1_2"][0]))
                rows(rows2[64:72, :], r(A["g_norm2_2"][0]))
                rows(rows2[72:104, :], A["w_conv_2"][0].rearrange("w (r n) -> (w r) n", n=P))
                rows(rows2[104:112, :], r(A["b_conv_2"][0]))
                rows(rows2[112:116, :], r(A["g_mlstm_head_2"][0]))
                ahead(sp)
                sp.dma_start(C.h[:, :, :], A["x"][0].rearrange("(t p) d -> p t d", p=P)).then_inc(x_in, 16)
                sp.wait_ge(x_in, 16)

            @block.gpsimd
            def _(pool):
                ch = Chain(pool, made)
                ch.link(pool.memset(rows1[:, :], 0.0))
                ch.link(pool.memset(rows2[:, :], 0.0))
                pool.sem_inc(zeroed, 2)
                for m, v in ((C.neghalf, -0.5), (C.ident, 0.0), (C.ones, 1.0), (C.later, 0.0), (C.ban, 0.0),
                             (C.ban_self, 0.0), (C.allow, 0.0)):
                    ch.link(pool.memset(m[:, :], v))
                ch.link(pool.affine_select(out=C.ident[:, :], in_=C.ident[:, :], compare_op=ALU.not_equal,
                                           fill=1.0, base=0, pattern=[[-1, P]], channel_multiplier=1))
                ch.link(pool.affine_select(out=C.later[:, :], in_=C.later[:, :], compare_op=ALU.is_ge,
                                           fill=1.0, base=0, pattern=[[-1, P]], channel_multiplier=1))
                for m, op, fill in ((C.ban, ALU.is_ge, BIG), (C.ban_self, ALU.is_gt, -BIG), (C.allow, ALU.is_ge, -BIG)):
                    ch.link(pool.affine_select(out=m[:, :], in_=m[:, :], compare_op=op, fill=fill,
                                               base=384, pattern=[[-1, 512]], channel_multiplier=1))

            @block.vector
            def _(dve):
                dve.wait_ge(cols_ready, 2)
                nc.vector.tensor_copy(C.cols1[:, :], turned[:, 0:P])
                nc.vector.tensor_copy(C.cols2[:, :], turned[:, P:2 * P])

            @block.tensor
            def _(pe):
                pe.wait_ge(rows_in, 16 * 19)
                pe.wait_ge(made, 10)
                nc.tensor.transpose(turned[:, 0:P], rows1[:, :], C.ident[:, :]).then_inc(cols_ready, 1)
                nc.tensor.transpose(turned[:, P:2 * P], rows2[:, :], C.ident[:, :]).then_inc(cols_ready, 1)


class BiasRows:

    def __init__(self, s, nc, C, A):
        self.nc, self.C, self.A = nc, C, A
        self.tbl = s.sb("tbl", [BUCKETS + 1, 8])
        self.onehot = s.sb("onehot", [BUCKETS + 1, BIAS_X])
        self.vrow = s.sb("vrow", [8, BIAS_X])
        self.vdram = nc.dram_tensor("bias_by_distance", [8, BIAS_X], F32).ap()
        self.upside = s.sb("upside", [P, 8, BIAS_C])
        self.cb = s.sb("cb", [P, NT, 256])
        self.flip = s.sb("flip", [P, P])
        self.vps = [s.bank(f"v_ps{i}") for i in range(3)]
        self.fps = [s.bank("flip_ps0"), s.bank("flip_ps1")]
        self.tbl_in = s.sem("tbl_in")
        self.negated = s.sem("negated")
        self.flip_made = s.sem("flip_made")
        self.v_ready = s.sem("v_ready")
        self.v_copied = s.sem("v_copied")
        self.v_out = s.sem("v_out")
        self.bias_in = s.sem("bias_in")
        self.flipped = s.sem("flipped")
        self.cb_out = s.sem("cb_out")
        self.b_copied = s.sem("b_copied")

    def pool(self, pool):
        pool.memset(self.tbl[BUCKETS:BUCKETS + 1, :], -BIG).then_inc(self.negated, 1)
        pool.wait_ge(self.negated, 1)
        pool.memset(self.flip[:, :], 0.0).then_inc(self.flip_made, 1)
        pool.wait_ge(self.flip_made, 1)
        pool.affine_select(out=self.flip[:, :], in_=self.flip[:, :], compare_op=ALU.not_equal, fill=1.0,
                           base=-(P - 1), pattern=[[1, P]], channel_multiplier=1).then_inc(self.flip_made, 1)

    def negate(self, dve):
        dve.wait_ge(self.tbl_in, 32)
        dve.wait_ge(self.negated, 1)
        self.nc.vector.tensor_scalar(self.tbl[:, :], self.tbl[:, :], -1.0, None, ALU.mult).then_inc(self.negated, 1)

    def copy_rows(self, dve):
        dve.wait_ge(self.v_ready, 3)
        for i in range(3):
            n = min(512, BIAS_X - 512 * i)
            self.nc.vector.tensor_copy(self.vrow[:, 512 * i:512 * i + n], self.vps[i][0:8, 0:n]).then_inc(self.v_copied, 1)

    def rows(self, pe):
        pe.wait_ge(self.negated, 2)
        for i in range(3):
            n = min(512, BIAS_X - 512 * i)
            self.nc.tensor.matmul(self.vps[i][0:8, 0:n], self.tbl[:, :], self.onehot[:, 512 * i:512 * i + n],
                                  start=True, stop=True).then_inc(self.v_ready, 1)

    def turn_over(self, pe):
        pe.wait_ge(self.flip_made, 2)
        pe.wait_ge(self.bias_in, 16)
        for h in range(8 + NT):
            if h >= 2:
                pe.wait_ge(self.b_copied, h - 1)
            if h < 8:
                out, src = self.fps[h % 2][:, :], self.upside[:, h, 0:512]
            else:
                first = TOK - P + CMP - 1 - P * (h - 8)
                out = self.fps[h % 2][:, 0:8 * CMP].rearrange("p (h c) -> p h c", c=CMP)
                src = self.upside[:, :, first:first + STRIDE * (CMP - 1) + 1:STRIDE]
            self.nc.tensor.matmul(out, self.flip[:, :], src, start=True, stop=True).then_inc(self.flipped, 1)

    def scalar(self, act):
        act.dma_start(self.onehot[:, :], self.A["onehot"]).then_inc(self.tbl_in, 16)
        act.dma_start(self.tbl[0:BUCKETS, :], self.A["rel_bias"]).then_inc(self.tbl_in, 16)
        act.wait_ge(self.v_copied, 3)
        act.dma_start(self.vdram, self.vrow[:, :]).then_inc(self.v_out, 16)
        act.wait_ge(self.v_out, 16)
        src = bass.AP(tensor=self.vdram.tensor, offset=0, ap=[[1, P], [BIAS_X, 8], [1, BIAS_C]])
        act.dma_start(self.upside[:, :, :], src).then_inc(self.bias_in, 16)
        for h in range(8):
            act.wait_ge(self.flipped, h + 1)
            self.nc.scalar.activation(self.C.bias[:, h, :], self.fps[h % 2][:, :], ACT.Copy).then_inc(self.b_copied, 1)
        for t in range(NT):
            act.wait_ge(self.flipped, 9 + t)
            src = self.fps[t % 2][:, 0:256].rearrange("p (f i c) -> p i f c", f=2, i=4)
            dst = self.cb[:, t, :].rearrange("p (i f c) -> p i f c", i=4, f=2)
            for i in range(4):
                ins = self.nc.scalar.activation(dst[:, i], src[:, i], ACT.Copy)
            ins.then_inc(self.b_copied, 1)
        act.wait_ge(self.b_copied, 8 + NT)
        act.dma_start(self.C.cbias_dram, self.cb[:, :, :].rearrange("p t n -> p (t n)")).then_inc(self.cb_out, 16)
        act.wait_ge(self.cb_out, 16)


def compressed_bias(nc, C):
    with Scope(nc) as s:
        cb_in = s.sem("cb_in")
        with nc.Block() as block:
            @block.sync
            def _(sp):
                sp.dma_start(C.cbias[:, :, :].rearrange("p t n -> p (t n)"), C.cbias_dram).then_inc(cb_in, 16)

            @block.vector
            def _(dve):
                dve.wait_ge(cb_in, 16)
                nc.vector.tensor_scalar(C.cmask[:, :, :], C.cbias[:, :, 0:CMP], 1e29, None, ALU.is_lt)


class Modulation:

    def __init__(self, s, nc, C, M, cols, w, bias, parts, tag):
        self.nc, self.C, self.M, self.cols, self.w, self.bias, self.parts = nc, C, M, cols, w, bias, parts
        self.units = [(m, n) for m in parts for n in range(2)]
        self.wbuf = [s.sb(f"adaw{i}{tag}", [P, KD, 512]) for i in range(2)]
        self.acc = [s.sb(f"acc{i}{tag}", [P, 512]) for i in range(2)]
        self.gbias = {m: M.gate[m // 3] for m in parts if m in (2, 5)}
        self.t = s.sb(f"t{tag}", [P, 4])
        self.ps = [s.bank(f"mod_ps{i}{tag}") for i in range(2)]
        self.landed = s.sems(f"ada_landed{tag}", 2)
        self.gb_in = s.sem(f"gb_in{tag}")
        self.summed = s.sem(f"ada_summed{tag}")
        self.spread_out = s.sem(f"ada_spread{tag}")
        self.finished = s.sem(f"ada_finished{tag}")
        self.own = s.sem(f"ada_own{tag}")
        self.chain = None

    def load(self, eng, first=0):
        self.load_biases(eng)
        for u in range(first, len(self.units)):
            self.load_unit(eng, u)

    def load_biases(self, eng):
        for m, dst in self.gbias.items():
            eng.dma_start(dst[:, :], rows_to_all(self.bias[m * D:(m + 1) * D], D)).then_inc(self.gb_in, 16)

    def load_unit(self, eng, u):
        m, n = self.units[u]
        if u >= 2:
            eng.wait_ge(self.summed, u - 1)
        eng.dma_start(self.wbuf[u % 2][:, :, :], chunk(self.w, m * D + 512 * n, 512)).then_inc(self.landed[u % 2], 16)

    def sum(self, dve, u):
        v, a, w, sc = self.nc.vector, self.acc[u % 2], self.wbuf[u % 2], self.M.sc
        self.chain = self.chain or Chain(dve, self.own)
        dve.wait_ge(self.landed[u % 2], 16 * (u // 2 + 1))
        if u >= 2:
            dve.wait_ge(self.spread_out, u - 1)
        self.chain.link(v.tensor_scalar(a[:, :], w[:, 0, :], sc[:, 0:1], None, ALU.mult))
        for k in range(1, KD):
            ins = v.scalar_tensor_tensor(out=a[:, :], in0=w[:, k, :], scalar=sc[:, k:k + 1], in1=a[:, :],
                                         op0=ALU.mult, op1=ALU.add)
            if k < KD - 1:
                self.chain.link(ins)
        ins.then_inc(self.summed, 1)

    def spread(self, pe, u):
        m, a, ps, ones = self.units[u][0], self.acc[u % 2], self.ps[u % 2], self.C.ones
        pe.wait_ge(self.summed, u + 1)
        if u >= 2:
            pe.wait_ge(self.finished, u - 1)
        if m in (2, 5):
            mm = self.nc.tensor.matmul(ps[:, :], ones[:, :], a[:, :], start=True, stop=True)
        else:
            for k in range(4):
                mm = self.nc.tensor.matmul(ps[:, k:k + 1], a[:, P * k:P * k + P], ones[:, 0:1], start=True, stop=True)
        mm.then_inc(self.spread_out, 1)

    def finish(self, dve, u):
        v, M, ps, (m, n) = self.nc.vector, self.M, self.ps[u % 2], self.units[u]
        c = slice(4 * n, 4 * n + 4)
        dve.wait_ge(self.spread_out, u + 1)
        if m in (2, 5):
            dve.wait_ge(self.gb_in, 16 * len(self.gbias))
            cols = slice(512 * n, 512 * n + 512)
            self.chain.link(v.tensor_tensor(M.gate[m // 3][:, cols], ps[:, :], self.gbias[m][:, cols], ALU.add))
        elif m in (0, 3):
            self.chain.link(v.tensor_tensor(M.shift[m // 3][:, c], ps[:, 0:4], self.cols[:, 8 * m + 4 * n:8 * m + 4 * n + 4],
                                            ALU.add))
        else:
            g = 56 + 8 * (m // 3) + 4 * n
            self.chain.link(v.tensor_tensor(self.t[:, :], ps[:, 0:4], self.cols[:, 8 * m + 4 * n:8 * m + 4 * n + 4], ALU.add))
            self.chain.link(v.scalar_tensor_tensor(out=M.scale[m // 3][:, c], in0=self.t[:, :], scalar=1.0,
                                                   in1=self.cols[:, g:g + 4], op0=ALU.add, op1=ALU.mult))
        dve.sem_inc(self.finished, 1)


def first_modulation(nc, C, M, A, mod):
    with Scope(nc) as s:
        rows = BiasRows(s, nc, C, A)
        sig_ready = s.sem("sc_sig")
        own = s.sem("sc_own")
        with nc.Block() as block:
            @block.sync
            def _(sp):
                mod.load(sp, 2)

            @block.scalar
            def _(act):
                for b, cols in enumerate((C.cols1, C.cols2)):
                    nc.scalar.activation(M[b].sc[:, :], cols[:, 48:56], ACT.Sigmoid).then_inc(sig_ready, 1)
                rows.scalar(act)

            @block.gpsimd
            def _(pool):
                rows.pool(pool)

            @block.vector
            def _(dve):
                ch = Chain(dve, own)
                dve.wait_ge(sig_ready, 2)
                for b, cols in enumerate((C.cols1, C.cols2)):
                    ch.link(nc.vector.tensor_tensor(M[b].sc[:, :], M[b].sc[:, :], cols[:, 48:56], ALU.mult))
                for u in range(5):
                    if u < 4:
                        mod.sum(dve, u)
                    if u == 0:
                        rows.negate(dve)
                    if u == 1:
                        rows.copy_rows(dve)
                    if u >= 1:
                        mod.finish(dve, u - 1)

            @block.tensor
            def _(pe):
                rows.rows(pe)
                for u in range(4):
                    mod.spread(pe, u)
                rows.turn_over(pe)


def norm_turn(nc, C, scale, shift, uT, tag, xn_dram=None, split=None):
    with Scope(nc) as s:
        xn = s.sb(f"xn{tag}", [P, NT, D])
        ssq = s.sb(f"ssq{tag}", [P, NT])
        var = s.sb(f"var{tag}", [P, NT])
        rstd = s.sb(f"rstd{tag}", [P, NT])
        ps = [s.bank(f"nt_ps{i}{tag}") for i in range(4)]
        squares = s.sem(f"squares{tag}")
        var_ready = s.sem(f"var_ready{tag}")
        rstd_ready = s.sem(f"rstd_ready{tag}")
        xn_ready = s.sem(f"xn_ready{tag}")
        turned = s.sem(f"turned{tag}")
        out_done = s.sems(f"out_done{tag}", 2)
        stored = s.sem(f"stored{tag}")
        high_ready = s.sem(f"high_ready{tag}")
        with nc.Block() as block:
            @block.scalar
            def _(act):
                for t in range(NT):
                    nc.scalar.activation(xn[:, t, :], C.h[:, t, :], ACT.Square,
                                         accum_out=ssq[:, t:t + 1]).then_inc(squares, 1)
                for k in range(1, KD, 2):
                    act.wait_ge(turned, k + 1)
                    nc.scalar.activation(uT[:, k, :], ps[k % 4][:, :], ACT.Identity, scale=scale[:, k:k + 1],
                                         bias=shift[:, k:k + 1]).then_inc(out_done[1], 1)
                    if split:
                        for j in (k - 1, k):
                            act.wait_ge(out_done[j % 2], j // 2 + 1)
                            nc.scalar.activation(split[0][:, j, :], uT[:, j, :], ACT.Copy).then_inc(high_ready, 1)

            @block.gpsimd
            def _(pool):
                pool.wait_ge(var_ready, 1)
                pool.tensor_tensor(rstd[:, :], var[:, :], C.neghalf[:, 0:NT], ALU.pow).then_inc(rstd_ready, 1)

            @block.vector
            def _(dve):
                dve.wait_ge(squares, NT)
                nc.vector.tensor_scalar(var[:, :], ssq[:, :], 1.0 / D, EPS, ALU.mult, ALU.add).then_inc(var_ready, 1)
                dve.wait_ge(rstd_ready, 1)
                for t in range(NT):
                    nc.vector.tensor_scalar(xn[:, t, :], C.h[:, t, :], rstd[:, t:t + 1], None,
                                            ALU.mult).then_inc(xn_ready, 1)
                for k in range(0, KD, 2):
                    dve.wait_ge(turned, k + 1)
                    nc.vector.tensor_scalar(uT[:, k, :], ps[k % 4][:, :], scale[:, k:k + 1], shift[:, k:k + 1],
                                            ALU.mult, ALU.add).then_inc(out_done[0], 1)
                if split:
                    for k in range(KD):
                        dve.wait_ge(high_ready, k + 1)
                        low(nc.vector, split[1][:, k, :], uT[:, k, :], split[0][:, k, :])

            @block.tensor
            def _(pe):
                pe.wait_ge(xn_ready, NT)
                for k in range(KD):
                    if k >= 4:
                        pe.wait_ge(out_done[k % 2], k // 2 - 1)
                    for t in range(NT):
                        mm = nc.tensor.transpose(ps[k % 4][:, P * t:P * t + P], xn[:, t, P * k:P * k + P], C.ident[:, :])
                    mm.then_inc(turned, 1)

            if xn_dram is not None:
                @block.sync
                def _(sp):
                    sp.wait_ge(xn_ready, NT)
                    sp.dma_start(xn_dram.rearrange("(t p) d -> p t d", p=P), xn[:, :, :]).then_inc(stored, 16)
                    sp.wait_ge(stored, 16)


def low(v, out, x, high):
    return v.tensor_tensor(out, x, high.bitcast(F32), ALU.subtract)


def matmul3(nc, ps, a, b, start, stop):
    (ah, al), (bh, bl) = a, b
    nc.tensor.matmul(ps, ah, bh, start=start, stop=False)
    nc.tensor.matmul(ps, ah, bl, start=False, stop=False)
    return nc.tensor.matmul(ps, al, bh, start=False, stop=stop)


class Weights:

    def __init__(self, s, nc, tag):
        self.nc = nc
        self.raw = [s.sb(f"w_raw{i}{tag}", [P, 4, 512]) for i in range(2)]
        self.hi = [s.sb(f"w_hi{i}{tag}", [P, 4, 512], F32R) for i in range(2)]
        self.lo = [s.twin(f"w_lo{i}{tag}", f"w_raw{i}{tag}", [P, 4, 512]) for i in range(2)]
        self.landed = s.sems(f"w_landed{tag}", 2)
        self.high_ready = s.sem(f"w_high{tag}")
        self.low_ready = s.sem(f"w_low{tag}")

    def load(self, sp, i, src, n=512, free=None):
        if free:
            sp.wait_ge(*free)
        sp.dma_start(self.raw[i % 2][:, :, 0:n], src).then_inc(self.landed[i % 2], 16)

    def high(self, act, i, n=512):
        act.wait_ge(self.landed[i % 2], 16 * (i // 2 + 1))
        self.nc.scalar.activation(self.hi[i % 2][:, :, 0:n], self.raw[i % 2][:, :, 0:n], ACT.Copy).then_inc(self.high_ready, 1)

    def low(self, dve, i, n=512):
        dve.wait_ge(self.high_ready, i + 1)
        low(self.nc.vector, self.lo[i % 2][:, :, 0:n], self.raw[i % 2][:, :, 0:n], self.hi[i % 2][:, :, 0:n]).then_inc(self.low_ready, 1)

    def get(self, i, k, c, n):
        return self.hi[i % 2][:, k, c:c + n], self.lo[i % 2][:, k, c:c + n]


def project(nc, C, split, w, steps, tag):
    u = lambda k, c, n: tuple(x[:, k, c:c + n] for x in split)
    with Scope(nc) as s:
        W = Weights(s, nc, tag)
        ps = [[s.bank(f"pp{i}{b}{tag}") for b in range(4)] for i in range(2)]
        half_used = s.sem(f"half_used{tag}")
        bank_ready = s.sem(f"bank_ready{tag}")
        bank_out = s.sem(f"bank_out{tag}")
        banks = [(n // P if turned else NT) for _, n, turned, _ in steps]
        upto = [sum(banks[:i]) for i in range(len(steps) + 1)]
        halves = 2 * len(steps)
        with nc.Block() as block:
            @block.sync
            def _(sp):
                for i in range(halves):
                    col, n, _, _ = steps[i // 2]
                    free = None
                    if i >= 2:
                        free = (bank_ready, upto[i // 2]) if i % 2 else (half_used, i // 2)
                    W.load(sp, i, w[512 * (i % 2):512 * (i % 2) + 512, col:col + n].rearrange("(k p) n -> p k n", p=P), n, free)

            @block.tensor
            def _(pe):
                for i in range(halves):
                    _, n, turned, _ = steps[i // 2]
                    pe.wait_ge(W.low_ready, i + 1)
                    if i >= 4 and i % 2 == 0:
                        pe.wait_ge(bank_out, upto[i // 2 - 1])
                    for b in range(banks[i // 2]):
                        bank = ps[i // 2 % 2][b]
                        for k in range(4):
                            start, stop, kk = (i % 2 == 0 and k == 0), (i % 2 == 1 and k == 3), 4 * (i % 2) + k
                            if turned:
                                mm = matmul3(nc, bank[:, :], W.get(i, k, P * b, P), u(kk, 0, TOK), start, stop)
                            else:
                                mm = matmul3(nc, bank[:, 0:n], u(kk, P * b, P), W.get(i, k, 0, n), start, stop)
                        if i % 2:
                            mm.then_inc(bank_ready, 1)
                    if i % 2 == 0:
                        mm.then_inc(half_used, 1)

            @block.vector
            def _(dve):
                for i in range(halves):
                    W.low(dve, i, steps[i // 2][1])

            @block.scalar
            def _(act):
                width = lambda i: steps[i // 2][1]
                W.high(act, 0, width(0))
                W.high(act, 1, width(1))
                for i, (_, _, _, out) in enumerate(steps):
                    if 2 * i + 2 < halves:
                        W.high(act, 2 * i + 2, width(2 * i + 2))
                    for b in range(banks[i]):
                        act.wait_ge(bank_ready, upto[i] + b + 1)
                        for dst, src, func, scale in out(b, ps[i % 2][b]):
                            ins = nc.scalar.activation(dst, src, func, scale=scale)
                        ins.then_inc(bank_out, 1)
                    if 2 * i + 3 < halves:
                        W.high(act, 2 * i + 3, width(2 * i + 3))


def head_norms(nc, C, B):
    with Scope(nc) as s:
        sq = s.sb("sq", [P, NT * 512])
        kn = s.sb("kn", [P, NT, 2, P])
        ss = s.sb("ss", [P, 48])
        rs = s.sb("rs", [P, 48])
        qn = s.sb("qn", [P, NT, 4, 2, HD])
        ps = [s.bank(f"hn_ps{i}") for i in range(6)]
        own = s.sem("hn_own")
        var_ready = s.sem("hn_var")
        rs_ready = s.sem("hn_rs")
        qn_ready = s.sem("qn_ready")
        turned = s.sem("hn_turned")
        zeroed = s.sem("hn_zeroed")
        with nc.Block() as block:
            @block.vector
            def _(dve):
                ch = Chain(dve, own)
                q = B.qa[:, :, :].rearrange("p t n -> p (t n)")
                ch.link(nc.vector.tensor_tensor(sq[:, :], q, q, ALU.mult))
                ch.link(nc.vector.tensor_reduce(ss[:, 0:32], sq[:, :].rearrange("p (h d) -> p h d", d=HD), AX.X, ALU.add))
                for w in range(2):
                    k = B.kv[:, :, 256 * w:256 * w + P]
                    o = sq[:, 0:NT * P].rearrange("p (t n) -> p t n", t=NT)
                    ch.link(nc.vector.tensor_tensor(o, k, k, ALU.mult))
                    ch.link(nc.vector.tensor_reduce(ss[:, 32 + 8 * w:40 + 8 * w],
                                                    sq[:, 0:NT * P].rearrange("p (h d) -> p h d", d=HD), AX.X, ALU.add))
                nc.vector.tensor_scalar(ss[:, :], ss[:, :], 1.0 / HD, EPS, ALU.mult, ALU.add).then_inc(var_ready, 1)
                dve.wait_ge(rs_ready, 1)
                for t in range(NT):
                    src = B.qa[:, t, :].rearrange("p (f i d) -> p i f d", f=2, i=4)
                    r = rs[:, 8 * t:8 * t + 8].rearrange("p (f i) -> p f i", f=2)
                    for f in range(2):
                        nc.vector.tensor_tensor(qn[:, t, :, f, :], src[:, :, f, :], bcast(r[:, f, :], HD), ALU.mult)
                    for w in range(2):
                        ins = nc.vector.tensor_tensor(
                            kn[:, t, w, :].rearrange("p (f d) -> p f d", f=2),
                            B.kv[:, t, 256 * w:256 * w + P].rearrange("p (f d) -> p f d", f=2),
                            bcast(rs[:, 32 + 8 * w + 2 * t:34 + 8 * w + 2 * t], HD), ALU.mult)
                    ins.then_inc(qn_ready, 1)
                for i in range(4):
                    dve.wait_ge(turned, i + 1)
                    nc.vector.tensor_scalar(B.qT[:, i, :], ps[i][:, :], C.cols1[:, 72:73], -HD ** -0.5, ALU.mult, ALU.mult)

            @block.gpsimd
            def _(pool):
                pool.memset(B.ksz[:, :, :], 0.0).then_inc(zeroed, 1)
                pool.memset(B.kwz[:, :, :], 0.0).then_inc(zeroed, 1)
                pool.wait_ge(var_ready, 1)
                pool.tensor_tensor(rs[:, :], ss[:, :], C.neghalf[:, 0:48], ALU.pow).then_inc(rs_ready, 1)

            @block.scalar
            def _(act):
                act.wait_ge(zeroed, 2)
                for w, kz in enumerate((B.ksz, B.kwz)):
                    act.wait_ge(turned, 5 + w)
                    for f in range(2):
                        r = slice(64 * f, 64 * f + 64)
                        nc.scalar.activation(kz[r, f, :], ps[4 + w][r, :], ACT.Identity, bias=0.0,
                                             scale=C.cols1[r, 74 + w:75 + w])

            @block.tensor
            def _(pe):
                pe.wait_ge(qn_ready, NT)
                for i in range(4):
                    for t in range(NT):
                        mm = nc.tensor.transpose(ps[i][:, P * t:P * t + P],
                                                 qn[:, t, i, :, :].rearrange("p f d -> p (f d)"), C.ident[:, :])
                    mm.then_inc(turned, 1)
                for w in range(2):
                    for t in range(NT):
                        mm = nc.tensor.transpose(ps[4 + w][:, P * t:P * t + P], kn[:, t, w, :], C.ident[:, :])
                    mm.then_inc(turned, 1)


def compress(nc, C, A, B):
    with Scope(nc) as s:
        w1 = [s.sb(f"cw1{i}", [P, CMP, P]) for i in range(2)]
        w2 = [s.sb(f"cw2{i}", [P, P]) for i in range(2)]
        post = s.sb("post", [P, CMP])
        posr = s.sb("posr", [CMP, P])
        win = [s.sb(f"win{i}", [P, CMP, CMP]) for i in range(2)]
        e = [s.sb(f"ce{i}", [P, CMP]) for i in range(2)]
        pre = [s.sb(f"cpre{i}", [P, CMP]) for i in range(2)]
        pc = [s.sb(f"cpc{i}", [P, 2]) for i in range(2)]
        hid = [s.sb(f"hid{i}", [P, 4, CMP]) for i in range(2)]
        kc = s.sb("kc", [64, P])
        ksq = s.sb("ksq", [64, P])
        ss = s.sb("css", [64, 1])
        rs = s.sb("crs", [64, 1])
        hps = [s.bank(f"hps{i}") for i in range(2)]
        ops = [s.bank(f"cops{i}") for i in range(2)]
        tps = s.bank("ctps")
        pps = s.bank("cpps")
        zeroed = s.sem("c_zeroed")
        w_in = s.sem("cw_in")
        pos_in = s.sem("pos_in")
        pos_ready = s.sem("pos_ready")
        pos_copied = s.sem("pos_copied")
        win_ready = s.sem("win_ready")
        hid_ps = s.sem("hid_ps")
        pre_ready = s.sem("pre_ready")
        exp_done = s.sem("c_exp")
        hid_ready = s.sem("hid_ready")
        out_ready = s.sem("c_out_ready")
        own = s.sem("c_own")
        var_ready = s.sem("c_var")
        rs_ready = s.sem("c_rs")
        kc_ready = s.sem("kc_ready")
        kc_turned = s.sem("kc_turned")
        with nc.Block() as block:
            @block.gpsimd
            def _(pool):
                ch = Chain(pool, zeroed)
                for i in range(2):
                    ch.link(pool.memset(w1[i][:, :, :], 0.0))
                    ch.link(pool.memset(w2[i][:, :], 0.0))
                    ch.link(pool.memset(hid[i][:, :, :], 0.0))
                ch.link(pool.memset(B.vcd[:, :], 0.0))
                pool.wait_ge(var_ready, 1)
                pool.tensor_tensor(rs[:, :], ss[:, :], C.neghalf[0:64, 0:1], ALU.pow).then_inc(rs_ready, 1)

            @block.sync
            def _(sp):
                for f in range(2):
                    sp.dma_start(posr[:, 64 * f:64 * f + 64], A["cmp_pos"][0]).then_inc(pos_in, 16)
                sp.wait_ge(zeroed, 7)
                for i, n in enumerate("kv"):
                    for f in range(2):
                        r = slice(64 * f, 64 * f + 64)
                        sp.dma_start(w1[i][r, :, r], A[f"cmp_{n}_w1"][0].rearrange("(j d) h -> d j h", d=HD)).then_inc(w_in, 16)
                        sp.dma_start(w2[i][r, r], A[f"cmp_{n}_w2"][0]).then_inc(w_in, 16)

            @block.vector
            def _(dve):
                ch = Chain(dve, own)
                dve.wait_ge(pos_ready, 1)
                nc.vector.tensor_copy(post[:, :], pps[:, 0:CMP]).then_inc(pos_copied, 1)
                dve.wait_ge(pos_copied, 1)
                for i, src in enumerate((B.kcT, B.vcT)):
                    base = src[:, :]
                    view = bass.AP(tensor=base.tensor, offset=base.offset, ap=[base.ap[0], [1, CMP], [STRIDE, NCMP]])
                    nc.vector.tensor_copy(win[i][:, :, 0:NCMP], view)
                    nc.vector.tensor_copy(win[i][:, :, NCMP:CMP], post[:, :].rearrange("p (j a) -> p j a", a=1)).then_inc(win_ready, 1)
                for i in range(2):
                    dve.wait_ge(hid_ps, i + 1)
                    ch.link(nc.vector.tensor_copy(pc[i][:, 0:1], hps[i][:, NCMP:CMP]))
                    ch.link(nc.vector.tensor_scalar(pre[i][:, :], hps[i][:, 0:CMP], pc[i][:, 0:1], None, ALU.add))
                    dve.sem_inc(pre_ready, 1)
                for i in range(2):
                    dve.wait_ge(exp_done, i + 1)
                    dve.wait_ge(zeroed, 7)
                    for g in range(4):
                        r = slice(64 * (g % 2), 64 * (g % 2) + 64)
                        if i == 0 and g >= 2:
                            continue
                        ins = nc.vector.tensor_tensor(hid[i][r, g, 0:NCMP], e[i][r, 0:NCMP], pre[i][r, 0:NCMP], ALU.mult)
                    ins.then_inc(hid_ready, 1)
                dve.wait_ge(out_ready, 1)
                ch.link(nc.vector.tensor_copy(kc[:, :], ops[0][0:64, 0:P]))
                ch.link(nc.vector.tensor_tensor(ksq[:, :], kc[:, :], kc[:, :], ALU.mult))
                ch.link(nc.vector.tensor_reduce(ss[:, :], ksq[:, :], AX.X, ALU.add))
                nc.vector.tensor_scalar(ss[:, :], ss[:, :], 1.0 / HD, EPS, ALU.mult, ALU.add).then_inc(var_ready, 1)
                dve.wait_ge(rs_ready, 1)
                nc.vector.tensor_scalar(kc[:, :], kc[:, :], rs[:, 0:1], None, ALU.mult).then_inc(kc_ready, 1)
                dve.wait_ge(out_ready, 2)
                for a in range(2):
                    r = slice(64 * a, 64 * a + 64)
                    nc.vector.tensor_copy(B.vcd[r, P * a:P * a + P], ops[1][r, 0:P])
                dve.wait_ge(kc_turned, 1)
                nc.vector.tensor_scalar(B.kcd[:, :], tps[:, 0:64], C.cols1[:, 73:74], None, ALU.mult)

            @block.scalar
            def _(act):
                for i in range(2):
                    act.wait_ge(pre_ready, i + 1)
                    nc.scalar.activation(e[i][:, :], pre[i][:, :], ACT.Sigmoid).then_inc(exp_done, 1)

            @block.tensor
            def _(pe):
                pe.wait_ge(pos_in, 32)
                nc.tensor.transpose(pps[:, 0:CMP], posr[:, :], C.ident[0:CMP, 0:CMP]).then_inc(pos_ready, 1)
                pe.wait_ge(w_in, 128)
                for i in range(2):
                    pe.wait_ge(win_ready, i + 1)
                    for j in range(CMP):
                        mm = nc.tensor.matmul(hps[i][:, 0:CMP], w1[i][:, j, :], win[i][:, j, :],
                                              start=(j == 0), stop=(j == CMP - 1))
                    mm.then_inc(hid_ps, 1)
                pe.wait_ge(hid_ready, 1)
                nc.tensor.matmul(ops[0][0:64, 0:P], hid[0][:, 0:2, :].rearrange("p g c -> p (g c)"), w2[0][:, :],
                                 start=True, stop=True).then_inc(out_ready, 1)
                pe.wait_ge(hid_ready, 2)
                nc.tensor.matmul(ops[1][:, 0:P], hid[1][:, :, :].rearrange("p g c -> p (g c)"), w2[1][:, :],
                                 start=True, stop=True).then_inc(out_ready, 1)
                pe.wait_ge(kc_ready, 1)
                nc.tensor.transpose(tps[:, 0:64], kc[:, :], C.ident[0:64, 0:64]).then_inc(kc_turned, 1)


def compressed_attention(nc, C, B):
    with Scope(nc) as s:
        L = [s.sb(f"cl{i}", [P, 8, CMP]) for i in range(2)]
        mn = s.sb("cmn", [P, 8])
        sm = s.sb("csm", [P, 8])
        pT = [s.sb(f"cpt{i}", [P, 2, P]) for i in range(2)]
        sps = [s.bank(f"csps{i}") for i in range(2)]
        tps = [s.bank(f"ctp{i}") for i in range(2)]
        ops = [s.bank(f"cop{i}") for i in range(2)]
        scores = s.sem("ca_scores")
        ready = s.sem("ca_ready")
        exps = s.sem("ca_exps")
        probs = s.sem("ca_probs")
        turned = s.sem("ca_turned")
        copied = s.sem("ca_copied")
        summed = s.sem("ca_summed")
        outs = s.sem("ca_outs")
        own = s.sem("ca_own")
        with nc.Block() as block:
            @block.tensor
            def _(pe):
                def score(j):
                    if j >= 2:
                        pe.wait_ge(ready, j - 1)
                    for i in range(4):
                        mm = nc.tensor.matmul(sps[j % 2][:, 64 * i:64 * i + 64], B.qT[:, i, P * j:P * j + P], B.kcd[:, :],
                                              start=True, stop=True)
                    mm.then_inc(scores, 1)

                score(0)
                for j in range(NT):
                    if j + 1 < NT:
                        score(j + 1)
                    pe.wait_ge(probs, j + 1)
                    if j >= 2:
                        pe.wait_ge(copied, j - 1)
                    for g in range(2):
                        mm = nc.tensor.transpose(tps[j % 2][:, P * g:P * g + P],
                                                 L[j % 2][:, 4 * g:4 * g + 4, :].rearrange("p h c -> p (h c)"), C.ident[:, :])
                    mm.then_inc(turned, 1)
                    pe.wait_ge(copied, j + 1)
                    if j >= 2:
                        pe.wait_ge(outs, j - 1)
                    for g in range(2):
                        mm = nc.tensor.matmul(ops[j % 2][:, 256 * g:256 * g + 256], pT[j % 2][:, g, :], B.vcd[:, :],
                                              start=True, stop=True)
                    mm.then_inc(summed, 1)

            @block.scalar
            def _(act):
                for j in range(NT):
                    act.wait_ge(ready, j + 1)
                    nc.scalar.activation(L[j % 2][:, :, :], L[j % 2][:, :, :], ACT.Exp, scale=-1.0).then_inc(exps, 1)
                    act.wait_ge(turned, j + 1)
                    if j >= 2:
                        act.wait_ge(summed, j - 1)
                    nc.scalar.activation(pT[j % 2][:, :, :].rearrange("p g c -> p (g c)"), tps[j % 2][:, 0:256],
                                         ACT.Copy).then_inc(copied, 1)

            @block.vector
            def _(dve):
                ch = Chain(dve, own)
                for j in range(NT):
                    l = L[j % 2]
                    if j >= 2:
                        dve.wait_ge(turned, j - 1)
                    dve.wait_ge(scores, j + 1)
                    ch.link(nc.vector.tensor_tensor(l[:, :, :].rearrange("p h c -> p (h c)"), sps[j % 2][:, 0:256],
                                                    C.cbias[:, j, :], ALU.add))
                    ch.link(nc.vector.tensor_reduce(mn[:, :], l[:, :, :], AX.X, ALU.min))
                    nc.vector.tensor_tensor(l[:, :, :], l[:, :, :], bcast(mn[:, :], CMP), ALU.subtract).then_inc(ready, 1)
                    dve.wait_ge(exps, j + 1)
                    base = C.cmask[:, j, :]
                    mask = bass.AP(tensor=base.tensor, offset=base.offset, ap=[base.ap[0], [0, 8], [1, CMP]])
                    ch.link(nc.vector.tensor_tensor(l[:, :, :], l[:, :, :], mask, ALU.mult))
                    dve.sem_inc(probs, 1)
                    ch.link(nc.vector.tensor_reduce(sm[:, :], l[:, :, :], AX.X, ALU.add))
                    ch.link(nc.vector.tensor_scalar(sm[:, :], sm[:, :], 1e-30, None, ALU.max))
                    ch.link(nc.vector.reciprocal(sm[:, :], sm[:, :]))
                    g0 = B.ga[:, j, 0:24:3].rearrange("p (f i) -> p i f", f=2)
                    ch.link(nc.vector.tensor_tensor(sm[:, :].rearrange("p (i f) -> p i f", f=2),
                                                    sm[:, :].rearrange("p (i f) -> p i f", f=2), g0, ALU.mult))
                    dve.wait_ge(summed, j + 1)
                    for f in range(2):
                        src = ops[j % 2][:, :].rearrange("p (i f d) -> p i f d", f=2, d=HD)[:, :, f, :]
                        r = sm[:, f:8:2]
                        ins = nc.vector.tensor_tensor(
                            B.oa[:, j, 256 * f:256 * f + 256].rearrange("p (i d) -> p i d", d=HD), src, bcast(r, HD), ALU.mult)
                    ins.then_inc(outs, 1)


def repeat(eng, start, end):
    return nullcontext(start) if end == start + 1 else eng.Fori(start, end)


class Heads:

    def __init__(self, s, nc, tag, qst, dv=HD):
        self.nc, self.dv = nc, dv
        self.qst = qst
        self.probs = [s.sb(f"probs{i}{tag}", [P, OFF[NT]]) for i in range(2)]
        self.pT = [s.sb(f"pT{i}{tag}", [P, 512]) for i in range(2)]
        self.sps = [s.bank(f"sps{j}{tag}") for j in range(NT)]
        self.tps = [s.bank(f"tps{j}{tag}") for j in range(2)]
        self.ops = [s.bank(f"ops{j}{tag}") for j in range(2)]
        self.probs_begin = 0
        self.q_staged = s.sem(f"q_staged{tag}")
        self.scores_ready = s.sem(f"scores_ready{tag}")
        self.scores_read = s.sem(f"scores_read{tag}")
        self.probs_ready = s.sem(f"probs_ready{tag}")
        self.turned = s.sem(f"turned{tag}")
        self.copied = s.sems(f"copied{tag}", 2)
        self.weighed = s.sem(f"weighed{tag}")
        self.head_out = s.sem(f"head_out{tag}")

    def pe(self, pe, C, units, keys, values):
        nc = self.nc

        def scores(n, half, i):
            pe.wait_ge(self.q_staged, i + 1)
            for j in range(NT):
                w = P * (j + 1)
                pe.wait_ge(self.scores_read, 4 * n + j + 1)
                nc.tensor.matmul(self.sps[j][:, 0:w], self.qst[half][:, P * j:P * j + P], keys(half, i, w),
                                 start=True, stop=True).then_inc(self.scores_ready, 1)

        def turn(n, half, j):
            pe.wait_ge(self.probs_ready, 4 * n + j + 1 + self.probs_begin)
            pe.wait_ge(self.copied[j % 2], 2 * n + j // 2 + 1)
            for b in range(j + 1):
                mm = nc.tensor.transpose(self.tps[j % 2][:, P * b:P * b + P],
                                         self.probs[half][:, OFF[j] + P * b:OFF[j] + P * b + P], C.ident[:, :])
            mm.then_inc(self.turned, 1)

        def weigh(n, half, i, j):
            if j == 0:
                pe.wait_ge(self.head_out, n + 1)
            pe.wait_ge(self.copied[j % 2], 2 * n + j // 2 + 2)
            for b in range(j + 1):
                mm = nc.tensor.matmul(self.ops[half][:, self.dv * j:self.dv * (j + 1)], self.pT[j % 2][:, P * b:P * b + P],
                                      values(b, half, i), start=(b == 0), stop=(b == j))
            mm.then_inc(self.weighed, 1)

        def head(n, half, i):
            turn(n, half, 0)
            turn(n, half, 1)
            weigh(n, half, i, 0)
            turn(n, half, 2)
            weigh(n, half, i, 1)
            turn(n, half, 3)
            weigh(n, half, i, 2)
            weigh(n, half, i, 3)

        pe.sem_inc(self.turned, 8)
        pe.sem_inc(self.weighed, 2)
        scores(0, 0, 0)
        with repeat(pe, 0, units - 1) as i:
            scores(2 * i + 1, 1, i)
            head(2 * i, 0, i)
            scores(2 * i + 2, 0, i + 1)
            head(2 * i + 1, 1, i)
        i = units - 1
        scores(2 * i + 1, 1, i)
        head(2 * i, 0, i)
        head(2 * i + 1, 1, i)

    def copy_turned(self, eng, n, j):
        w = P * (j + 1)
        eng.wait_ge(self.turned, 4 * n + j + 9)
        eng.wait_ge(self.weighed, 4 * n + j + 1)
        if j % 2:
            self.nc.scalar.activation(self.pT[1][:, 0:w], self.tps[1][:, 0:w], ACT.Copy).then_inc(self.copied[1], 1)
        else:
            self.nc.vector.tensor_copy(self.pT[0][:, 0:w], self.tps[0][:, 0:w]).then_inc(self.copied[0], 1)

    def run(self, eng, units, rounds):
        rounds(None, (0, 0, 0))
        with repeat(eng, 0, units - 1) as i:
            rounds((2 * i, 0, i), (2 * i + 1, 1, i))
            rounds((2 * i + 1, 1, i), (2 * i + 2, 0, i + 1))
        i = units - 1
        rounds((2 * i, 0, i), (2 * i + 1, 1, i))
        rounds((2 * i + 1, 1, i), None)


def softmax_attention(nc, C, tag, qT, keys, values, out, units=4, bias=None, gate=None, add=False):
    with Scope(nc) as s:
        qst = s.sb(f"qst{tag}", [P, 512])
        H = Heads(s, nc, tag, [qst, qst])
        bst = [s.sb(f"bst{i}{tag}", [P, 512]) for i in range(2)] if bias else [C.ban, C.ban]
        low = [s.sb(f"low{i}{tag}", [P, NT]) for i in range(2)]
        sums = [s.sb(f"sums{i}{tag}", [P, NT]) for i in range(2)]
        coef = [s.sb(f"coef{i}{tag}", [P, NT]) for i in range(2)]
        tmp = s.sb(f"tmp{tag}", [P, NT, HD])
        bias_staged = s.sem(f"bias_staged{tag}")
        begun = s.sem(f"begun{tag}")
        own = s.sem(f"own{tag}")
        links = 1 + bool(gate) + bool(add) + 1
        with nc.Block() as block:
            @block.tensor
            def _(pe):
                H.pe(pe, C, units, keys, values)

            @block.gpsimd
            def _(pool):
                def stage(i, first):
                    if not first:
                        pool.wait_ge(H.scores_ready, 8 * i)
                    pool.tensor_copy(qst[:, :], qT(i)).then_inc(H.q_staged, 1)
                    if bias:
                        for half in range(2):
                            if not first:
                                pool.wait_ge(H.scores_read, 8 * i + 4 * half)
                            pool.tensor_copy(bst[half][:, :], bias(half, i)).then_inc(bias_staged, 1)
                stage(0, True)
                with pool.Fori(1, units) as i:
                    stage(i, False)

            @block.vector
            def _(dve):
                def logits(n, half, j):
                    w = P * (j + 1)
                    if j == 0:
                        dve.wait_ge(H.turned, 4 * n + 4)
                        if bias:
                            dve.wait_ge(bias_staged, n + 1)
                    dve.wait_ge(H.scores_ready, 4 * n + j + 1)
                    dve.sem_inc(begun, 1)
                    nc.vector.tensor_tensor_reduce(H.probs[half][:, OFF[j]:OFF[j + 1]], H.sps[j][:, 0:w],
                                                   bst[half][:, P * (NT - 1 - j):512], 1.0, 3e38, ALU.add, ALU.min,
                                                   low[half][:, j:j + 1]).then_inc(H.scores_read, 1)

                def finish(n, half, i):
                    ch = Chain(dve, own, n * links)
                    dve.wait_ge(H.weighed, 4 * n + 6)
                    ch.link(nc.vector.reciprocal(coef[half][:, :], sums[half][:, :]))
                    if gate:
                        ch.link(nc.vector.tensor_tensor(coef[half][:, :], coef[half][:, :], gate(half, i), ALU.mult))
                    o = H.ops[half][:, 0:NT * HD].rearrange("p (t d) -> p t d", d=HD)
                    if add:
                        ch.link(nc.vector.tensor_tensor(tmp[:, :, :], o, bcast(coef[half][:, :], HD), ALU.mult))
                        ch.link(nc.vector.tensor_tensor(out(half, i), out(half, i), tmp[:, :, :], ALU.add))
                    else:
                        ch.link(nc.vector.tensor_tensor(out(half, i), o, bcast(coef[half][:, :], HD), ALU.mult))
                    dve.sem_inc(H.head_out, 1)
                    assert ch.n == links

                def rounds(now, nxt):
                    for j in range(NT):
                        if nxt:
                            logits(nxt[0], nxt[1], j)
                        if now and j % 2 == 0:
                            H.copy_turned(dve, now[0], j)
                    if now:
                        finish(*now)
                dve.sem_inc(H.scores_read, 4)
                dve.sem_inc(H.copied[0], 1)
                dve.sem_inc(H.head_out, 2)
                H.run(dve, units, rounds)

            @block.scalar
            def _(act):
                def rounds(now, nxt):
                    for j in range(NT):
                        if now and j % 2:
                            H.copy_turned(act, now[0], j)
                        if nxt:
                            n, half, _ = nxt
                            if j == 0:
                                act.wait_ge(H.head_out, n + 1)
                            act.wait_ge(H.scores_read, 4 * n + j + 5)
                            p = H.probs[half][:, OFF[j]:OFF[j + 1]]
                            nc.scalar.activation(p, p, ACT.Exp, scale=-1.0, bias=low[half][:, j:j + 1],
                                                 accum_out=sums[half][:, j:j + 1]).then_inc(H.probs_ready, 1)
                act.sem_inc(H.copied[1], 1)
                H.run(act, units, rounds)


def stick_breaking(nc, C, B):
    with Scope(nc) as s:
        qst = s.sb("sb_qst", [P, 512])
        H = Heads(s, nc, "sb", [qst, qst])
        soft = [s.sb(f"soft{i}", [P, OFF[NT]]) for i in range(2)]
        pos = [s.sb(f"pos{i}", [P, OFF[NT]]) for i in range(2)]
        abs_ready = s.sem("sb_abs")
        soft_ready = s.sem("sb_soft")
        exponent_ready = s.sem("sb_exponent")
        own = s.sem("sb_own")
        act_own = s.sem("sb_act_own")
        with nc.Block() as block:
            @block.tensor
            def _(pe):
                H.pe(pe, C, 4, lambda half, i, w: B.sbk[:, bass.ds(i, 1), half, 0:w].rearrange("p a n -> p (a n)"),
                     lambda b, half, i: B.sbv[:, b, bass.ds(i * 128 + 64 * half, 64)])

            @block.gpsimd
            def _(pool):
                src = lambda i: B.sbq[:, bass.ds(i, 1), :].rearrange("p a n -> p (a n)")
                pool.tensor_copy(qst[:, :], src(0)).then_inc(H.q_staged, 1)
                with pool.Fori(1, 4) as i:
                    pool.wait_ge(H.scores_ready, 8 * i)
                    pool.tensor_copy(qst[:, :], src(i)).then_inc(H.q_staged, 1)

            @block.vector
            def _(dve):
                links = 3 * NT

                def logits(ch, n, half, j):
                    z, w = H.probs[half][:, OFF[j]:OFF[j + 1]], P * (j + 1)
                    if j == 0:
                        dve.wait_ge(H.turned, 4 * n + 4)
                    dve.wait_ge(H.scores_ready, 4 * n + j + 1)
                    nc.vector.tensor_tensor(z, H.sps[j][:, 0:w], C.ban_self[:, P * (NT - 1 - j):512],
                                            ALU.add).then_inc(H.scores_read, 1)
                    dve.wait_ge(H.scores_read, 4 * n + j + 5)
                    nc.vector.scalar_tensor_tensor(out=soft[half][:, OFF[j]:OFF[j + 1]], in0=z, scalar=-1.0, in1=z,
                                                   op0=ALU.mult, op1=ALU.min).then_inc(abs_ready, 1)
                    ch.link(nc.vector.tensor_scalar(pos[half][:, OFF[j]:OFF[j + 1]], z, 0.0, None, ALU.max))

                def suffix(ch, n, half, j):
                    z = H.probs[half][:, OFF[j]:OFF[j + 1]]
                    p = pos[half][:, OFF[j]:OFF[j + 1]]
                    dve.wait_ge(soft_ready, n + 1)
                    ch.link(nc.vector.tensor_tensor_scan(p[:, ::-1], p[:, ::-1], soft[half][:, OFF[j]:OFF[j + 1]][:, ::-1],
                                                         0.0, ALU.add, ALU.add))
                    nc.vector.tensor_tensor(z, z, p, ALU.subtract).then_inc(exponent_ready, 1)
                    ch.link(dve.nop())

                def rounds(now, nxt):
                    if nxt:
                        ch = Chain(dve, own, nxt[0] * links)
                    for j in range(NT):
                        if nxt:
                            logits(ch, nxt[0], nxt[1], j)
                        if now and j % 2 == 0:
                            H.copy_turned(dve, now[0], j)
                    if nxt:
                        for j in range(NT):
                            suffix(ch, nxt[0], nxt[1], j)
                        assert ch.n == links
                    if now:
                        n, half, i = now
                        dve.wait_ge(H.weighed, 4 * n + 6)
                        nc.vector.tensor_copy(B.ob[:, :, bass.ds(i * 128 + 64 * half, 64)],
                                              H.ops[half][:, 0:NT * HD].rearrange("p (t d) -> p t d", d=HD)).then_inc(H.head_out, 1)
                dve.sem_inc(H.scores_read, 4)
                dve.sem_inc(H.copied[0], 1)
                dve.sem_inc(H.head_out, 2)
                H.run(dve, 4, rounds)

            @block.scalar
            def _(act):
                def softplus(n, half):
                    x = soft[half][:, :]
                    act.wait_ge(abs_ready, 4 * n + 4)
                    ch = Chain(act, act_own, n)
                    ch.link(nc.scalar.activation(x, x, ACT.Exp))
                    nc.scalar.activation(x, x, ACT.Ln, bias=1.0).then_inc(soft_ready, 1)

                def weights(n, half, j):
                    x = H.probs[half][:, OFF[j]:OFF[j + 1]]
                    act.wait_ge(exponent_ready, 4 * n + j + 1)
                    nc.scalar.activation(x, x, ACT.Exp).then_inc(H.probs_ready, 1)

                def rounds(now, nxt):
                    for j in range(1, NT, 2):
                        if now:
                            H.copy_turned(act, now[0], j)
                    if nxt:
                        softplus(nxt[0], nxt[1])
                        for j in range(NT):
                            weights(nxt[0], nxt[1], j)
                act.sem_inc(H.copied[1], 1)
                H.run(act, 4, rounds)


def turn_tokens(nc, C, jobs, tag):
    with Scope(nc) as s:
        ps = [s.bank(f"tt_ps{i}{tag}") for i in range(4)]
        turned = s.sem(f"tt_turned{tag}")
        out = s.sems(f"tt_out{tag}", 2)
        with nc.Block() as block:
            @block.tensor
            def _(pe):
                for k, (src, _, _) in enumerate(jobs):
                    if k >= 4:
                        pe.wait_ge(out[k % 2], k // 2 - 1)
                    for t in range(NT):
                        mm = nc.tensor.transpose(ps[k % 4][:, P * t:P * t + P], src(t), C.ident[:, :])
                    mm.then_inc(turned, 1)

            @block.vector
            def _(dve):
                for k in range(0, len(jobs), 2):
                    dve.wait_ge(turned, k + 1)
                    _, dst, scale = jobs[k]
                    if scale is None:
                        ins = nc.vector.tensor_copy(dst, ps[k % 4][:, :])
                    else:
                        ins = nc.vector.tensor_scalar(dst, ps[k % 4][:, :], scale, None, ALU.mult)
                    ins.then_inc(out[0], 1)

            @block.scalar
            def _(act):
                for k in range(1, len(jobs), 2):
                    act.wait_ge(turned, k + 1)
                    _, dst, scale = jobs[k]
                    nc.scalar.activation(dst, ps[k % 4][:, :], ACT.Copy,
                                         scale=1.0 if scale is None else scale).then_inc(out[1], 1)


def mix_branches(nc, C, A, B, mixed):
    with Scope(nc) as s:
        wu = [s.sb(f"wu{i}", [P, 4, D]) for i in range(2)]
        tmp = [s.sb(f"mixt{i}", [P, 512]) for i in range(2)]
        ps = [[s.bank(f"mx{i}{b}") for b in range(2)] for i in range(2)]
        w_in = s.sems("up_in", 2)
        ready = s.sem("mx_ready")
        own = s.sem("mx_own")
        read = s.sem("mx_read")
        summed = s.sem("mx_sum")
        parts = [(t, n) for n in range(2) for t in range(NT)]
        with nc.Block() as block:
            @block.sync
            def _(sp):
                for b, n in enumerate(("w_up_nsa", "w_up_sb")):
                    sp.dma_start(wu[b][:, :, :], A[n][0].rearrange("(k p) n -> p k n", p=P)).then_inc(w_in[b], 16)

            @block.tensor
            def _(pe):
                for i, (t, n) in enumerate(parts):
                    if i >= 2:
                        pe.wait_ge(read, i - 1)
                    for b in range(2):
                        if i == 0:
                            pe.wait_ge(w_in[b], 16)
                        for k in range(4):
                            mm = nc.tensor.matmul(ps[i % 2][b][:, :], B.oT[b][:, k, P * t:P * t + P],
                                                  wu[b][:, k, 512 * n:512 * n + 512], start=(k == 0), stop=(k == 3))
                    mm.then_inc(ready, 1)

            @block.vector
            def _(dve):
                ch = Chain(dve, own)
                for i, (t, n) in enumerate(parts):
                    dve.wait_ge(ready, i + 1)
                    dst = mixed[:, t, 512 * n:512 * n + 512]
                    if i >= 2:
                        dve.wait_ge(summed, i - 1)
                    ch.link(nc.vector.tensor_tensor(dst, ps[i % 2][0][:, :], B.sig[:, t, 512 * n:512 * n + 512], ALU.mult))
                    ch.link(nc.vector.tensor_tensor(tmp[i % 2][:, :], ps[i % 2][1][:, :],
                                                    B.sig[:, t, D + 512 * n:D + 512 * n + 512], ALU.mult))
                    dve.sem_inc(read, 1)

            @block.gpsimd
            def _(pool):
                for i, (t, n) in enumerate(parts):
                    pool.wait_ge(read, i + 1)
                    dst = mixed[:, t, 512 * n:512 * n + 512]
                    pool.tensor_tensor(dst, dst, tmp[i % 2][:, :], ALU.add).then_inc(summed, 1)


def project_residual(nc, C, aT, w, gate, tag, make_modulation, after, early):
    kc = w.shape[0] // P
    slots = kc // KD
    with Scope(nc) as s:
        wbuf = [s.sb(f"rw{i}{tag}", [P, KD, 512]) for i in range(2)]
        tmp = [s.sb(f"rt{i}{tag}", [P, 512]) for i in range(2)]
        banks = [s.bank(f"rp{b}{tag}") for b in range(6)]
        mod = make_modulation(s)
        units = len(mod.units)
        landed = s.sems(f"r_landed{tag}", 2)
        used = s.sem(f"r_used{tag}")
        ready = s.sem(f"r_ready{tag}")
        scaled = s.sem(f"r_scaled{tag}")
        added = s.sem(f"r_added{tag}")
        with nc.Block() as block:
            @block.sync
            def _(sp):
                for i in range(2 * slots):
                    if i >= 2:
                        sp.wait_ge(used, i - 1)
                    n, q = i // slots, i % slots
                    sp.dma_start(wbuf[i % 2][:, :, :], chunk(w[q * D:(q + 1) * D, :], 512 * n, 512)).then_inc(landed[i % 2], 16)

            @block.scalar
            def _(act):
                mod.load(act)

            @block.tensor
            def _(pe):
                unit = 0
                for i in range(2 * slots):
                    n, q = i // slots, i % slots
                    pe.wait_ge(landed[i % 2], 16 * (i // 2 + 1))
                    for t in range(NT):
                        b = NT * n + t
                        if b >= 6 and q == 0:
                            pe.wait_ge(scaled, b - 5)
                        for k in range(KD):
                            first, last = (q == 0 and k == 0), (q == slots - 1 and k == KD - 1)
                            mm = nc.tensor.matmul(banks[b % 6][:, :], aT[:, KD * q + k, P * t:P * t + P], wbuf[i % 2][:, k, :],
                                                  start=first, stop=last)
                        if q == slots - 1 and t < NT - 1:
                            mm.then_inc(ready, 1)
                        if t == NT - 1:
                            mm.then_inc(used, 1)
                        while unit < units and after(unit) == NT * i + t:
                            mod.spread(pe, unit)
                            unit += 1
                for u in range(unit, units):
                    mod.spread(pe, u)

            @block.vector
            def _(dve):
                def take(n):
                    for t in range(NT):
                        i = NT * n + t
                        if t < NT - 1:
                            dve.wait_ge(ready, (NT - 1) * n + t + 1)
                        else:
                            dve.wait_ge(used, slots * (n + 1))
                        if i >= 2:
                            dve.wait_ge(added, i - 1)
                        nc.vector.tensor_tensor(tmp[i % 2][:, :], banks[i % 6][:, :], gate[:, 512 * n:512 * n + 512],
                                                ALU.mult).then_inc(scaled, 1)
                mod.sum(dve, 0)
                for u in range(units):
                    if u == early:
                        take(0)
                    if u + 1 < units:
                        mod.sum(dve, u + 1)
                    mod.finish(dve, u)
                take(1)

            @block.gpsimd
            def _(pool):
                for i in range(2 * NT):
                    n, t = i // NT, i % NT
                    pool.wait_ge(scaled, i + 1)
                    dst = C.h[:, t, 512 * n:512 * n + 512]
                    pool.tensor_tensor(dst, dst, tmp[i % 2][:, :], ALU.add).then_inc(added, 1)


def gate_rows(nc, C, A, G):
    with Scope(nc) as s:
        rows = {n: s.sb(f"gr_{n}", [4, TOK]) for n in ("i", "f", "low", "soft", "F", "a", "top", "m")}
        bias = s.sb("gbias_if", [4, 2])
        zero = s.sb("gr_zero", [4, TOK])
        rps = [s.bank(f"gr_ps{i}") for i in range(2)]
        tps = [s.bank(f"gr_t{i}") for i in range(2)]
        aps = [s.bank(f"gr_a{i}") for i in range(4)]
        bias_in = s.sem("gr_bias_in")
        zeroed = s.sem("gr_zeroed")
        rows_ready = s.sem("gr_rows")
        abs_ready = s.sem("gr_abs")
        act_own = s.sem("gr_act_own")
        soft_ready = s.sem("gr_soft")
        own = s.sem("gr_own")
        scanned = s.sem("gr_scanned")
        cols_ready = s.sem("gr_cols")
        spread = s.sem("gr_spread")
        m_ready = s.sem("gr_m")
        with nc.Block() as block:
            @block.sync
            def _(sp):
                b = A["b_gates_2"][0]
                sp.dma_start(bias[:, 0:1], b[0:4].rearrange("(n a) -> n a", a=1)).then_inc(bias_in, 16)
                sp.dma_start(bias[:, 1:2], b[4:8].rearrange("(n a) -> n a", a=1)).then_inc(bias_in, 16)

            @block.gpsimd
            def _(pool):
                pool.memset(zero[:, :], 0.0).then_inc(zeroed, 1)

            @block.tensor
            def _(pe):
                for g in range(2):
                    for t in range(NT):
                        mm = nc.tensor.transpose(rps[g][0:4, P * t:P * t + P], G.gt[:, t, 4 * g:4 * g + 4], C.ident[:, :])
                    mm.then_inc(rows_ready, 1)
                pe.wait_ge(scanned, 2)
                for g, n in enumerate(("top", "m")):
                    for t in range(NT):
                        mm = nc.tensor.transpose(tps[g][:, 4 * t:4 * t + 4], rows[n][:, P * t:P * t + P], C.ident[0:4, 0:4])
                    mm.then_inc(cols_ready, 1)
                for h in range(4):
                    one = C.ident[0:4, h:h + 1]
                    pick = bass.AP(tensor=one.tensor, offset=one.offset, ap=[one.ap[0], [0, P]])
                    nc.tensor.matmul(aps[h][:, :], pick, rows["a"][:, :], start=True, stop=True).then_inc(spread, 1)

            @block.scalar
            def _(act):
                act.wait_ge(abs_ready, 1)
                ch = Chain(act, act_own)
                ch.link(nc.scalar.activation(rows["soft"][:, :], rows["soft"][:, :], ACT.Exp))
                nc.scalar.activation(rows["soft"][:, :], rows["soft"][:, :], ACT.Ln, bias=1.0).then_inc(soft_ready, 1)
                act.wait_ge(m_ready, 1)
                nc.scalar.activation(G.em[:, :], G.em[:, :], ACT.Exp, scale=-1.0)
                for h in range(4):
                    act.wait_ge(spread, h + 1)
                    nc.scalar.activation(G.a[h][:, :], aps[h][:, :], ACT.Copy)

            @block.vector
            def _(dve):
                ch = Chain(dve, own)
                dve.wait_ge(bias_in, 32)
                dve.wait_ge(rows_ready, 2)
                ch.link(nc.vector.tensor_scalar(rows["i"][:, :], rps[0][0:4, :], bias[:, 0:1], None, ALU.add))
                ch.link(nc.vector.tensor_scalar(rows["f"][:, :], rps[1][0:4, :], bias[:, 1:2], None, ALU.add))
                nc.vector.scalar_tensor_tensor(out=rows["soft"][:, :], in0=rows["f"][:, :], scalar=-1.0, in1=rows["f"][:, :],
                                               op0=ALU.mult, op1=ALU.min).then_inc(abs_ready, 1)
                ch.link(nc.vector.tensor_scalar(rows["low"][:, :], rows["f"][:, :], 0.0, None, ALU.min))
                dve.wait_ge(soft_ready, 1)
                ch.link(nc.vector.tensor_tensor_scan(rows["F"][:, :], rows["low"][:, :], rows["soft"][:, :], 0.0,
                                                     ALU.add, ALU.subtract))
                ch.link(nc.vector.tensor_tensor(rows["a"][:, :], rows["i"][:, :], rows["F"][:, :], ALU.subtract))
                dve.wait_ge(zeroed, 1)
                nc.vector.tensor_tensor_scan(rows["top"][:, :], rows["a"][:, :], zero[:, :], 0.0,
                                             ALU.max, ALU.max).then_inc(scanned, 1)
                dve.wait_ge(scanned, 1)
                nc.vector.tensor_tensor(rows["m"][:, :], rows["F"][:, :], rows["top"][:, :], ALU.add).then_inc(scanned, 1)
                dve.wait_ge(cols_ready, 2)
                nc.vector.tensor_scalar(G.negtop[:, :], tps[0][:, 0:16], -1.0, None, ALU.mult)
                nc.vector.tensor_copy(G.em[:, :], tps[1][:, 0:16]).then_inc(m_ready, 1)


def convolve(nc, C, G):
    with Scope(nc) as s:
        sg = [s.sb(f"cv_s{i}", [P, TOK]) for i in range(2)]
        own = s.sem("cv_own")
        summed = s.sem("cv_sum")
        sig_ready = s.sem("cv_sig")
        out = s.sem("cv_out")
        with nc.Block() as block:
            @block.vector
            def _(dve):
                ch = Chain(dve, own)

                def taps(g):
                    dst = G.qk[:, g, :]
                    ch.link(nc.vector.tensor_scalar(dst, G.raw[:, g, 0:TOK], C.cols2[:, 72 + g:73 + g],
                                                    C.cols2[:, 104 + g:105 + g], ALU.mult, ALU.add))
                    for j in range(1, 4):
                        w = C.cols2[:, 72 + 8 * j + g:73 + 8 * j + g]
                        ch.link(nc.vector.scalar_tensor_tensor(out=dst, in0=G.raw[:, g, j:j + TOK], scalar=w, in1=dst,
                                                               op0=ALU.mult, op1=ALU.add))
                    dve.sem_inc(summed, 1)
                taps(0)
                for g in range(KD):
                    if g + 1 < KD:
                        taps(g + 1)
                    dve.wait_ge(sig_ready, g + 1)
                    nc.vector.scalar_tensor_tensor(out=G.qk[:, g, :], in0=G.qk[:, g, :], scalar=(P ** -0.5 if g < 4 else 1.0),
                                                   in1=sg[g % 2][:, :], op0=ALU.mult, op1=ALU.mult).then_inc(out, 1)

            @block.scalar
            def _(act):
                for g in range(KD):
                    act.wait_ge(summed, g + 1)
                    if g >= 2:
                        act.wait_ge(out, g - 1)
                    nc.scalar.activation(sg[g % 2][:, :], G.qk[:, g, :], ACT.Sigmoid).then_inc(sig_ready, 1)


def mlstm(nc, C, G, hm):
    with Scope(nc) as s:
        qst = [s.sb(f"ml_q{i}", [P, 512]) for i in range(2)]
        H = Heads(s, nc, "ml", qst, dv=P)
        decay = [s.sb(f"decay{i}", [P, OFF[NT]]) for i in range(2)]
        den = [s.sb(f"den{i}", [P, NT]) for i in range(2)]
        exponent_ready = s.sem("ml_exponent")
        decay_ready = s.sem("ml_decay")
        own = s.sem("ml_own")
        H.probs_ready, H.probs_begin = H.scores_read, 4
        links = 4
        with nc.Block() as block:
            @block.tensor
            def _(pe):
                H.pe(pe, C, 2, lambda half, i, w: G.qk[:, 4 + 2 * i + half, 0:w],
                     lambda b, half, i: G.vm[:, b, P * (2 * i + half):P * (2 * i + half) + P])

            @block.gpsimd
            def _(pool):
                for i in range(2):
                    if i:
                        pool.wait_ge(H.scores_ready, 8 * i)
                    pool.tensor_copy(qst[0][:, :], G.qk[:, 2 * i, :])
                    pool.tensor_copy(qst[1][:, :], G.qk[:, 2 * i + 1, :]).then_inc(H.q_staged, 1)

            @block.vector
            def _(dve):
                def exponents(n, half, j):
                    w = P * (j + 1)
                    if n >= 2:
                        dve.wait_ge(H.scores_read, 4 * (n - 2) + j + 5)
                    nc.vector.scalar_tensor_tensor(out=decay[half][:, OFF[j]:OFF[j + 1]], in0=G.a[n][:, 0:w],
                                                   scalar=G.negtop[:, 4 * j + n:4 * j + n + 1],
                                                   in1=C.allow[:, P * (NT - 1 - j):512],
                                                   op0=ALU.add, op1=ALU.min).then_inc(exponent_ready, 1)

                def logits(n, half, j):
                    if j == 0:
                        dve.wait_ge(H.turned, 4 * n + 4)
                    dve.wait_ge(H.scores_ready, 4 * n + j + 1)
                    dve.wait_ge(decay_ready, 4 * n + j + 1)
                    nc.vector.tensor_tensor_reduce(H.probs[half][:, OFF[j]:OFF[j + 1]], H.sps[j][:, 0:P * (j + 1)],
                                                   decay[half][:, OFF[j]:OFF[j + 1]], 1.0, 0.0, ALU.mult, ALU.add,
                                                   den[half][:, j:j + 1]).then_inc(H.scores_read, 1)

                def rounds(now, nxt):
                    if nxt:
                        for j in range(NT):
                            exponents(nxt[0], nxt[1], j)
                    for j in range(NT):
                        if now and j % 2 == 0:
                            H.copy_turned(dve, now[0], j)
                        if nxt:
                            logits(nxt[0], nxt[1], j)
                    if now:
                        n, half, i = now
                        d = den[half][:, :]
                        ch = Chain(dve, own, n * links)
                        dve.wait_ge(H.weighed, 4 * n + 6)
                        ch.link(nc.vector.scalar_tensor_tensor(out=d, in0=d, scalar=-1.0, in1=d, op0=ALU.mult, op1=ALU.max))
                        ch.link(nc.vector.tensor_tensor(d, d, G.em[:, n:16:4], ALU.max))
                        ch.link(nc.vector.reciprocal(d, d))
                        ch.link(nc.vector.tensor_tensor(hm[:, :, P * n:P * n + P],
                                                        H.ops[half][:, :].rearrange("p (t d) -> p t d", d=P), bcast(d, P), ALU.mult))
                        dve.sem_inc(H.head_out, 1)
                dve.sem_inc(H.scores_read, 4)
                dve.sem_inc(H.copied[0], 1)
                dve.sem_inc(H.head_out, 2)
                H.run(dve, 2, rounds)

            @block.scalar
            def _(act):
                def rounds(now, nxt):
                    for j in range(NT):
                        if nxt:
                            n, half, _ = nxt
                            x = decay[half][:, OFF[j]:OFF[j + 1]]
                            act.wait_ge(exponent_ready, 4 * n + j + 1)
                            nc.scalar.activation(x, x, ACT.Exp).then_inc(decay_ready, 1)
                        if now and j % 2:
                            H.copy_turned(act, now[0], j)
                act.sem_inc(H.copied[1], 1)
                H.run(act, 2, rounds)


def norm_heads_gate(nc, C, hm, so):
    with Scope(nc) as s:
        sq = s.sb("nh_sq", [P, NT * 512])
        ss = s.sb("nh_ss", [P, 16])
        rs = s.sb("nh_rs", [P, 16])
        own = s.sem("nh_own")
        var_ready = s.sem("nh_var")
        rs_ready = s.sem("nh_rs")
        with nc.Block() as block:
            @block.vector
            def _(dve):
                ch = Chain(dve, own)
                x = hm[:, :, :].rearrange("p t n -> p (t n)")
                x3 = x.rearrange("p (h d) -> p h d", d=P)
                ch.link(nc.vector.tensor_tensor(sq[:, :], x, x, ALU.mult))
                ch.link(nc.vector.tensor_reduce(ss[:, :], sq[:, :].rearrange("p (h d) -> p h d", d=P), AX.X, ALU.add))
                nc.vector.tensor_scalar(ss[:, :], ss[:, :], 1.0 / P, EPS, ALU.mult, ALU.add).then_inc(var_ready, 1)
                ch.link(nc.vector.tensor_tensor(x, x, so[:, :, :].rearrange("p t n -> p (t n)"), ALU.mult))
                dve.wait_ge(rs_ready, 1)
                ch.link(nc.vector.tensor_tensor(x3, x3, bcast(rs[:, :], P), ALU.mult))

            @block.gpsimd
            def _(pool):
                pool.wait_ge(var_ready, 1)
                pool.tensor_tensor(rs[:, :], ss[:, :], C.neghalf[:, 0:16], ALU.pow).then_inc(rs_ready, 1)


def route(nc, C, A, uT, R):
    with Scope(nc) as s:
        wr = s.sb("wr", [P, KD, 36])
        rb = s.sb("rb", [P, 36])
        L = s.sb("rl", [P, NT, 40])
        top = s.sb("rtop", [P, NT, 8])
        idx = s.sb("ridx", [P, NT, 8], U32)
        gi = s.sb("rgi", [P, NT])
        ex = s.sb("rex", [P, NT, 4])
        gsum = s.sb("rgsum", [P, NT])
        ngm = s.sb("rngm", [P, NT])
        gid = s.sb("gid", [P, EXPERTS])
        pen = s.sb("pen", [P, NT, EXPERTS])
        top2 = s.sb("rtop2", [P, NT, 8])
        idx2 = s.sb("ridx2", [P, NT, 8], U32)
        e = s.sb("re", [P, NT, 2])
        d = s.sb("rd", [P, NT, 1])
        oh = [s.sb(f"roh{i}", [P, NT, EXPERTS]) for i in range(2)]
        both = s.sb("rboth", [P, NT, EXPERTS])
        junk = s.sb("rjunk", [P, 2 * NT, EXPERTS])
        cnt = s.sb("rcnt", [P, EXPERTS])
        pmax = s.sb("rpmax", [1, LEVELS, PAIRS])
        ohs = s.sb("rohs", [P, 2, 8, P])
        row = s.sb("rrow", [P, NT, 2])
        kk = s.sb("rkk", [P, NT, 2])
        tf = s.sb("rtf", [P, PAIRS])
        te = s.sb("rte", [P, PAIRS])
        lps = [s.bank(f"r_l{t}") for t in range(NT)]
        kps = s.bank("r_rank")
        cps = s.bank("r_cnt")
        xps = s.bank("r_idx")
        w_in = s.sem("r_w_in")
        fill = s.sem("r_fill")
        logits = s.sem("r_logits")
        own = s.sem("r_own")
        ng_ready = s.sem("r_ng")
        exps = s.sem("r_exps")
        dd_ready = s.sem("r_dd")
        exp2 = s.sem("r_exp2")
        oh_ready = s.sem("r_oh")
        ranks = s.sem("r_ranks")
        slots_ready = s.sem("r_slots")
        table = s.sem("r_table")
        with nc.Block() as block:
            @block.sync
            def _(sp):
                sp.dma_start(wr[:, :, 0:4], A["w_router_group_2"][0].rearrange("(k p) n -> p k n", p=P)).then_inc(w_in, 16)
                sp.dma_start(wr[:, :, 4:36], A["w_router_expert_2"][0].rearrange("(k p) n -> p k n", p=P)).then_inc(w_in, 16)
                sp.dma_start(rb[:, 0:4], rows_to_all(A["b_router_group_2"][0], 4)).then_inc(w_in, 16)
                sp.dma_start(rb[:, 4:36], rows_to_all(A["b_router_expert_2"][0], EXPERTS)).then_inc(w_in, 16)

            @block.gpsimd
            def _(pool):
                ch = Chain(pool, fill)
                ok = dict(allow_small_or_imprecise_dtypes=True)
                ch.link(pool.memset(L[:, :, :], -3e38))
                ch.link(pool.iota(gid[:, :], pattern=[[1, 4], [0, 8]], base=0, channel_multiplier=0, **ok))
                ch.link(pool.iota(R.eid[:, :], pattern=[[1, P]], base=0, channel_multiplier=0, **ok))
                ch.link(pool.iota(R.aid[:, :, :], pattern=[[TOK, 2], [P, NT]], base=1, channel_multiplier=1, **ok))
                ch.link(pool.iota(R.spare[:, :], pattern=[[1, 1]], base=2 * TOK, channel_multiplier=1, **ok))

            @block.tensor
            def _(pe):
                pe.wait_ge(w_in, 64)
                for t in range(NT):
                    for k in range(KD):
                        mm = nc.tensor.matmul(lps[t][:, 0:36], uT[:, k, P * t:P * t + P], wr[:, k, :],
                                              start=(k == 0), stop=(k == KD - 1))
                    mm.then_inc(logits, 1)
                pe.wait_ge(oh_ready, 1)
                for t in range(NT):
                    for u in range(t + 1):
                        nc.tensor.matmul(kps[:, EXPERTS * t:EXPERTS * (t + 1)], C.ones[:, :] if u < t else C.later[:, :],
                                         both[:, u, :], start=(u == 0), stop=(u == t))
                for u in range(NT):
                    mm = nc.tensor.matmul(cps[:, 0:EXPERTS], C.ones[:, :], both[:, u, :], start=(u == 0), stop=(u == NT - 1))
                mm.then_inc(ranks, 1)
                for m in range(2):
                    pe.wait_ge(slots_ready, m + 1)
                    for q in range(8):
                        mm = nc.tensor.matmul(xps[:, PAIRS * m:PAIRS * (m + 1)], ohs[:, m, q, :], R.ptok[:, q, :],
                                              start=(q == 0), stop=(q == 7))
                    mm.then_inc(table, 1)

            @block.scalar
            def _(act):
                act.wait_ge(ng_ready, 1)
                for t in range(NT):
                    ins = nc.scalar.activation(ex[:, t, :], L[:, t, 0:4], ACT.Exp, bias=ngm[:, t:t + 1],
                                               accum_out=gsum[:, t:t + 1])
                ins.then_inc(exps, 1)
                act.wait_ge(dd_ready, 1)
                nc.scalar.activation(R.w[:, :, 1:2], d[:, :, :], ACT.Exp).then_inc(exp2, 1)

            @block.vector
            def _(dve):
                ch = Chain(dve, own)
                v = nc.vector

                def for_all(make, over):
                    for x in over:
                        ins = make(*x)
                    ch.link(ins)
                tiles = [(t,) for t in range(NT)]
                both_of = [(t, j) for t in range(NT) for j in range(2)]
                dve.wait_ge(fill, 5)
                for t in range(NT):
                    dve.wait_ge(logits, t + 1)
                    v.tensor_tensor(L[:, t, 0:4], lps[t][:, 0:4], rb[:, 0:4], ALU.add)
                    ins = v.tensor_tensor(L[:, t, 8:40], lps[t][:, 4:36], rb[:, 4:36], ALU.add)
                ch.link(ins)
                for_all(lambda t: v.max(top[:, t, :], L[:, t, 0:8]), tiles)
                v.tensor_scalar(ngm[:, :], top[:, :, 0], -1.0, None, ALU.mult).then_inc(ng_ready, 1)
                for_all(lambda t: v.max_index(idx[:, t, :], top[:, t, :], L[:, t, 0:8]), tiles)
                ch.link(v.tensor_copy(gi[:, :], idx[:, :, 0]))
                for_all(lambda t: v.tensor_scalar(pen[:, t, :], gid[:, :], gi[:, t:t + 1], 1.0, ALU.is_equal, ALU.subtract), tiles)
                for_all(lambda t: v.scalar_tensor_tensor(out=pen[:, t, :], in0=pen[:, t, :], scalar=3e38, in1=L[:, t, 8:40],
                                                         op0=ALU.mult, op1=ALU.add), tiles)
                for_all(lambda t: v.max(top2[:, t, :], pen[:, t, :]), tiles)
                v.tensor_tensor(d[:, :, :], top2[:, :, 1:2], top2[:, :, 0:1], ALU.subtract).then_inc(dd_ready, 1)
                for_all(lambda t: v.max_index(idx2[:, t, :], top2[:, t, :], pen[:, t, :]), tiles)
                ch.link(v.tensor_copy(e[:, :, :], idx2[:, :, 0:2]))
                for_all(lambda t, j: v.tensor_scalar(oh[j][:, t, :], R.eid[:, 0:EXPERTS], e[:, t, j:j + 1], None, ALU.is_equal),
                        both_of)
                v.tensor_tensor(both[:, :, :], oh[0][:, :, :], oh[1][:, :, :], ALU.add).then_inc(oh_ready, 1)
                dve.wait_ge(exps, 1)
                dve.wait_ge(exp2, 1)
                ch.link(v.reciprocal(gsum[:, :], gsum[:, :]))
                w0, w1 = R.w[:, :, 0], R.w[:, :, 1]
                ch.link(v.tensor_scalar(w0, w1, 1.0, None, ALU.add))
                ch.link(v.reciprocal(w0, w0))
                ch.link(v.tensor_tensor(w0, w0, gsum[:, :], ALU.mult))
                ch.link(v.tensor_tensor(w1, w1, w0, ALU.mult))
                dve.wait_ge(ranks, 1)
                for_all(lambda t, j: v.tensor_tensor_reduce(junk[:, 2 * t + j, :], oh[j][:, t, :],
                                                            kps[:, EXPERTS * t:EXPERTS * (t + 1)], 1.0, 0.0, ALU.mult, ALU.add,
                                                            R.rank[:, t, j:j + 1]), both_of)
                ch.link(v.tensor_scalar(R.level[:, :, :], R.rank[:, :, :], float(CAP), None, ALU.is_ge))
                for m in range(2, LEVELS):
                    ch.link(v.scalar_tensor_tensor(out=R.level[:, :, :], in0=R.rank[:, :, :], scalar=float(CAP * m),
                                                   in1=R.level[:, :, :], op0=ALU.is_ge, op1=ALU.add))
                ch.link(v.scalar_tensor_tensor(out=row[:, :, :], in0=e[:, :, :], scalar=float(CAP), in1=R.rank[:, :, :],
                                               op0=ALU.mult, op1=ALU.add))
                ch.link(v.tensor_scalar(R.pair[:, :, :], e[:, :, :], 2.0, None, ALU.is_ge))
                for m in range(2, PAIRS):
                    ch.link(v.scalar_tensor_tensor(out=R.pair[:, :, :], in0=e[:, :, :], scalar=2.0 * m,
                                                   in1=R.pair[:, :, :], op0=ALU.is_ge, op1=ALU.add))
                ch.link(v.scalar_tensor_tensor(out=kk[:, :, :], in0=R.level[:, :, :], scalar=-float(CAP),
                                               in1=row[:, :, :], op0=ALU.mult, op1=ALU.add))
                ch.link(v.scalar_tensor_tensor(out=R.place[:, :, :], in0=R.pair[:, :, :], scalar=-2.0 * CAP,
                                               in1=kk[:, :, :], op0=ALU.mult, op1=ALU.add))
                for_all(lambda t, j: v.tensor_scalar(R.ptok[:, 2 * t + j, :], R.eid[:, 0:PAIRS], R.pair[:, t, j:j + 1],
                                                     R.aid[:, j, t:t + 1], ALU.is_equal, ALU.mult), both_of)
                for m in range(2):
                    place_onehots(v, ch, R, kk[:, :, :], ohs[:, m, :, :], float(m))
                    dve.sem_inc(slots_ready, 1)
                for m in range(2):
                    dve.wait_ge(table, 2)
                    fill_table(v, ch, R, xps[:, PAIRS * m:PAIRS * (m + 1)], m, tf[:, :], te[:, :])
                ch.link(v.tensor_copy(cnt[:, :], cps[:, 0:EXPERTS]))
                for m in range(LEVELS):
                    ch.link(v.tensor_reduce(pmax[:, m, :], cnt[0:1, :].rearrange("p (q f) -> p q f", f=2), AX.X, ALU.max))
                    ch.link(v.tensor_scalar(pmax[:, m, :], pmax[:, m, :], float(-CAP * m), None, ALU.add))
                v.tensor_copy(R.over[:, 0:LEVELS * PAIRS], pmax[:, :, :].rearrange("p m q -> p (m q)"))
                ch.link(v.tensor_reduce(R.most[:, :], pmax[:, :, :], AX.X, ALU.max))


class Experts:

    def __init__(self, s, nc, C, A, M, R, xn, y, tag):
        self.nc, self.C, self.A, self.M, self.R, self.xn, self.y, self.tag = nc, C, A, M, R, xn, y, tag
        self.w = [s.sb(f"x_w{i}{tag}", [P, KD, DE]) for i in range(6)]
        self.landed = s.sems(f"x_landed{tag}", 6)

    def open(self, s):
        tag = self.tag
        sb, sem = (lambda n, sh, dt=F32: s.sb(f"{n}{tag}", sh, dt)), (lambda n: s.sem(f"{n}{tag}"))
        self.ids = sb("x_ids", [P, 1], U32)
        self.to = sb("x_to", [P, 1], U32)
        self.xg = sb("x_g", [P, D])
        self.xT = sb("x_T", [P, KD, P])
        self.act = sb("x_act", [P, DE])
        self.sig = sb("x_sig", [P, DE])
        self.aT = sb("x_aT", [P, 4, P])
        self.out = sb("x_out", [P, D])
        self.tps = [s.bank(f"x_t{i}{tag}") for i in range(2)]
        self.gps = s.bank(f"x_gp{tag}")
        self.ups = s.bank(f"x_up{tag}")
        self.aps = s.bank(f"x_ap{tag}")
        self.yps = [s.bank(f"x_y{i}{tag}") for i in range(2)]
        self.ids_ready = sem("x_ids_ready")
        self.to_ready = sem("x_to_ready")
        self.out_free = sem("x_out_free")
        self.asked = sem("x_asked")
        self.gathered = sem("x_gathered")
        self.turned = sem("x_turned")
        self.modulated = [sem("x_mod_dve"), sem("x_mod_act")]
        self.gate_ready = sem("x_gate")
        self.up_ready = sem("x_up_s")
        self.sig_ready = sem("x_sig_s")
        self.act_ready = sem("x_act_s")
        self.act_turned = sem("x_act_turned")
        self.act_copied = sem("x_act_copied")
        self.down_ready = sem("x_down")
        self.out_ready = [sem("x_out_dve"), sem("x_out_act")]
        self.stored = sem("x_stored")
        self.own = sem("x_own")

    def begin(self, pool):
        for sem, n in ([(x, 16) for x in self.landed] + [(self.turned, 2), (self.own, 2)]
                       + [(x, 4) for x in self.modulated]
                       + [(x, 1) for x in (self.ids_ready, self.to_ready, self.gate_ready, self.up_ready, self.sig_ready,
                                           self.act_ready, self.act_turned, self.out_free, self.act_copied, self.down_ready,
                                           *self.out_ready)]):
            pool.sem_inc(sem, n)

    def load(self, sp, done, q):
        free = (self.gate_ready, self.up_ready, self.down_ready) if done is not None else None
        names = ("w_expert_gate_2", "w_expert_up_2", "w_expert_down_2")
        for m in range(6):
            if free:
                sp.wait_ge(free[m // 2], done)
            w = self.A[names[m // 2]][0][bass.ds(q * 2 + m % 2, 1)]
            if m < 4:
                dst, src = self.w[m][:, :, :], w.rearrange("a (k p) n -> p (a k) n", p=P)
            else:
                dst = self.w[m][:, :, :].rearrange("p (k f) n -> p k (f n)", k=4)
                src = w.rearrange("a (k p) n -> p (a k) n", p=P)
            sp.dma_start(dst, src).then_inc(self.landed[m], 16)

    def gather(self, pool, i, col):
        pool.wait_ge(self.turned, 2 * i)
        pool.sem_inc(self.asked, 1)
        pool.tensor_copy(self.ids[:, :], self.R.tokens[:, bass.ds(col, 1)]).then_inc(self.ids_ready, 1)
        pool.wait_ge(self.ids_ready, i + 1)
        pool.sem_inc(self.asked, 1)
        pool.indirect_dma_start(out=self.xg[:, :], out_offset=None, in_=self.xn,
                                in_offset=bass.IndirectOffsetOnAxis(ap=self.ids[:, 0:1], axis=0)).then_inc(self.gathered, 16)

    def aim(self, pool, col):
        pool.tensor_copy(self.to[:, :], self.R.rows[:, bass.ds(col, 1)]).then_inc(self.to_ready, 1)

    def scatter(self, pool, i):
        pool.wait_ge(self.to_ready, i + 1)
        for f in range(2):
            pool.wait_ge(self.out_ready[f], i + 1)
        pool.sem_inc(self.asked, 1)
        pool.indirect_dma_start(out=self.y, out_offset=bass.IndirectOffsetOnAxis(ap=self.to[:, 0:1], axis=0),
                                in_=self.out[:, :], in_offset=None).then_inc(self.stored, 16)
        pool.wait_ge(self.stored, 16 * i)
        pool.sem_inc(self.out_free, 1)

    def pe(self, pe, i, pair):
        nc, C = self.nc, self.C
        pe.wait_ge(self.gathered, 16 * i)
        for b in range(2):
            for k in range(4):
                mm = nc.tensor.transpose(self.tps[b][:, P * k:P * k + P], self.xg[:, P * (4 * b + k):P * (4 * b + k) + P],
                                         C.ident[:, :])
            mm.then_inc(self.turned, 1)
        for m, ps, ready in ((0, self.gps, self.gate_ready), (2, self.ups, self.up_ready)):
            if m == 0:
                for b in range(2):
                    pe.wait_ge(self.modulated[b], 4 * i + 4)
            pe.wait_ge(self.act_ready, i)
            for f in range(2):
                pe.wait_ge(self.landed[m + f], 16 * pair + 16)
            for k in range(KD):
                for f in range(2):
                    mm = nc.tensor.matmul(ps[CAP * f:CAP * f + CAP, :], self.xT[:, k, CAP * f:CAP * f + CAP], self.w[m + f][:, k, :],
                                          start=(k == 0), stop=(k == KD - 1))
            mm.then_inc(ready, 1)
        pe.wait_ge(self.act_ready, i + 1)
        for k in range(4):
            mm = nc.tensor.transpose(self.aps[:, P * k:P * k + P], self.act[:, P * k:P * k + P], C.ident[:, :])
        mm.then_inc(self.act_turned, 1)
        pe.wait_ge(self.act_copied, i + 1)
        for f in range(2):
            pe.wait_ge(self.landed[4 + f], 16 * pair + 16)
            pe.wait_ge(self.out_ready[f], i)
        for n in range(2):
            for k in range(4):
                for f in range(2):
                    w = self.w[4 + f][:, 2 * k + n, :]
                    mm = nc.tensor.matmul(self.yps[n][CAP * f:CAP * f + CAP, :], self.aT[:, k, CAP * f:CAP * f + CAP], w,
                                          start=(k == 0), stop=(k == 3))
        mm.then_inc(self.down_ready, 1)

    def dve(self, dve, i):
        nc, M = self.nc, self.M
        ch = Chain(dve, self.own, i * 2)
        dve.wait_ge(self.turned, 2 * i + 1)
        dve.wait_ge(self.up_ready, i)
        for k in range(4):
            nc.vector.tensor_scalar(self.xT[:, k, :], self.tps[0][:, P * k:P * k + P], M.scale[1][:, k:k + 1],
                                    M.shift[1][:, k:k + 1], ALU.mult, ALU.add).then_inc(self.modulated[0], 1)
        dve.wait_ge(self.sig_ready, i + 1)
        ch.link(nc.vector.tensor_tensor(self.sig[:, :], self.sig[:, :], self.gps[:, :], ALU.mult))
        dve.wait_ge(self.act_turned, i)
        dve.wait_ge(self.up_ready, i + 1)
        ch.link(nc.vector.tensor_tensor(self.act[:, :], self.sig[:, :], self.ups[:, :], ALU.mult))
        dve.sem_inc(self.act_ready, 1)
        dve.wait_ge(self.down_ready, i + 1)
        dve.wait_ge(self.out_free, i)
        nc.vector.tensor_copy(self.out[:, 0:512], self.yps[0][:, :]).then_inc(self.out_ready[0], 1)

    def scalar(self, act, i):
        nc, M = self.nc, self.M
        act.wait_ge(self.turned, 2 * i + 2)
        act.wait_ge(self.up_ready, i)
        for k in range(4, 8):
            nc.scalar.activation(self.xT[:, k, :], self.tps[1][:, P * (k - 4):P * (k - 4) + P], ACT.Identity,
                                 scale=M.scale[1][:, k:k + 1], bias=M.shift[1][:, k:k + 1]).then_inc(self.modulated[1], 1)
        act.wait_ge(self.gate_ready, i + 1)
        act.wait_ge(self.act_ready, i)
        nc.scalar.activation(self.sig[:, :], self.gps[:, :], ACT.Sigmoid).then_inc(self.sig_ready, 1)
        act.wait_ge(self.act_turned, i + 1)
        nc.scalar.activation(self.aT[:, :, :].rearrange("p k n -> p (k n)"), self.aps[:, :], ACT.Copy).then_inc(self.act_copied, 1)
        act.wait_ge(self.down_ready, i + 1)
        act.wait_ge(self.out_free, i)
        nc.scalar.activation(self.out[:, 512:D], self.yps[1][:, :], ACT.Copy).then_inc(self.out_ready[1], 1)


def first_places(nc, X, R):
    with Scope(nc) as s:
        X.open(s)

        def count(eng, tag):
            ran = eng.alloc_register(f"ran_{tag}")
            eng.reg_mov(ran, 1)
            return ran

        def on_both(eng, ran, q, round_):
            round_(eng.snap(ran), q)
            eng.reg_add(ran, ran, 1)
            on_next(eng, ran, q, round_)

        def on_next(eng, ran, q, round_):
            over = eng.value_load(R.over[0:1, bass.ds(q + PAIRS, 1)])
            with eng.If(over > 0):
                round_(eng.snap(ran), q + PAIRS)
                eng.reg_add(ran, ran, 1)

        with nc.Block() as block:
            @block.sync
            def _(sp):
                ran = count(sp, "load")
                on_both(sp, ran, 0, lambda i, col: None)
                with sp.Fori(1, PAIRS) as q:
                    X.load(sp, sp.snap(ran), q)
                    on_both(sp, ran, q, lambda i, col: None)

            @block.gpsimd
            def _(pool):
                def move(i, col):
                    X.gather(pool, i, col)
                    X.scatter(pool, i - 1)
                    X.aim(pool, col)
                X.begin(pool)
                ran = count(pool, "move")
                X.gather(pool, 1, 0)
                X.aim(pool, 0)
                pool.reg_add(ran, ran, 1)
                on_next(pool, ran, 0, move)
                with pool.Fori(1, PAIRS) as q:
                    on_both(pool, ran, q, move)
                X.scatter(pool, pool.snap(ran) - 1)

            @block.tensor
            def _(pe):
                ran = count(pe, "multiply")
                with pe.Fori(0, PAIRS) as q:
                    on_both(pe, ran, q, lambda i, col: X.pe(pe, i, q + 1))

            @block.vector
            def _(dve):
                ran = count(dve, "vector")
                with dve.Fori(0, PAIRS) as q:
                    on_both(dve, ran, q, lambda i, col: X.dve(dve, i))

            @block.scalar
            def _(act):
                ran = count(act, "scalar")
                with act.Fori(0, PAIRS) as q:
                    on_both(act, ran, q, lambda i, col: X.scalar(act, i))


def fill_table(v, ch, R, ps, level, f, e):
    cols = slice(level * PAIRS, (level + 1) * PAIRS)
    ch.link(v.tensor_scalar(f, ps, -1.0, 0.0, ALU.add, ALU.max))
    ch.link(v.tensor_scalar(e, f, float(TOK), -float(TOK), ALU.is_ge, ALU.mult))
    ch.link(v.tensor_tensor(R.tokens[:, cols], f, e, ALU.add))
    ch.link(v.tensor_scalar(e, ps, 0.0, R.spare[:, 0:1], ALU.is_equal, ALU.mult))
    ch.link(v.tensor_tensor(R.rows[:, cols], f, e, ALU.add))


FILL_LINKS = 5


def place_onehots(v, ch, R, kk, ohs, level):
    ch.link(v.tensor_scalar(kk, R.level[:, :, :], level, None, ALU.is_equal))
    ch.link(v.scalar_tensor_tensor(out=kk, in0=R.place[:, :, :], scalar=1.0, in1=kk, op0=ALU.add, op1=ALU.mult))
    ch.link(v.tensor_scalar(kk, kk, -1.0, None, ALU.add))
    for q in range(8):
        t, j = q // 2, q % 2
        ins = v.tensor_scalar(ohs[:, q, :], R.eid[:, :], kk[:, t, j:j + 1], None, ALU.is_equal)
    ch.link(ins)


ONEHOT_LINKS = 4


def later_places(nc, C, A, M, R, xn, y):
    links = ONEHOT_LINKS + FILL_LINKS
    with Scope(nc) as s:
        X = Experts(s, nc, C, A, M, R, xn, y, "b")
        X.open(s)
        kk = s.sb("lp_kk", [P, NT, 2])
        ohs = s.sb("lp_ohs", [P, 8, P])
        f = s.sb("lp_f", [P, PAIRS])
        e = s.sb("lp_e", [P, PAIRS])
        xps = s.bank("lp_ps")
        own = s.sem("lp_own")
        ohs_ready = s.sem("lp_ohs_ready")
        summed = s.sem("lp_summed")
        tables = s.sem("lp_tables")

        def levels(eng, start, round_):
            ran = eng.alloc_register(f"ran_{start.__name__}")
            eng.reg_mov(ran, 1)
            with eng.Fori(2, LEVELS) as m:
                most = eng.value_load(R.most[0:1, bass.ds(m, 1)])
                with eng.If(most > 0):
                    start(eng, m, ran)
                    with eng.Fori(0, PAIRS) as q:
                        over = eng.value_load(R.over[0:1, bass.ds(m * PAIRS + q, 1)])
                        with eng.If(over > 0):
                            round_(eng, eng.snap(ran), q)
                            eng.reg_add(ran, ran, 1)

        with nc.Block() as block:
            @block.sync
            def _(sp):
                def load_start(sp, m, ran):
                    pass
                levels(sp, load_start, X.load)

            @block.gpsimd
            def _(pool):
                def move_start(pool, m, ran):
                    pool.wait_ge(tables, m - 1)
                    pool.sem_inc(X.asked, 1)

                def move(pool, i, q):
                    X.gather(pool, i, q)
                    X.aim(pool, q)
                    X.scatter(pool, i)
                X.begin(pool)
                levels(pool, move_start, move)

            @block.tensor
            def _(pe):
                def table_sums(pe, m, ran):
                    pe.wait_ge(ohs_ready, m - 1)
                    for q in range(8):
                        mm = nc.tensor.matmul(xps[:, 0:PAIRS], ohs[:, q, :], R.ptok[:, q, :], start=(q == 0), stop=(q == 7))
                    mm.then_inc(summed, 1)
                levels(pe, table_sums, lambda pe, i, q: X.pe(pe, i, i))

            @block.vector
            def _(dve):
                def table_fill(dve, m, ran):
                    ch = Chain(dve, own, (m - 2) * links)
                    before = dve.snap(ran)
                    place_onehots(nc.vector, ch, R, kk[:, :, :], ohs[:, :, :], R.eid[:, bass.ds(m, 1)])
                    dve.sem_inc(ohs_ready, 1)
                    dve.wait_ge(summed, m - 1)
                    dve.wait_ge(X.out_free, before)
                    fill_table(nc.vector, ch, R, xps[:, 0:PAIRS], 0, f[:, :], e[:, :])
                    dve.sem_inc(tables, 1)
                levels(dve, table_fill, lambda dve, i, q: X.dve(dve, i))

            @block.scalar
            def _(act):
                def scalar_start(act, m, ran):
                    pass
                levels(act, scalar_start, lambda act, i, q: X.scalar(act, i))


def combine(nc, C, A, M, R, y, out):
    with Scope(nc) as s:
        yg = [[s.sb(f"yg{t}{j}", [P, D]) for j in range(2)] for t in range(NT)]
        tmp = s.sb("cb_tmp", [P, NT, D])
        gain = s.sb("gain", [P, D])
        ssq = s.sb("cb_ssq", [P, NT])
        rs = s.sb("cb_rs", [P, NT])
        got = [s.sems(f"cb_got{j}", NT) for j in range(2)]
        gain_in = s.sem("cb_gain")
        own = s.sem("cb_own")
        summed = s.sem("cb_summed")
        squares = s.sem("cb_squares")
        var_ready = s.sem("cb_var")
        rs_ready = s.sem("cb_rs_s")
        res = s.sem("cb_res")
        stored = s.sem("cb_stored")
        with nc.Block() as block:
            @block.gpsimd
            def _(pool):
                for t in range(NT):
                    pool.wait_ge(var_ready, t + 1)
                    pool.tensor_tensor(rs[:, t:t + 1], ssq[:, t:t + 1], C.neghalf[:, 0:1], ALU.pow).then_inc(rs_ready, 1)

            @block.sync
            def _(sp):
                for t in range(NT):
                    for j in range(2):
                        src = y[j * TOK + P * t:j * TOK + P * t + P, :]
                        sp.dma_start(yg[t][j][:, :], src).then_inc(got[j][t], 16)
                sp.dma_start(gain[:, :], rows_to_all(A["g_final_2"], D)).then_inc(gain_in, 16)
                for t in range(NT):
                    sp.wait_ge(res, t + 1)
                    sp.dma_start(out[0, P * t:P * t + P, :], tmp[:, t, :]).then_inc(stored, 16)
                sp.wait_ge(stored, 16 * NT)

            @block.scalar
            def _(act):
                for t in range(NT):
                    act.wait_ge(summed, t + 1)
                    nc.scalar.activation(tmp[:, t, :], C.h[:, t, :], ACT.Square, accum_out=ssq[:, t:t + 1]).then_inc(squares, 1)

            @block.vector
            def _(dve):
                ch = Chain(dve, own)
                v = nc.vector

                def scaled(t):
                    dve.wait_ge(rs_ready, t + 1)
                    v.scalar_tensor_tensor(out=tmp[:, t, :], in0=C.h[:, t, :], scalar=rs[:, t:t + 1], in1=gain[:, :],
                                           op0=ALU.mult, op1=ALU.mult).then_inc(res, 1)
                for t in range(NT):
                    dve.wait_ge(got[0][t], 16)
                    ch.link(v.tensor_scalar(yg[t][0][:, :], yg[t][0][:, :], R.w[:, t, 0:1], None, ALU.mult))
                    dve.wait_ge(got[1][t], 16)
                    ch.link(v.scalar_tensor_tensor(out=yg[t][0][:, :], in0=yg[t][1][:, :], scalar=R.w[:, t, 1:2],
                                                   in1=yg[t][0][:, :], op0=ALU.mult, op1=ALU.add))
                    ch.link(v.tensor_tensor(yg[t][0][:, :], yg[t][0][:, :], M.gate[1][:, :], ALU.mult))
                    ch.link(v.tensor_tensor(C.h[:, t, :], C.h[:, t, :], yg[t][0][:, :], ALU.add))
                    dve.sem_inc(summed, 1)
                    dve.wait_ge(squares, t + 1)
                    v.tensor_scalar(ssq[:, t:t + 1], ssq[:, t:t + 1], 1.0 / D, EPS, ALU.mult, ALU.add).then_inc(var_ready, 1)
                dve.wait_ge(gain_in, 16)
                for t in range(NT):
                    scaled(t)


def project_second(nc, C, A, G, split):
    with Scope(nc) as s:
        zeroed = s.sem("kaz_zeroed")
        with nc.Block() as block:
            @block.gpsimd
            def _(pool):
                ch = Chain(pool, zeroed)
                ch.link(pool.memset(G.kaz[:, :, :, :], 0.0))
                ch.link(pool.memset(G.raw[:, :, 0:3], 0.0))

    def halves(b, ps):
        return [(G.kaz[64 * f:64 * f + 64, b, f, :], ps[64 * f:64 * f + 64, :], ACT.Copy, 1.0) for f in range(2)]

    w = P * NT
    steps = [
        (0, 512, True, lambda b, ps: [(G.raw[:, b, 3:3 + TOK], ps[:, :], ACT.Copy, 1.0)]),
        (512, 512, True, lambda b, ps: [(G.raw[:, 4 + b, 3:3 + TOK], ps[:, :], ACT.Copy, 1.0)]),
        (1024, 512, False, lambda b, ps: [(G.vm[:, b, :], ps[:, :], ACT.Copy, 1.0)]),
        (1536, 512, False, lambda b, ps: [(G.so[:, b, :], ps[:, :], ACT.Sigmoid, 1.0)]),
        (2056, 512, True, lambda b, ps: [(G.qa[:, b, :], ps[:, :], ACT.Copy, -HD ** -0.5)]),
        (2568, 512, True, halves),
        (3080, 512, False, lambda b, ps: [(G.va[:, b, :], ps[:, :], ACT.Copy, 1.0)]),
        (2048, 8, False, lambda b, ps: [(G.gt[:, b, :], ps[:, 0:8], ACT.Copy, 1.0)]),
    ]
    project(nc, C, split, A["w_in_2"][0], steps, "p2")


def mlp_up(nc, C, split, w, hT, modulation):
    halves = 2 * FF // 512
    with Scope(nc) as s:
        W = Weights(s, nc, "m")
        mod = modulation(s)
        units = len(mod.units)
        banks = [s.bank(f"mp{i}") for i in range(6)]
        half_used = s.sem("m_half_used")
        ready = s.sem("m_ready")
        relued = s.sem("m_relued")
        squared = s.sem("m_squared")
        with nc.Block() as block:
            @block.sync
            def _(sp):
                for i in range(halves):
                    src = w[512 * (i % 2):512 * (i % 2) + 512, 512 * (i // 2):512 * (i // 2) + 512]
                    free = None
                    if i >= 2:
                        free = (ready, 4 * (i // 2)) if i % 2 else (half_used, i // 2)
                    W.load(sp, i, src.rearrange("(k p) n -> p k n", p=P), 512, free)
                    if i == 1:
                        mod.load_unit(sp, 0)
                        mod.load_unit(sp, 1)
                        mod.load_biases(sp)
                    elif 2 <= i < units:
                        mod.load_unit(sp, i)

            @block.tensor
            def _(pe):
                for i in range(halves):
                    pe.wait_ge(W.low_ready, i + 1)
                    for g in range(4):
                        b = 4 * (i // 2) + g
                        if b >= 6 and i % 2 == 0:
                            pe.wait_ge(relued, b - 5)
                        for k in range(4):
                            kk = 4 * (i % 2) + k
                            mm = matmul3(nc, banks[b % 6][:, :], W.get(i, k, P * g, P),
                                         (split[0][:, kk, :], split[1][:, kk, :]), kk == 0, kk == KD - 1)
                        if i % 2:
                            mm.then_inc(ready, 1)
                        elif g == 3:
                            mm.then_inc(half_used, 1)
                        if g == 0 and 0 <= i - 2 < units:
                            mod.spread(pe, i - 2)

            @block.vector
            def _(dve):
                for i in range(halves):
                    W.low(dve, i)
                    if 0 <= i - 1 < units:
                        mod.sum(dve, i - 1)
                    if 0 <= i - 2 < units:
                        mod.finish(dve, i - 2)

            @block.scalar
            def _(act):
                W.high(act, 0)
                W.high(act, 1)
                for c in range(halves // 2):
                    if 2 * c + 2 < halves:
                        W.high(act, 2 * c + 2)
                    for b in range(4 * c, 4 * c + 4):
                        act.wait_ge(ready, b + 1)
                        nc.scalar.activation(hT[:, b, :], banks[b % 6][:, :], ACT.Relu).then_inc(relued, 1)
                    if 2 * c + 3 < halves:
                        W.high(act, 2 * c + 3)

            @block.gpsimd
            def _(pool):
                for b in range(2 * halves):
                    pool.wait_ge(relued, b + 1)
                    if b:
                        pool.wait_ge(squared, b)
                    pool.tensor_tensor(hT[:, b, :], hT[:, b, :], hT[:, b, :], ALU.mult).then_inc(squared, 1)


def project_out(nc, C, hT, w, gate, tag, ahead=None):
    rounds = w.shape[0] // 256
    with Scope(nc) as s:
        W = Weights(s, nc, tag)
        ah = [s.sb(f"ah{i}{tag}", [P, 2, TOK], F32R) for i in range(2)]
        al = [s.sb(f"al{i}{tag}", [P, 2, TOK], F32R) for i in range(2)]
        tmp = [s.sb(f"dt{i}{tag}", [P, 512]) for i in range(2)]
        ps = [s.bank(f"dp{b}{tag}") for b in range(2 * NT)]
        a_high = s.sem(f"d_a_high{tag}")
        a_low = s.sem(f"d_a_low{tag}")
        used = s.sem(f"d_used{tag}")
        ready = s.sem(f"d_ready{tag}")
        scaled = s.sem(f"d_scaled{tag}")
        added = s.sem(f"d_added{tag}")

        def in_pairs(eng, body):
            for slot in range(2):
                body(slot, slot, 0)
            if rounds > 4:
                with eng.Fori(1, rounds // 2 - 1) as j:
                    for slot in range(2):
                        body(j * 2 + slot, slot, j)
            for slot in range(2):
                body(rounds - 2 + slot, slot, rounds // 2 - 1)

        with nc.Block() as block:
            @block.sync
            def _(sp):
                def load(i, slot, j):
                    if not isinstance(i, int) or i >= 2:
                        sp.wait_ge(used, i - 1)
                    src = w[bass.ds(i * 256, 256), :].rearrange("(k p) n -> p k n", p=P)
                    sp.dma_start(W.raw[slot][:, :, :].rearrange("p (k f) n -> p k (f n)", k=2), src).then_inc(W.landed[slot], 16)
                in_pairs(sp, load)
                if ahead:
                    ahead(sp)

            @block.scalar
            def _(act):
                def high(i, slot, j):
                    act.wait_ge(W.landed[slot], j * 16 + 16)
                    nc.scalar.activation(W.hi[slot][:, :, :], W.raw[slot][:, :, :], ACT.Copy).then_inc(W.high_ready, 1)
                    nc.scalar.activation(ah[slot][:, :, :], hT[:, bass.ds(i * 2, 2), :], ACT.Copy).then_inc(a_high, 1)
                in_pairs(act, high)

            @block.tensor
            def _(pe):
                def multiply(i, slot, j):
                    pe.wait_ge(W.low_ready, i + 1)
                    pe.wait_ge(a_low, i + 1)
                    first, last = isinstance(i, int) and i == 0, isinstance(i, int) and i == rounds - 1
                    for b in range(2 * NT):
                        t, n = b % NT, b // NT
                        for k in range(2):
                            a = (ah[slot][:, k, P * t:P * t + P], al[slot][:, k, P * t:P * t + P])
                            mm = matmul3(nc, ps[b][:, :], a, W.get(slot, 2 * k + n, 0, 512), first and k == 0, last and k == 1)
                        if last:
                            mm.then_inc(ready, 1)
                    if not last:
                        mm.then_inc(used, 1)
                in_pairs(pe, multiply)

            @block.vector
            def _(dve):
                def lows(i, slot, j):
                    dve.wait_ge(W.high_ready, i + 1)
                    low(nc.vector, W.lo[slot][:, :, :], W.raw[slot][:, :, :], W.hi[slot][:, :, :]).then_inc(W.low_ready, 1)
                    dve.wait_ge(a_high, i + 1)
                    nc.vector.tensor_tensor(al[slot][:, :, :], hT[:, bass.ds(i * 2, 2), :], ah[slot][:, :, :].bitcast(F32),
                                            ALU.subtract).then_inc(a_low, 1)
                in_pairs(dve, lows)
                for b in range(2 * NT):
                    n = b // NT
                    dve.wait_ge(ready, b + 1)
                    if b >= 2:
                        dve.wait_ge(added, b - 1)
                    nc.vector.tensor_tensor(tmp[b % 2][:, :], ps[b][:, :], gate[:, 512 * n:512 * n + 512],
                                            ALU.mult).then_inc(scaled, 1)

            @block.gpsimd
            def _(pool):
                for b in range(2 * NT):
                    n, t = b // NT, b % NT
                    pool.wait_ge(scaled, b + 1)
                    dst = C.h[:, t, 512 * n:512 * n + 512]
                    pool.tensor_tensor(dst, dst, tmp[b % 2][:, :], ALU.add).then_inc(added, 1)


class Bag:
    pass


def first_attention(nc, C, M, A):
    pass


def program(nc, A, out, dump=None):
    Scope.used.clear()
    with Scope(nc) as s:
        C = Bag()
        C.h = s.sb("h", [P, NT, D])
        C.ident = s.sb("ident", [P, P])
        C.ones = s.sb("ones", [P, P])
        C.later = s.sb("later", [P, P])
        C.ban = s.sb("ban", [P, 512])
        C.ban_self = s.sb("ban_self", [P, 512])
        C.allow = s.sb("allow", [P, 512])
        C.neghalf = s.sb("neghalf", [P, 48])
        C.cols1 = s.sb("cols1", [P, P])
        C.cols2 = s.sb("cols2", [P, P])
        M = [Bag(), Bag()]
        gates = s.sb("gates", [P, 4, D])
        C.bias = gates[:, :, :].rearrange("p g (a n) -> p (g a) n", a=2)
        for b in range(2):
            M[b].sc = s.sb(f"silu_c{b}", [P, KD])
            M[b].scale = [s.sb(f"scale{b}{i}", [P, KD]) for i in range(2)]
            M[b].shift = [s.sb(f"shift{b}{i}", [P, KD]) for i in range(2)]
            M[b].gate = [gates[:, 2 * b + i, :] for i in range(2)]
        C.cbias_dram = nc.dram_tensor("compressed_bias", [P, NT * 256], F32).ap()
        with Scope(nc) as s1:
            mod = Modulation(s1, nc, C, M[0], C.cols1, A["ada_w"][0], A["ada_b"][0], [1, 0], "m1")
            constants(nc, C, A, lambda sp: [mod.load_unit(sp, u) for u in range(2)])
            first_modulation(nc, C, M, A, mod)
        B = Bag()
        with Scope(nc) as s0:
            mT = s0.sb("mT", [P, KD, TOK])
            with Scope(nc) as s1:
                B.sig = s1.sb("sig", [P, NT, 2 * D])
                B.oa, B.ob = mT[:, 0:NT, :], mT[:, NT:2 * NT, :]
                with Scope(nc) as s1b:
                    B.sbq = s1b.sb("sbq", [P, 4, TOK])
                    B.sbk = s1b.sb("sbk", [P, 4, 2, TOK])
                    B.sbv = s1b.sb("sbv", [P, NT, 512])
                    with Scope(nc) as s2:
                        B.kv = s2.sb("kv", [P, NT, 512])
                        B.ga = s2.sb("ga", [P, NT, 24])
                        B.qT = s2.sb("qT", [P, 4, TOK])
                        B.ksz = s2.sb("ksz", [P, 2, TOK])
                        B.kwz = s2.sb("kwz", [P, 2, TOK])
                        B.kcd = s2.sb("kcd", [P, 64])
                        B.vcd = s2.sb("vcd", [P, 256])
                        with Scope(nc) as s3:
                            B.qa = s3.sb("qa", [P, NT, 512])
                            B.kcT = s3.sb("kcT", [P, TOK])
                            B.vcT = s3.sb("vcT", [P, TOK])
                            with Scope(nc) as s4:
                                uT = s4.sb("uT", [P, KD, TOK])
                                split = s4.twin("u1_high", "mT", [P, KD, TOK]), s4.twin("u1_low", "uT", [P, KD, TOK])
                                norm_turn(nc, C, M[0].scale[0], M[0].shift[0], uT, "n1", split=split)
                                project_first(nc, C, A, B, split)
                            head_norms(nc, C, B)
                            compress(nc, C, A, B)
                        if dump: dump("prep", B.qT[:, 1, :], B.kcd[:, :], B.vcd[:, :], B.ksz[:, 1, :])
                        C.cbias = s2.sb("cbias", [P, NT, 256])
                        C.cmask = s2.sb("cmask", [P, NT, CMP])
                        compressed_bias(nc, C)
                        compressed_attention(nc, C, B)
                        for tag, kz, branch in (("sl", B.ksz, 1), ("wn", B.kwz, 2)):
                            softmax_attention(
                                nc, C, tag, lambda i: B.qT[:, bass.ds(i, 1), :].rearrange("p a n -> p (a n)"),
                                lambda half, i, w: kz[:, half, 0:w],
                                lambda b, half, i: B.kv[:, b, 256 * branch - 128 + 64 * half:256 * branch - 64 + 64 * half],
                                lambda half, i: B.oa[:, :, bass.ds(i * 64 + 256 * half, 64)],
                                bias=lambda half, i: C.bias[:, bass.ds(i + 4 * half, 1), :].rearrange("p a n -> p (a n)"),
                                gate=lambda half, i: B.ga[:, :, bass.ds(i * 3 + 12 * half + branch, 1)].rearrange("p t a -> p (t a)"),
                                add=True)
                        if dump: dump("nsa", B.oa[:, 0, :],  B.oa[:, 3, :])
                    stick_breaking(nc, C, B)
                    if dump: dump("sb", B.ob[:, :, :])
                    B.oT = [s1b.sb(f"oT{i}", [P, 4, TOK]) for i in range(2)]
                    turn_tokens(nc, C, [(lambda t, o=o, k=k: o[:, t, P * k:P * k + P], B.oT[i][:, k, :], None)
                                        for i, o in enumerate((B.oa, B.ob)) for k in range(4)], "oT")
                    mixed = s1b.sb("mixed", [P, NT, D])
                    mix_branches(nc, C, A, B, mixed)
                    turn_tokens(nc, C, [(lambda t, k=k: mixed[:, t, P * k:P * k + P], mT[:, k, :], None)
                                        for k in range(KD)], "mT")
            rest = lambda sc: Modulation(sc, nc, C, M[0], C.cols1, A["ada_w"][0], A["ada_b"][0], [2, 4, 3, 5], "m2")
            project_residual(nc, C, mT, A["w_out"][0], M[0].gate[0], "o1", rest, lambda u: u + 1, 3)
        if dump: dump("res1", C.h[:, :, :])
        Scope.clear(nc)
        with Scope(nc) as s1:
            hT = s1.sb("hT", [P, FF // P, TOK])
            with Scope(nc) as s2:
                uT = s2.sb("uT2", [P, KD, TOK])
                high = s2.sb("uh2", [P, KD, TOK], F32R)
                split = high, s2.twin("u2_low", "uT2", [P, KD, TOK])
                norm_turn(nc, C, M[0].scale[1], M[0].shift[1], uT, "n2", split=split)
                second = lambda sc: Modulation(sc, nc, C, M[1], C.cols2, A["w_ada_2"][0], A["b_ada_2"][0],
                                               [1, 0, 2, 4, 3, 5], "m3")
                mlp_up(nc, C, split, A["mlp_w1"][0], hT, second)
            project_out(nc, C, hT, A["mlp_w2"][0], M[0].gate[1], "o2")
        if dump: dump("h1", C.h[:, :, :])
        Scope.clear(nc)
        R = Bag()
        R.w = s.sb("rw", [P, NT, 2])
        R.rank = s.sb("rrank", [P, NT, 2])
        R.level = s.sb("rlevel", [P, NT, 2])
        R.pair = s.sb("rpair", [P, NT, 2])
        R.place = s.sb("rplace", [P, NT, 2])
        R.eid = s.sb("eid", [P, P])
        R.aid = s.sb("aid", [P, 2, NT])
        R.spare = s.sb("spare", [P, 1])
        R.ptok = s.sb("ptok", [P, 8, PAIRS])
        R.tokens = s.sb("slot_tokens", [P, 2 * PAIRS], U32)
        R.rows = s.sb("slot_rows", [P, 2 * PAIRS], U32)
        R.over = s.sb("over", [1, LEVELS * PAIRS], I32)
        R.most = s.sb("most", [1, LEVELS], I32)
        xn = nc.dram_tensor("normed_rows", [TOK, D], F32).ap()
        y = nc.dram_tensor("expert_rows", [2 * TOK + P, D], F32).ap()
        with Scope(nc) as s0:
            uT = s0.sb("uT3", [P, KD, TOK])
            with Scope(nc) as s1:
                heads_out = s1.sb("heads_out", [P, 2 * NT, 512])
                cat = [heads_out[:, 0:NT, :], heads_out[:, NT:2 * NT, :]]
                with Scope(nc) as s2:
                    G = Bag()
                    G.vm = s2.sb("vm", [P, NT, 512])
                    G.so = s2.sb("so", [P, NT, 512])
                    G.gt = s2.sb("gt", [P, NT, 8])
                    G.qa = s2.sb("qa2", [P, 4, TOK])
                    G.kaz = s2.sb("kaz", [P, 4, 2, TOK])
                    G.va = s2.sb("va", [P, NT, 512])
                    G.qk = s2.sb("qk", [P, KD, TOK])
                    G.a = [s2.sb(f"ga{h}", [P, TOK]) for h in range(4)]
                    G.negtop = s2.sb("negtop", [P, 16])
                    G.em = s2.sb("em", [P, 16])
                    with Scope(nc) as s3:
                        G.raw = s3.sb("raw", [P, KD, TOK + 3])
                        with Scope(nc) as s4:
                            split = s4.twin("u3_high", "heads_out", [P, KD, TOK]), s4.twin("u3_low", "uT3", [P, KD, TOK])
                            norm_turn(nc, C, M[1].scale[0], M[1].shift[0], uT, "n3", split=split)
                            project_second(nc, C, A, G, split)
                        gate_rows(nc, C, A, G)
                        convolve(nc, C, G)
                    mlstm(nc, C, G, cat[0])
                    norm_heads_gate(nc, C, cat[0], G.so)
                    softmax_attention(
                        nc, C, "ma", lambda i: G.qa[:, bass.ds(i, 1), :].rearrange("p a n -> p (a n)"),
                        lambda half, i, w: G.kaz[:, bass.ds(i, 1), half, 0:w].rearrange("p a n -> p (a n)"),
                        lambda b, half, i: G.va[:, b, bass.ds(i * 128 + 64 * half, 64)],
                        lambda half, i: cat[1][:, :, bass.ds(i * 128 + 64 * half, 64)])
                    if dump: dump("cat", cat[0][:, :, :], cat[1][:, :, :])
                turn_tokens(nc, C, [(lambda t, k=k: cat[k // 4][:, t, P * (k % 4):P * (k % 4) + P], uT[:, k, :],
                                     C.cols2[:, 112 + k:113 + k] if k < 4 else None) for k in range(KD)], "cT")
            Scope.clear(nc)
            X = Experts(s0, nc, C, A, M[1], R, xn, y, "a")
            project_out(nc, C, uT, A["w_out_2"][0], M[1].gate[0], "o3", ahead=lambda sp: X.load(sp, None, 0))
            norm_turn(nc, C, M[1].scale[1], M[1].shift[1], uT, "n4", xn_dram=xn)
            route(nc, C, A, uT, R)
            first_places(nc, X, R)
        later_places(nc, C, A, M[1], R, xn, y)
        combine(nc, C, A, M[1], R, y, out)


def project_first(nc, C, A, B, split):
    copy = lambda dst: (lambda b, ps: [(dst(b), ps, ACT.Copy, 1.0)])
    with Scope(nc) as s:
        zeroed = s.sem("sbk_zeroed")
        with nc.Block() as block:
            @block.gpsimd
            def _(pool):
                pool.memset(B.sbk[:, :, :, :], 0.0).then_inc(zeroed, 1)
                pool.wait_ge(zeroed, 1)

    def halves(b, ps):
        return [(B.sbk[64 * f:64 * f + 64, b, f, :], ps[64 * f:64 * f + 64, :], ACT.Copy, 1.0) for f in range(2)]

    steps = [
        (0, 512, False, lambda b, ps: [(B.qa[:, b, :], ps[:, :], ACT.Copy, 1.0)]),
        (768, 512, False, lambda b, ps: [(B.kv[:, b, :], ps[:, :], ACT.Copy, 1.0)]),
        (1304, 512, True, lambda b, ps: [(B.sbq[:, b, :], ps[:, :], ACT.Copy, HD ** -0.5)]),
        (1816, 512, True, halves),
        (2328, 512, False, lambda b, ps: [(B.sbv[:, b, :], ps[:, :], ACT.Copy, 1.0)]),
    ] + [
        (2840 + 512 * m, 512, False,
         lambda b, ps, m=m: [(B.sig[:, b, 512 * m:512 * m + 512], ps[:, :], ACT.Sigmoid, 1.0)]) for m in range(4)
    ] + [
        (512, 256, True, lambda b, ps: [((B.kcT, B.vcT)[b][:, :], ps[:, :], ACT.Copy, 1.0)]),
        (1280, 24, False, lambda b, ps: [(B.ga[:, b, :], ps[:, 0:24], ACT.Sigmoid, 1.0)]),
    ]
    project(nc, C, split, A["w_in"][0], steps, "p1")


def distance_onehots():
    dist = TOK - 1 - np.arange(BIAS_X)
    n = np.maximum(dist, 0)
    exact = BUCKETS // 2
    nf = np.maximum(n, 1).astype(np.float32)
    large = exact + (np.log(nf / np.float32(exact)) / np.float32(np.log(128 / exact)) * (BUCKETS - exact)).astype(np.int32)
    bucket = np.where(n < exact, n, np.minimum(large, BUCKETS - 1))
    bucket = np.where(dist < 0, BUCKETS, bucket)
    return (bucket[None, :] == np.arange(BUCKETS + 1)[:, None]).astype(np.float32)


def kernel(**inputs):
    import concourse.bacc as bacc
    from concourse.bass_utils import run_bass_kernel_spmd

    nc = bacc.Bacc("TRN2", target_bir_lowering=False, num_devices=1)
    arrays, A = {}, {}
    for name in [*_INS, "onehot"]:
        a = distance_onehots() if name == "onehot" else np.ascontiguousarray(inputs[name])
        arrays[f"in_{name}_dram"] = a
        A[name] = nc.dram_tensor(f"in_{name}_dram", a.shape, mybir.dt.from_np(a.dtype), kind="ExternalInput").ap()
    out = nc.dram_tensor("out_0_dram", (1, TOK, D), F32, kind="ExternalOutput").ap()
    program(nc, A, out)
    r = run_bass_kernel_spmd(nc, [arrays], core_ids=[0])
    return r.results[0]["out_0_dram"]
```
